# Optimizing a Trainium2 kernel written in Bass

```python
import math
import jax, jax.numpy as jnp
from jax import lax
import numpy as np

D_MODEL = 1024
BATCH = 1
SEQ = 512
DEPTH = 2
DEC_BATCH = 8
DEC_SEQ = 1
PAST_LEN = 4096
PAGE_SIZE = 128

N_MIXERS = 2
N_S5 = (DEPTH + 1) // 2
N_HG = DEPTH // 2
S5_GROUP = 16
S5_GROUPS = D_MODEL // S5_GROUP
S5_STATE = 64
S5_DT_MIN = 0.001
S5_DT_MAX = 0.1
HG_DK = 128
HG_HEADS = D_MODEL // HG_DK
HG_DV = D_MODEL // HG_HEADS
HG_WIDTH = HG_HEADS * HG_DK
HG_CHUNK = 64
N_MEM = 256
MEM_HEADS = 4
MEM_HD = D_MODEL // MEM_HEADS
FFN_DIM = 2816
EPS = 1e-6

kernel_name = "hybrid_s5_hgrn2_macaron_memxattn_step"

def rmsnorm(x, g):
    xf = x.astype(jnp.float32)
    y = xf * lax.rsqrt(jnp.mean(xf * xf, axis=-1, keepdims=True) + EPS)
    return (y * g.astype(jnp.float32)).astype(x.dtype)

def swiglu(x, w_in, w_out):
    gate, up = jnp.split(x @ w_in, 2, axis=-1)
    return (jax.nn.silu(gate) * up) @ w_out

def s5_mixer(u, h0_re, h0_im, a_re, a_im, log_dt, b_re, b_im, c_re, c_im, d, w_glu):
    bsz, t, _ = u.shape
    f32 = jnp.float32
    ug = u.astype(f32).reshape(bsz, t, S5_GROUPS, S5_GROUP)
    lam = lax.complex(a_re.astype(f32), a_im.astype(f32))
    dt = jnp.exp(log_dt.astype(f32))[:, None]
    lam_bar = jnp.exp(lam * dt)
    b = lax.complex(b_re.astype(f32), b_im.astype(f32))
    b_bar = ((lam_bar - 1.0) / lam)[..., None] * b
    c = lax.complex(c_re.astype(f32), c_im.astype(f32))
    bu = jnp.einsum('btgc,gpc->btgp', ug.astype(jnp.complex64), b_bar)
    a_seq = jnp.broadcast_to(lam_bar, (1, t, S5_GROUPS, S5_STATE))

    def combine(e1, e2):
        a1, x1 = e1
        a2, x2 = e2
        return a1 * a2, a2 * x1 + x2

    a_cum, x_cum = lax.associative_scan(combine, (a_seq, bu), axis=1)
    h0 = lax.complex(h0_re.astype(f32), h0_im.astype(f32))
    h = x_cum + a_cum * h0[:, None]
    y = jnp.einsum('btgp,gcp->btgc', h, c).real + d.astype(f32) * ug
    y = jax.nn.gelu(y.reshape(bsz, t, D_MODEL))
    ya, yb = jnp.split(y @ w_glu.astype(f32), 2, axis=-1)
    out = ya * jax.nn.sigmoid(yb)
    h_last = h[:, -1]
    return out.astype(u.dtype), h_last.real.astype(h0_re.dtype), h_last.imag.astype(h0_im.dtype)

def hgrn2_chunked(q, k, v, logf, s0):
    bsz, t = q.shape[:2]
    c = min(HG_CHUNK, t)
    n = -(-t // c)
    pad = n * c - t

    def prep(a):
        if pad:
            a = jnp.pad(a, ((0, 0), (0, pad), (0, 0), (0, 0)))
        return a.reshape(bsz, n, c, a.shape[2], a.shape[3]).transpose(1, 0, 2, 3, 4)

    qs, ks, vs, gs = prep(q), prep(k), prep(v), prep(logf)
    pos = jnp.arange(c)
    causal = (pos[:, None] >= pos[None, :])[None, :, :, None, None]

    def step(s, inp):
        qc, kc, vc, gc = inp
        bcum = jnp.cumsum(gc, axis=1)
        btot = bcum[:, -1]
        o_inter = jnp.einsum('bthk,bhkv->bthv', qc * jnp.exp(bcum), s)
        diff = bcum[:, :, None] - bcum[:, None, :]
        decay = jnp.exp(jnp.where(causal, diff, -jnp.inf))
        att = jnp.einsum('bthk,bshk,btshk->bhts', qc, kc, decay)
        o_intra = jnp.einsum('bhts,bshv->bthv', att, vc)
        k_dec = kc * jnp.exp(btot[:, None] - bcum)
        s_new = jnp.exp(btot)[..., None] * s + jnp.einsum('bshk,bshv->bhkv', k_dec, vc)
        return s_new, o_inter + o_intra

    s_fin, o = lax.scan(step, s0.astype(jnp.float32), (qs, ks, vs, gs))
    o = o.transpose(1, 0, 2, 3, 4).reshape(bsz, n * c, HG_HEADS, HG_DV)[:, :t]
    return o, s_fin

def hgrn2_mixer(x, s0, lb, w_in, norm_g, w_out):
    bsz, t, _ = x.shape
    f32 = jnp.float32
    proj = (x @ w_in).astype(f32)
    q, fz, i_in, g = jnp.split(proj, [HG_WIDTH, 2 * HG_WIDTH, 2 * HG_WIDTH + HG_HEADS * HG_DV], axis=-1)
    q = jax.nn.silu(q)
    lbf = lb.astype(f32)
    logf = jnp.logaddexp(jnp.log(lbf), jnp.log1p(-lbf) + jax.nn.log_sigmoid(fz))
    k = -jnp.expm1(logf)
    heads = lambda a, dd: a.reshape(bsz, t, HG_HEADS, dd)
    o, s_fin = hgrn2_chunked(heads(q, HG_DK), heads(k, HG_DK), heads(i_in, HG_DV), heads(logf, HG_DK), s0)
    o = rmsnorm(o, norm_g).reshape(bsz, t, HG_HEADS * HG_DV) * jax.nn.silu(g)
    return o.astype(x.dtype) @ w_out, s_fin.astype(s0.dtype)

def mem_kv(mem, norm_g, w_kv):
    bsz = mem.shape[0]
    kk, vv = jnp.split(rmsnorm(mem, norm_g) @ w_kv, 2, axis=-1)
    return kk.reshape(bsz, N_MEM, MEM_HEADS, MEM_HD), vv.reshape(bsz, N_MEM, MEM_HEADS, MEM_HD)

def cross_attend(x, mk, mv, w_q, w_o):
    bsz, t, _ = x.shape
    q = (x @ w_q).reshape(bsz, t, MEM_HEADS, MEM_HD).astype(jnp.float32)
    s = jnp.einsum('bthd,bmhd->bhtm', q, mk.astype(jnp.float32)) * (1.0 / math.sqrt(MEM_HD))
    p = jax.nn.softmax(s, axis=-1)
    o = jnp.einsum('bhtm,bmhd->bthd', p, mv.astype(jnp.float32)).reshape(bsz, t, D_MODEL)
    return o.astype(x.dtype) @ w_o

def trunk(x, s5_re, s5_im, hg_s, mem_k, mem_v, lower_bounds, p):
    new_re, new_im, new_hg = [], [], []
    for i in range(DEPTH):
        j = i // N_MIXERS
        x = x + 0.5 * swiglu(rmsnorm(x, p['ffn1_norm'][i]), p['ffn1_w_in'][i], p['ffn1_w_out'][i])
        h = rmsnorm(x, p['mix_norm'][i])
        if i % N_MIXERS == 0:
            y, hr, hi = s5_mixer(h, s5_re[j], s5_im[j], p['s5_a_re'][j], p['s5_a_im'][j], p['s5_log_dt'][j],
                                 p['s5_b_re'][j], p['s5_b_im'][j], p['s5_c_re'][j], p['s5_c_im'][j],
                                 p['s5_d'][j], p['s5_w_glu'][j])
            new_re.append(hr)
            new_im.append(hi)
        else:
            y, sn = hgrn2_mixer(h, hg_s[j], lower_bounds[i], p['hg_w_in'][j], p['hg_norm'][j], p['hg_w_out'][j])
            new_hg.append(sn)
        x = x + y
        x = x + cross_attend(rmsnorm(x, p['xattn_norm'][i]), mem_k[i], mem_v[i], p['xattn_w_q'][i], p['xattn_w_o'][i])
        x = x + 0.5 * swiglu(rmsnorm(x, p['ffn2_norm'][i]), p['ffn2_w_in'][i], p['ffn2_w_out'][i])
    x = rmsnorm(x, p['final_norm'])
    return x, jnp.stack(new_re), jnp.stack(new_im), jnp.stack(new_hg)

def setup_inputs(seed: int = 0) -> dict:
    key = jax.random.key(seed)
    ks = iter(jax.random.split(key, 48))
    f32 = jnp.float32

    def nrm(shape, scale):
        return jax.random.normal(next(ks), shape, f32) * scale

    def gain(shape):
        return 1.0 + 0.05 * jax.random.normal(next(ks), shape, f32)

    G, P, GC = S5_GROUPS, S5_STATE, S5_GROUP
    n_idx = jnp.arange(P, dtype=f32)
    return {
        "x_prompt": nrm((BATCH, SEQ, D_MODEL), 1.0),
        "x_sample": nrm((DEC_BATCH, DEC_SEQ, D_MODEL), 1.0),
        "mem_prompt": nrm((BATCH, N_MEM, D_MODEL), 1.0),
        "state_s5_re": nrm((N_S5, DEC_BATCH, G, P), 0.1),
        "state_s5_im": nrm((N_S5, DEC_BATCH, G, P), 0.1),
        "state_hgrn": nrm((N_HG, DEC_BATCH, HG_HEADS, HG_DK, HG_DV), 0.3),
        "cache_mem_k": nrm((DEPTH, DEC_BATCH, N_MEM, MEM_HEADS, MEM_HD), 1.0),
        "cache_mem_v": nrm((DEPTH, DEC_BATCH, N_MEM, MEM_HEADS, MEM_HD), 1.0),
        "ffn1_norm": gain((DEPTH, D_MODEL)),
        "ffn1_w_in": nrm((DEPTH, D_MODEL, 2 * FFN_DIM), D_MODEL ** -0.5),
        "ffn1_w_out": nrm((DEPTH, FFN_DIM, D_MODEL), FFN_DIM ** -0.5),
        "mix_norm": gain((DEPTH, D_MODEL)),
        "xattn_norm": gain((DEPTH, D_MODEL)),
        "mem_norm": gain((DEPTH, D_MODEL)),
        "xattn_w_q": nrm((DEPTH, D_MODEL, D_MODEL), D_MODEL ** -0.5),
        "xattn_w_kv": nrm((DEPTH, D_MODEL, 2 * D_MODEL), D_MODEL ** -0.5),
        "xattn_w_o": nrm((DEPTH, D_MODEL, D_MODEL), D_MODEL ** -0.5),
        "ffn2_norm": gain((DEPTH, D_MODEL)),
        "ffn2_w_in": nrm((DEPTH, D_MODEL, 2 * FFN_DIM), D_MODEL ** -0.5),
        "ffn2_w_out": nrm((DEPTH, FFN_DIM, D_MODEL), FFN_DIM ** -0.5),
        "s5_a_re": -0.5 + nrm((N_S5, G, P), 0.01),
        "s5_a_im": jnp.pi * n_idx + nrm((N_S5, G, P), 0.01),
        "s5_log_dt": jax.random.uniform(next(ks), (N_S5, G), f32, math.log(S5_DT_MIN), math.log(S5_DT_MAX)),
        "s5_b_re": nrm((N_S5, G, P, GC), (2 * GC) ** -0.5),
        "s5_b_im": nrm((N_S5, G, P, GC), (2 * GC) ** -0.5),
        "s5_c_re": nrm((N_S5, G, GC, P), 2 ** -0.5),
        "s5_c_im": nrm((N_S5, G, GC, P), 2 ** -0.5),
        "s5_d": nrm((N_S5, G, GC), 1.0),
        "s5_w_glu": nrm((N_S5, D_MODEL, 2 * D_MODEL), D_MODEL ** -0.5),
        "hg_w_in": nrm((N_HG, D_MODEL, 2 * HG_WIDTH + 2 * HG_HEADS * HG_DV), D_MODEL ** -0.5),
        "hg_lb_logits": nrm((DEPTH, HG_WIDTH), 0.5),
        "hg_norm": gain((N_HG, HG_DV)),
        "hg_w_out": nrm((N_HG, HG_HEADS * HG_DV, D_MODEL), D_MODEL ** -0.5),
        "final_norm": gain((D_MODEL,)),
    }

def reference(x_prompt, x_sample, mem_prompt, state_s5_re, state_s5_im, state_hgrn, cache_mem_k, cache_mem_v,
              ffn1_norm, ffn1_w_in, ffn1_w_out, mix_norm, xattn_norm, mem_norm, xattn_w_q, xattn_w_kv, xattn_w_o,
              ffn2_norm, ffn2_w_in, ffn2_w_out, s5_a_re, s5_a_im, s5_log_dt, s5_b_re, s5_b_im, s5_c_re, s5_c_im,
              s5_d, s5_w_glu, hg_w_in, hg_lb_logits, hg_norm, hg_w_out, final_norm):
    p = dict(ffn1_norm=ffn1_norm, ffn1_w_in=ffn1_w_in, ffn1_w_out=ffn1_w_out, mix_norm=mix_norm,
             xattn_norm=xattn_norm, xattn_w_q=xattn_w_q, xattn_w_o=xattn_w_o, ffn2_norm=ffn2_norm,
             ffn2_w_in=ffn2_w_in, ffn2_w_out=ffn2_w_out, s5_a_re=s5_a_re, s5_a_im=s5_a_im, s5_log_dt=s5_log_dt,
             s5_b_re=s5_b_re, s5_b_im=s5_b_im, s5_c_re=s5_c_re, s5_c_im=s5_c_im, s5_d=s5_d, s5_w_glu=s5_w_glu,
             hg_w_in=hg_w_in, hg_norm=hg_norm, hg_w_out=hg_w_out, final_norm=final_norm)
    sm = jax.nn.softmax(hg_lb_logits.astype(jnp.float32), axis=0)
    lower_bounds = jnp.cumsum(sm, axis=0) - sm[0]

    bp = x_prompt.shape[0]
    z_re = jnp.zeros((N_S5, bp, S5_GROUPS, S5_STATE), state_s5_re.dtype)
    z_hg = jnp.zeros((N_HG, bp, HG_HEADS, HG_DK, HG_DV), state_hgrn.dtype)
    kv = [mem_kv(mem_prompt, mem_norm[i], xattn_w_kv[i]) for i in range(DEPTH)]
    mem_k_p = jnp.stack([a for a, _ in kv])
    mem_v_p = jnp.stack([b for _, b in kv])
    y_prompt, s5_re_p, s5_im_p, hg_p = trunk(x_prompt, z_re, z_re, z_hg, mem_k_p, mem_v_p, lower_bounds, p)

    y_sample, s5_re_s, s5_im_s, hg_s = trunk(x_sample, state_s5_re, state_s5_im, state_hgrn,
                                             cache_mem_k, cache_mem_v, lower_bounds, p)
    return (y_prompt, y_sample, s5_re_p, s5_im_p, s5_re_s, s5_im_s, hg_p, hg_s, mem_k_p, mem_v_p)


_drawn_inputs = setup_inputs


def setup_inputs(seed=0):
    import zlib

    import numpy as np

    out = dict(_drawn_inputs(seed))
    spreads = {}
    factors = {'xattn_norm': 8.0, 's5_a_re': 4.162}
    for name, (base, spread) in spreads.items():
        noise = np.random.default_rng([zlib.crc32(name.encode()), seed]).standard_normal(out[name].shape)
        drawn = base * np.exp(spread * noise) if base else spread * noise
        out[name] = __import__('jax').numpy.asarray(drawn.astype(out[name].dtype))
    for name, factor in factors.items():
        out[name] = (out[name] * factor).astype(out[name].dtype)
    return out
```

```python
import math
import numpy as np
import concourse.bass as bass
from concourse import mybir

F32 = mybir.dt.float32
F32R = mybir.dt.float32r
I32 = mybir.dt.int32
ALU = mybir.AluOpType
ACT = mybir.ActivationFunctionType
AX = mybir.AxisListType

P = 128
D = 1024
KD = D // P
SEQ = 512
NS = 8
NT = SEQ + NS
HT = NT // 2
DEPTH = 2
FFN = 2816
FH = FFN // P // 2
NM = 256
MH = 4
EPS = 1e-6
SG, SC, SP_, CS = 64, 16, 64, 8
NJ = SG // 2
NC = SEQ // CS
CB = 8
UC = NC + 2 * NS
YC = NC + NS
HH = 8
HC = 64
NHC = SEQ // HC
LEVELS = (32, 16, 8)

V_FFN1, V_MIX, V_XA, V_MEM, V_FFN2, V_FIN, V_D, V_LB, V_HG = 0, 16, 32, 48, 64, 80, 88, 96, 112
NVEC = 113


class Chain:

    def __init__(self, eng, sem):
        self.eng, self.sem, self.n, self.off = eng, sem, 0, 0

    def link(self, ins):
        ins.then_inc(self.sem, 1)
        self.n += 1
        self.eng.wait_ge(self.sem, self.off + self.n)

    def loop(self, i, first, per):
        self.off = (i - first) * per
        self.start, self.per = self.n, per

    def done(self, turns):
        assert self.n == self.start + self.per, (self.n - self.start, self.per)
        self.n = self.start + self.per * turns
        self.off = 0


BLOCKS = [("ffn1", 0), ("s5", 0), ("xattn", 0), ("ffn2", 0), ("ffn1", 1), ("hgrn", 1), ("xattn", 1), ("ffn2", 1)]
GAIN_ROW = {"ffn1": V_FFN1, "s5": V_MIX, "hgrn": V_MIX, "xattn": V_XA, "ffn2": V_FFN2}


class Groups:

    def __init__(self, groups, filled, emptied, banks=4):
        self.groups, self.filled, self.emptied, self.banks = groups, filled, emptied, banks

    def before(self, q, engine):
        return sum(g[2] == engine for g in self.groups[:q])

    def reuse(self, eng, q):
        if q >= self.banks:
            owner = self.groups[q - self.banks][2]
            eng.wait_ge(self.emptied[owner], self.before(q - self.banks + 1, owner))

    def all_emptied(self, eng, q):
        for owner, semaphore in self.emptied.items():
            if self.before(q, owner):
                eng.wait_ge(semaphore, self.before(q, owner))

    def first(self, what):
        return next(q for q, g in enumerate(self.groups) if g[0] == what)

    def at(self, what, a):
        return next(q for q, g in enumerate(self.groups) if g[:2] == (what, a))

    def after(self, what):
        return 1 + max(q for q, g in enumerate(self.groups) if g[0] == what)


def streams():
    out = []
    for layer in range(DEPTH):
        out += [("k", layer, 4, KD), ("v", layer, 4, KD)]
    for block, layer in BLOCKS:
        if block in ("ffn1", "ffn2"):
            for half in range(2):
                out += [(f"{block}_in{half}", layer, FH, KD), (f"{block}_out{half}", layer, 4, FH)]
        elif block == "s5":
            out += [("glu", layer, 8, KD)]
        elif block == "hgrn":
            out += [("hg_qf", layer, 8, KD), ("hg_vg", layer, 8, KD), ("hg_out", layer, 4, KD)]
        else:
            out += [("xq", layer, 4, KD), ("xo", layer, 4, KD)]
    return out


LAST = {"ffn1": "ffn1_out1", "ffn2": "ffn2_out1", "s5": "glu", "hgrn": "hg_out", "xattn": "xo"}
FIRST = {"ffn1": "ffn1_in0", "ffn2": "ffn2_in0", "hgrn": "hg_qf", "xattn": "xq"}


def trunk_kernel(nc, i_, o_):
    ST = streams()
    first_pair, at_pair = {}, 0
    for name, layer, pairs, _ in ST:
        first_pair[name, layer] = at_pair
        at_pair += pairs
    ALL_PAIRS = at_pair
    NORM_ROW = [GAIN_ROW[b] + KD * l for b, l in BLOCKS] + [V_FIN]
    NORMS = len(NORM_ROW)
    norm_of = {(FIRST[b], l): r for r, (b, l) in enumerate(BLOCKS) if b in FIRST}
    norm_after = {(LAST[b], l): r + 1 for r, (b, l) in enumerate(BLOCKS)}
    split_norms = [r for r, (b, l) in enumerate(BLOCKS) if b in FIRST]
    gain_after = {k: r for k, r in norm_after.items() if r in split_norms}

    def at(name, shape, dtype, offset):
        return nc.alloc_sbuf_tensor_at(name, shape, dtype, offset=offset)

    base = (nc.sbuf_base + 63) // 64 * 64
    TILE = NT * 4
    off = base
    o_x = off; off += KD * TILE
    o_ah = off; off += KD * TILE
    o_al = off; off += KD * TILE
    CH = FH * P * 4
    o_raw = off; off += 2 * CH
    o_wh = off; off += 2 * CH
    o_wl = off; off += 2 * CH
    o_hid = off; off += 2 * FH * TILE
    o_small = off; off += 16640
    o_s0 = off; off += 33536
    o_kv = off; off += DEPTH * 16384
    assert off <= nc.sbuf_usable_end, (off, nc.sbuf_usable_end)
    assert 3 * KD * TILE <= 33536 + 16384

    xT = at("xT", [P, KD, NT], F32, o_x)
    a_hi = at("a_hi", [P, KD, NT], F32R, o_ah)
    a_lo = at("a_lo", [P, KD, NT], F32R, o_al)
    raw = at("raw", [P, 2, FH, P], F32, o_raw)
    w_hi = at("w_hi", [P, 2, FH, P], F32R, o_wh)
    w_lo = at("w_lo", [P, 2, FH, P], F32R, o_wl)
    h_hi = at("h_hi", [P, FH, NT], F32R, o_hid)
    h_lo = at("h_lo", [P, FH, NT], F32R, o_hid + FH * TILE)
    s = o_small
    ident = at("ident", [P, P], F32, s); s += 512
    ones = at("ones", [P, P], F32, s); s += 512
    zeros = at("zeros", [P, P], F32, s); s += 512
    eps = at("eps", [P, 1], F32, s); s += 32
    vec = at("vec", [P, NVEC], F32, s); s += 480
    assert s == o_small + 2048
    rstd = at("rstd", [P, NT], F32, s); s += TILE
    t1 = at("t1", [P, NT], F32, s); s += TILE
    t2 = at("t2", [P, NT], F32, s); s += TILE
    t3 = at("t3", [P, NT], F32, s); s += TILE
    t4 = at("t4", [P, NT], F32, s); s += TILE
    sqt = at("sqt", [P, NT], F32, s); s += TILE
    acc = at("acc", [P, NT], F32, s); s += TILE
    assert s <= o_small + 16640
    kT = [at(f"kT{l}", [P, KD, NM], F32, o_kv + l * 16384) for l in range(DEPTH)]
    vM = [at(f"vM{l}", [P, 2, D], F32, o_kv + l * 16384 + 8192) for l in range(DEPTH)]

    xin = at("xin", [P, 4, D], F32, o_hid)
    xsin = at("xsin", [NS, D], F32, o_hid + 16384)
    min_ = at("min_", [P, 2, D], F32, o_hid + 20480)
    vrows = at("vrows", [P, P], F32, o_hid + 28672)
    kOut = at("kOut", [P, 2, D], F32, o_hid)
    vT = at("vT", [P, KD, NM], F32, o_hid + 8192)
    mT = at("mT", [P, KD, NM], F32, o_s0)
    m_hi = at("m_hi", [P, KD, NM], F32R, o_s0 + 8192)
    m_lo = at("m_lo", [P, KD, NM], F32R, o_s0 + 16384)
    m_rstd = at("m_rstd", [P, NM], F32, o_s0 + 24576)
    m_acc = at("m_acc", [P, NM], F32, o_s0 + 25600)
    m_sq = at("m_sq", [P, NM], F32, o_s0 + 26624)
    qT = at("qT", [P, KD, NT], F32, o_s0)
    qb = at("qb", [P, 2, D], F32, o_ah)
    kc = at("kc", [P, 2, D], F32, o_ah + 8192)
    pP = at("pP", [P, 4, 2, NM], F32, o_ah + 16384)
    pT = at("pT", [P, 2, 2, SEQ], F32, o_ah + 24576)
    vc = [at(f"vc{q}", [P, 2, D], F32, (o_s0 + 16640, o_s0 + 24832, o_ah, o_ah + 8192)[q]) for q in range(4)]
    c = o_hid + KD * TILE
    qs = at("qs", [NS, D], F32, c); c += 4096
    c = o_hid + (FH + KD) * TILE
    sT = at("sT", [P, 2, NS * MH], F32, c); c += 256
    pS = at("pS", [NS * MH, NM], F32, c); c += 1024
    pW = at("pW", [P, 2, NS * MH], F32, c); c += 256
    mx = at("mx", [P, 8, 2], F32, c); c += 64
    nmx = at("nmx", [P, 8, 2], F32, c); c += 64
    den = at("den", [P, 8, 2], F32, c); c += 64
    rden = at("rden", [P, 8, 2], F32, c); c += 64
    ssm = at("ssm", [NS * MH, 4], F32, c); c += 32
    assert c <= o_hid + 2 * FH * TILE
    q_rows = nc.dram_tensor("q_rows", (DEPTH, NS, D), F32, kind="Internal").ap()
    hgQ = at("hgQ", [P, KD, NT], F32, o_hid)
    hgK = at("hgK", [P, KD, NT], F32, o_hid + KD * TILE)
    hgF = at("hgF", [P, KD, NT], F32, o_s0)
    hgV = at("hgV", [P, KD, NT], F32, o_s0 + KD * TILE)
    hgG = at("hgG", [P, KD, NT], F32, o_s0 + 2 * KD * TILE)
    lvl = [[at(f"lvl{e}{u}", [P, SEQ], F32, o_ah + 16384 * e + 2048 * u) for u in range(len(LEVELS))]
           for e in range(2)]
    dgQ = [at(f"dgQ{e}", [P, SEQ], F32, o_ah + 16384 * e + 6144) for e in range(2)]
    dgK = [at(f"dgK{e}", [P, SEQ], F32, o_ah + 16384 * e + 8192) for e in range(2)]
    inQ = [at(f"inQ{e}", [P, SEQ], F32, o_ah + 16384 * e + 10240) for e in range(2)]
    outK = [at(f"outK{e}", [P, SEQ], F32, o_ah + 16384 * e + 12288) for e in range(2)]
    ebt = [at(f"ebt{e}", [P, NHC], F32, o_ah + 16384 * e + 14336) for e in range(2)]
    sS = at("sS", [P, NS, HH, P], F32, o_ah)
    hS = at("hS", [P, NHC, P], F32, o_small + 2048 + TILE)
    bC = [at(f"bC{e}", [P, SEQ], F32, o_small + 2048 + TILE * (3 + e)) for e in range(2)]
    c = o_hid + 2 * KD * TILE
    attn = [at(f"attn{e}", [P, 4, P], F32, c + 2048 * e) for e in range(2)]; c += 4096
    vTok = at("vTok", [P, 4, P], F32, c); c += 2048
    kTok = at("kTok", [P, 4, P], F32, c); c += 2048
    pair_mask = at("pair_mask", [P, 4, P], F32, c); c += 2048
    lbv = at("lbv", [P, 6, HH], F32, c); c += 192
    fS = at("fS", [P, HH, NS], F32, c); c += 256
    chunk_start = at("chunk_start", [P, SEQ], F32, o_small + 2048 + TILE * 5)
    assert c <= o_hid + 2 * FH * TILE
    sX = at("sX", [UC, SG // 2, CS, SC], F32, o_hid)
    sY = at("sY", [YC, CS, 512], F32, o_hid)
    sFH = at("sFH", [P, NJ, 2, 1 + UC], F32, o_hid + 16384)
    c = o_hid + 37120
    par = at("par", [P, 96], F32, c); c += 384
    pw = at("pw", [P, 2, CS + 1, NJ], F32, c); c += 2304
    sm = at("sm", [P, 12, NJ], F32, c); c += 1536
    smi = at("smi", [P, NJ], I32, c); c += 128
    cw = at("cw", [P, 2, CB + 1, NJ], F32, c); c += 2304
    hfin = at("hfin", [P, 2, NJ], F32, c); c += 256
    prow = at("prow", [96, P], F32, c); c += 512
    ldrow = at("ldrow", [96, 2], F32, c); c += 32
    assert c <= o_hid + 2 * FH * TILE
    sc = [at(f"sc{e}", [P, NJ * NC], F32, o_hid + 8192 * e) for e in range(2)]
    sG = at("sG", [P, 2, NJ, CS + 1, SC], F32, o_hid)
    sF = at("sF", [P, 2, NJ, CS, SC], F32, o_s0)
    bRaw = at("bRaw", [P, 2, NJ, SC], F32, o_ah)
    bBar = at("bBar", [P, 2, NJ, SC], F32, o_ah + 4096)
    cRaw = at("cRaw", [P, 2, 4, P], F32, o_ah + 8192)
    cT = at("cT", [P, 2, NJ, SC], F32, o_ah + 12288)
    sTmp = at("sTmp", [P, NJ * (CS + 1) * SC], F32, o_al - 256)
    sFst = at("sFst", [P, 2, 512], F32, o_ah + 8192)
    sK = at("sK", [SC, SG, P], F32, o_ah)
    u32 = at("u32", [P, KD, NT], F32, o_al)
    sZ = at("sZ", [P, 2, CS, UC], F32, o_ah)
    hs0 = at("hs0", [P, 2, NS, NJ], F32, o_ah + 5120)
    hs1 = at("hs1", [P, 2, NS, NJ], F32, o_ah + 7168)
    hst = at("hst", [P, 2, NS, NJ], F32, o_ah + 9216)
    hrow = at("hrow", [P, 2, 2, P], F32, o_ah + 11264)
    frow = at("frow", [64, P], F32, o_ah + 13312)
    sU = at("sU", [P, SG, UC], F32, o_s0)
    sTab = at("sTab", [P, 2, 768], F32, o_s0 + 20480)
    sTabF = at("sTabF", [P, 2, 512], F32, o_s0 + 26624)
    s5_fg = nc.dram_tensor("s5_fg", (NJ, P, 512), F32, kind="Internal").ap()
    s5_k = nc.dram_tensor("s5_k", (SG, SC, 2 * P - SC), F32, kind="Internal").ap()
    yT = at("yT", [P, KD, NT], F32, o_ah)
    yout = at("yout", [P, 4, D], F32, o_hid)
    ysout = at("ysout", [NS, D], F32, o_hid + 16384)

    lin = nc.alloc_psum_tensor("lin", [P, 2, 2, 512], F32)
    mis = nc.alloc_psum_tensor("mis", [P, 4, 512], F32)

    def lslot(j, n=NT):
        return lin[:, j, :, 0:HT] if n == NT else lin[:, j, 0, 0:n]

    def two(ap):
        return ap.rearrange("p (a b) -> p a b", a=2)

    def tile(t, m):
        return t[:, bass.ds(m, 1), :].rearrange("p o n -> p (o n)")

    def twotile(t, m):
        return t[:, bass.ds(m, 1), :].rearrange("p o (a b) -> p (o a) b", a=2)

    def sem(name):
        return nc.alloc_semaphore(name)

    loaded = sem("loaded")
    vrows_loaded = sem("vrows_loaded")
    raw_arrived = [sem("raw_arrived0"), sem("raw_arrived1")]
    hi_ready = sem("hi_ready")
    lo_ready = sem("lo_ready")
    chunk_done = sem("chunk_done")
    used = [sem("used0"), sem("used1")]
    a_hi_done = sem("a_hi_done")
    a_lo_done = sem("a_lo_done")
    squares_done = sem("squares_done")
    sums_done = sem("sums_done")
    root_done = sem("root_done")
    gate_out = sem("gate_out")
    h_hi_done = sem("h_hi_done")
    h_lo_done = sem("h_lo_done")
    dve_step, act_step, pool_step = sem("dve_step"), sem("act_step"), sem("pool_step")
    f_out = sem("f_out")
    gated = sem("gated")
    s5_rows, s5_bc, s5_small = sem("s5_rows"), sem("s5_bc"), sem("s5_small")
    s5_coef, s5_sin, s5_phase = sem("s5_coef"), sem("s5_sin"), sem("s5_phase")
    s5_tables_made = sem("s5_tables_made")
    s5_fill, s5_void = sem("s5_fill"), {"dve": sem("s5_void_dve"), "act": sem("s5_void_act")}
    s5_f_out = [sem("s5_f_out0"), sem("s5_f_out1")]
    s5_tab_out, s5_zeros_out = sem("s5_tab_out"), sem("s5_zeros_out")
    s5_state_in, s5_state_out = sem("s5_state_in"), sem("s5_state_out")
    s5_u, s5_z, s5_scanned, s5_gelu, s5_fin = sem("s5_u"), sem("s5_z"), sem("s5_scanned"), sem("s5_gelu"), sem("s5_fin")
    s5_tab_in = [sem("s5_tab_in0"), sem("s5_tab_in1")]
    s5_tabf_in = [sem("s5_tabf_in0"), sem("s5_tabf_in1")]
    s5_tab_used = sem("s5_tab_used")
    s5_tables_f = sem("s5_tables_f")
    s5_tab_clear = sem("s5_tab_clear")
    s5_state_done = sem("s5_state_done")
    xa = []
    for l in range(DEPTH):
        xa.append(dict(fill=sem(f"xa_fill{l}"), void={"dve": sem(f"xa_void_dve{l}"), "act": sem(f"xa_void_act{l}")},
                       max=sem(f"xa_max{l}"), exp=sem(f"xa_exp{l}"), prob=sem(f"xa_prob{l}"), q_out=sem(f"xa_q_out{l}"),
                       qb=[sem(f"xa_qb0{l}"), sem(f"xa_qb1{l}")], kc=[sem(f"xa_kc0{l}"), sem(f"xa_kc1{l}")],
                       score=sem(f"xa_score{l}"), vc=[sem(f"xa_vc{q}{l}") for q in range(4)], pv=sem(f"xa_pv{l}"),
                       s_max=sem(f"xa_s_max{l}"), s_exp=sem(f"xa_s_exp{l}"), s_prob=sem(f"xa_s_prob{l}"),
                       o_hi=sem(f"xa_o_hi{l}")))
    hg = {name: sem("hg_" + name) for name in
          ("fill", "void_dve", "void_act", "lb_diff", "lb_exp", "lb", "consts", "log", "decay", "exps", "scaled_pool",
           "scaled_dve", "state", "state_out", "s_decay", "s_state", "s_out", "squares", "root", "normed")}
    hg_s_in = [sem(f"hg_s_in{b}") for b in range(NS)]
    consts_done = sem("consts_done")
    vec_tr, vec_done = sem("vec_tr"), sem("vec_done")
    in_tr, in_evac = sem("in_tr"), sem("in_evac")
    mem_squares, mem_sums, mem_root, mem_rstd = sem("mem_squares"), sem("mem_sums"), sem("mem_root"), sem("mem_rstd")
    m_hi_done, m_lo_done = sem("m_hi_done"), sem("m_lo_done")
    kv_tr, kv_evac, kv_out = sem("kv_tr"), sem("kv_evac"), sem("kv_out")
    y_normed, y_tr, y_evac, y_out = sem("y_normed"), sem("y_tr"), sem("y_evac"), sem("y_out")

    def weights(n, i, j):
        name, layer, _, kt = ST[n]
        if name in ("k", "v"):
            w, c = i_["xattn_w_kv"][layer], (2 * i + j) * P + (D if name == "v" else 0)
        elif name[:3] == "ffn" and name[4:7] == "_in":
            half = int(name[7])
            w, c = i_[f"ffn{name[3]}_w_in"][layer], (i + half * FH) * P + j * FFN
        elif name[:3] == "ffn":
            half = int(name[8])
            w = i_[f"ffn{name[3]}_w_out"][layer][half * FH * P:(half + 1) * FH * P, :]
            c = (2 * i + j) * P
        elif name == "glu":
            return i * P, i_["s5_w_glu"][0].rearrange("(k p) (a n) -> p k a n", p=P, a=2)[:, :, 1 - j, :]
        elif name == "hg_qf":
            w, c = i_["hg_w_in"][0], i * P + j * D
        elif name == "hg_vg":
            w, c = i_["hg_w_in"][0], i * P + (2 + j) * D
        elif name == "hg_out":
            w, c = i_["hg_w_out"][0], (2 * i + j) * P
        elif name == "xq":
            w, c = i_["xattn_w_q"][layer], (2 * i + j) * P
        else:
            w, c = i_["xattn_w_o"][layer], (2 * i + j) * P
        return c, w.rearrange("(k p) n -> p k n", p=P)

    def over_pairs(eng, n, body):
        name, layer, pairs, _ = ST[n]
        p0 = first_pair[name, layer]
        body(p0, 0, True, False)
        with eng.Fori(0, pairs - 2) as i:
            body(p0 + 1 + i, 1 + i, False, False)
        body(p0 + pairs - 1, pairs - 1, False, True)

    def tiles_of(n, p, j, last):
        if j == 0 or not last:
            return ST[n][3]
        return ST[n + 1][3] if n + 1 < len(ST) else None

    def from_hidden(name):
        return FH if name[:3] == "ffn" and "_out" in name else KD if name in ("glu", "xo", "hg_out") else 0

    def hidden_before(n):
        return sum(from_hidden(s_[0]) for s_ in ST[:n])

    def number(name, layer=0):
        return next(n for n, s_ in enumerate(ST) if s_[:2] == (name, layer))

    def gate_base(n):
        per = {"ffn1_in0": FH, "ffn1_in1": FH, "ffn2_in0": FH, "ffn2_in1": FH, "hg_qf": 8, "hg_vg": 8}
        return sum(per.get(s_[0], 0) for s_ in ST[:n])

    def is_in(name):
        return name[:3] == "ffn" and "_in" in name

    def is_out(name):
        return (name[:3] == "ffn" and "_out" in name) or name in ("xo", "hg_out")

    def wait(eng, semaphore, value):
        if isinstance(value, int) and value <= 0:
            return
        eng.wait_ge(semaphore, value)

    made = [("Q", 0, "dve"), ("Q", 1, "dve"), ("S", (0, 0), "act"), ("S", (0, 1), "act")]
    for h in range(MH):
        made += [("S", (h + 1, e), "act") for e in range(2) if h + 1 < MH]
        made += [("P", (h, e), "act" if e else "dve") for e in range(2)]
        made += [("O", (h, e), "dve") for e in range(2)]
    made += [("T", 0, "act"), ("W", 0, "dve"), ("V", 0, "dve")]
    XAG = [Groups(made, xa[l]["fill"], xa[l]["void"]) for l in range(DEPTH)]
    XA_SCALE = 1.0 / math.sqrt(D // MH)

    made = []
    for h in range(HH + 1):
        if h < HH:
            made += [("A", (h, u), "dve") for u in range(len(LEVELS) + 1)]
        if h:
            made += [("O", h - 1, "act")]
        if h < HH:
            made += [("V", h, "act"), ("K", h, "act"), ("D", (h, 0), "dve"), ("D", (h, 1), "dve")]
    made += [("B", (b, e), "dve") for b in range(NS) for e in range(2)]
    made += [("S", 0, "dve")]
    made += [("N", (h, e), "act") for h in range(HH) for e in range(2)]
    HG = Groups(made, hg["fill"], {"dve": hg["void_dve"], "act": hg["void_act"]}, banks=8)

    EXPS, DECAYS = 3 + len(LEVELS), 3 + len(LEVELS)

    def hg_bank(q):
        q %= 8
        return mis[:, q, :] if q < 4 else lin[:, (q - 4) // 2, q % 2, :]

    made = [("par", 0, "dve"), ("c", 0, "dve"), ("c", 1, "dve")]
    made += [("F", q, "act") for q in range(NJ // 2)]
    made += [("K", q, "act" if q % 2 else "dve") for q in range(SG // 4)]
    S5_MADE = len(made)
    made += [("h0", 0, "dve")]
    for hf in range(2):
        made += [("X", (4 * hf + f, e), "act") for f in range(4) for e in range(2)]
        made += [("U", 8 * hf + q, "dve" if q % 2 else "act") for q in range(8)]
    made += [("FU", q, "dve" if q % 2 else "act") for q in range(NJ // 2)]
    made += [("hfin", 0, "dve"), ("hs1", 0, "dve")]
    for hf in range(2):
        made += [("Y", 8 * hf + q, "dve" if q % 2 else "act") for q in range(8)]
        made += [("y", (4 * hf + f, e), "dve") for f in range(4) for e in range(2)]
    S5G = Groups(made, s5_fill, s5_void)
    s5_norm = next((r for r, (b, l) in enumerate(BLOCKS) if b == "s5"), None)

    block = nc.Block()
    with block:
        @block.sync
        def _(sp):
            sp.dma_start(xin[:], i_["x_prompt"][0].rearrange("(t p) d -> p t d", p=P)).then_inc(loaded, 16)
            sp.dma_start(xsin[:], i_["x_sample"].rearrange("b o d -> (b o) d")).then_inc(loaded, 16)
            sp.dma_start(min_[:], i_["mem_prompt"][0].rearrange("(t p) d -> p t d", p=P)).then_inc(loaded, 16)

            def caches(layer):
                X = xa[layer]

                def values(b):
                    sp.dma_start(vc[b % 4][:], i_["cache_mem_v"][layer, b].rearrange("(t p) h d -> p t (h d)", p=P))\
                        .then_inc(X["vc"][b % 4], 16)

                sp.wait_ge(chunk_done, 2 * first_pair["xq", layer] + 1)
                for b in range(2):
                    values(b)
                sp.wait_ge(chunk_done, 2 * first_pair["xo", layer])
                for q in range(2 * NS):
                    wait(sp, X["score"], q - 1)
                    b, t = q // 2, q % 2
                    sp.dma_start(kc[:, q % 2, :], i_["cache_mem_k"][layer, b, t * P:(t + 1) * P]
                                 .rearrange("p h d -> p (h d)")).then_inc(X["kc"][q % 2], 16)
                sp.wait_ge(X["score"], 2 * NS)
                for b in range(2, NS):
                    wait(sp, X["pv"], b - 3)
                    values(b)

            def s5_tables(sp):
                sp.wait_ge(chunk_done, 2 * first_pair["glu", 0])
                for q, name in enumerate(("s5_a_re", "s5_a_im")):
                    sp.dma_start(prow[32 * q:32 * q + 32, :], i_[name][0].rearrange("(j g) p -> j (g p)", g=2))\
                        .then_inc(s5_rows, 16)
                sp.dma_start(ldrow[64:96, :], i_["s5_log_dt"][0].rearrange("(j g) -> j g", g=2)).then_inc(s5_rows, 16)
                for q, name in enumerate(("s5_b_re", "s5_b_im")):
                    b = i_[name][0].rearrange("(j g) p c -> g p j c", g=2)
                    for g in range(2):
                        sp.dma_start(bRaw[64 * g:64 * g + 64, q], b[g]).then_inc(s5_bc, 16)
                for q, name in enumerate(("s5_c_re", "s5_c_im")):
                    for b in range(4):
                        for g in range(2):
                            src = i_[name][0][16 * b:16 * b + 16].rearrange("(j g) c p -> g j c p", g=2)
                            for j in range(8):
                                sp.dma_start(cRaw[16 * j:16 * j + 16, q, b, 64 * g:64 * g + 64], src[g, j])\
                                    .then_inc(s5_bc, 16)
                for q in range(NJ // 2):
                    S = S5G.first("F") + q
                    sp.wait_ge(s5_void["act"], S5G.before(S + 1, "act"))
                    sp.dma_start(s5_fg[2 * q:2 * q + 2, :, 0:256].rearrange("j p n -> p j n"),
                                 sFst[:, q % 2, :].rearrange("p (j n) -> p j n", j=2)).then_inc(s5_f_out[q % 2], 16)
                sp.wait_ge(s5_tables_made, 1)
                for e in range(2):
                    sp.dma_start(s5_fg[:, :, 256 + P * e:256 + P * (e + 1)].rearrange("j p n -> p j n"),
                                 sG[:, e, :, 1:, :].rearrange("p j d c -> p j (d c)")).then_inc(s5_tab_out, 16)
                S5G.all_emptied(sp, S5G.after("K"))
                sp.dma_start(s5_k[:, :, 7 * SC:].rearrange("g c n -> c g n"), sK[:]).then_inc(s5_tab_out, 16)
                sp.wait_ge(s5_tab_out, 16 * 3)
                sp.wait_ge(s5_zeros_out, 16)
                sp.wait_ge(s5_f_out[0], 16 * NJ // 4)
                sp.wait_ge(s5_f_out[1], 16 * NJ // 4)
                for q, name in enumerate(("state_s5_re", "state_s5_im")):
                    rows = i_[name][0].rearrange("b (j g) p -> (b j) (g p)", g=2)
                    for e in range(2):
                        sp.dma_start(hrow[:, q, e, :], rows[e * P:(e + 1) * P, :]).then_inc(s5_state_in, 16)
                for q in range(NJ // 2):
                    if q >= 2:
                        sp.wait_ge(s5_fill, S5G.first("FU") + q - 1)
                    sp.dma_start(sTabF[:, q % 2, :].rearrange("p (j n) -> p j n", j=2),
                                 s5_fg[2 * q:2 * q + 2, :, 0:256].rearrange("j p n -> p j n"))\
                        .then_inc(s5_tabf_in[q % 2], 16)
                for q in range(NJ):
                    if q == 0:
                        sp.wait_ge(s5_tab_clear, 1)
                    if q < 2:
                        pass
                    elif q % 2 == 0:
                        sp.wait_ge(s5_tab_used, q // 2)
                    else:
                        sp.wait_ge(s5_fill, S5G.at("Y", q // 2 - 1) + 1)
                    for g in range(2):
                        k = s5_k[2 * q + g]
                        src = bass.AP(tensor=k.tensor, offset=k.offset, ap=[[SC, CS], [2 * P - SC, SC], [1, P]])
                        sp.dma_start(sTab[:, q % 2, g * P:(g + 1) * P], src).then_inc(s5_tab_in[q % 2], 16)
                        sp.dma_start(sTab[64 * g:64 * g + 64, q % 2, 256 + 256 * g:512 + 256 * g],
                                     s5_fg[q, 64 * g:64 * g + 64, 256:512]).then_inc(s5_tab_in[q % 2], 16)
                rows = hfin_out = None
                sp.wait_ge(s5_fin, 1)
                sp.dma_start(o_["s5_re_p"][0, 0].rearrange("(j g) p -> j (g p)", g=2), frow[0:32, :])\
                    .then_inc(s5_state_out, 16)
                sp.dma_start(o_["s5_im_p"][0, 0].rearrange("(j g) p -> j (g p)", g=2), frow[32:64, :])\
                    .then_inc(s5_state_out, 16)
                sp.wait_ge(s5_fin, 2)
                for q, name in enumerate(("s5_re_s", "s5_im_s")):
                    rows = o_[name][0].rearrange("b (j g) p -> (b j) (g p)", g=2)
                    for e in range(2):
                        sp.dma_start(rows[e * P:(e + 1) * P, :], hrow[:, q, e, :]).then_inc(s5_state_out, 16)
                sp.wait_ge(s5_state_out, 16 * 6)

            def states():
                for h in range(HH):
                    sp.wait_ge(hg["state"], h + 1)
                    sp.dma_start(o_["hg_p"][0, 0, h], hS[:, NHC - 1, :]).then_inc(hg["state_out"], 16)
                for b in range(NS):
                    sp.wait_ge(hg["fill"], HG.at("O", HH - 2 if b < NS // 2 else HH - 1) + 1)
                    sp.dma_start(sS[:, b], i_["state_hgrn"][0, b].rearrange("h k v -> k h v")).then_inc(hg_s_in[b], 16)
                for b in range(NS):
                    sp.wait_ge(hg["s_state"], 2 * (b + 1))
                    sp.dma_start(o_["hg_s"][0, b].rearrange("h k v -> k h v"), sS[:, b]).then_inc(hg["s_out"], 16)
                sp.wait_ge(hg["s_out"], 16 * NS)

            def stream(n):
                def body(p, i, first, last):
                    for j in range(2):
                        column, src = weights(n, i, j)
                        if ST[n][0] == "glu" and not (first or last):
                            if j == 0:
                                sp.wait_ge(lo_ready, 2 * p)
                        else:
                            wait(sp, lo_ready, 2 * p + j - 1)
                        sp.dma_start(raw[:, j, 0:ST[n][3], :], src[:, :, bass.ds(column, P)])\
                            .then_inc(raw_arrived[j], 16)
                        if first and j == 0 and ST[n][0] == "glu":
                            s5_tables(sp)
                        if first and j == 0 and ST[n][0] == "xo":
                            caches(ST[n][1])
                        if first and j == 0 and ST[n][0] == "hg_out":
                            states()
                over_pairs(sp, n, body)

            for n in range(len(ST)):
                stream(n)
            for t in range(4):
                sp.wait_ge(y_evac, 2 * (t + 1))
                sp.dma_start(o_["y_prompt"][0, t * P:(t + 1) * P, :], yout[:, t, :]).then_inc(y_out, 16)
            sp.wait_ge(y_evac, 10)
            sp.dma_start(o_["y_sample"].rearrange("b o d -> (b o) d"), ysout[:]).then_inc(y_out, 16)
            sp.wait_ge(y_out, 16 * 5)
            sp.wait_ge(kv_out, 16 * 2 * DEPTH)
            if any(s_[0] == "hg_out" for s_ in ST):
                sp.wait_ge(hg["state_out"], 16 * HH)

        @block.gpsimd
        def _(pool):
            step = Chain(pool, pool_step)
            pool.memset(ones[:], 1.0).then_inc(consts_done, 1)
            pool.memset(eps[:], EPS).then_inc(consts_done, 1)
            step.link(pool.memset(ident[:], 0.0))
            pool.affine_select(out=ident[:], in_=ident[:], compare_op=ALU.not_equal, fill=1.0, base=0,
                               pattern=[[-1, P]], channel_multiplier=1).then_inc(consts_done, 1)
            pool.memset(zeros[:], 0.0).then_inc(consts_done, 1)
            step.link(pool.memset(vrows[:], 0.0))
            for name, row in (("ffn1_norm", V_FFN1), ("mix_norm", V_MIX), ("xattn_norm", V_XA), ("mem_norm", V_MEM),
                              ("ffn2_norm", V_FFN2), ("hg_lb_logits", V_LB)):
                pool.dma_start(vrows[row:row + 2 * KD, :], i_[name].rearrange("l (k p) -> (l k) p", p=P))\
                    .then_inc(vrows_loaded, 16)
            pool.dma_start(vrows[V_FIN:V_FIN + KD, :], i_["final_norm"].rearrange("(k p) -> k p", p=P))\
                .then_inc(vrows_loaded, 16)
            pool.dma_start(vrows[V_D:V_D + KD, :], i_["s5_d"][0].rearrange("(k g) c -> k (g c)", k=KD))\
                .then_inc(vrows_loaded, 16)
            pool.dma_start(vrows[V_HG:V_HG + 1, :], i_["hg_norm"]).then_inc(vrows_loaded, 16)

            pool.wait_ge(in_evac, KD + 1 + 4)
            step.link(pool.tensor_tensor(m_acc[:], mT[:, 0, :], mT[:, 0, :], ALU.mult))
            for m in range(1, KD):
                step.link(pool.tensor_tensor(m_sq[:], mT[:, m, :], mT[:, m, :], ALU.mult))
                ins = pool.tensor_tensor(m_acc[:], m_acc[:], m_sq[:], ALU.add)
                if m < KD - 1:
                    step.link(ins)
                else:
                    ins.then_inc(mem_squares, 1)

            pool.wait_ge(in_evac, KD + 1)
            step.link(pool.tensor_tensor(acc[:], xT[:, 0, :], xT[:, 0, :], ALU.mult))
            for m in range(1, KD):
                step.link(pool.tensor_tensor(sqt[:], xT[:, m, :], xT[:, m, :], ALU.mult))
                ins = pool.tensor_tensor(acc[:], acc[:], sqt[:], ALU.add)
                if m < KD - 1:
                    step.link(ins)
                else:
                    ins.then_inc(squares_done, 1)

            def squares(n, r):
                one = ST[n][0] == "glu"
                pool.wait_ge(sums_done, r)

                def body(p, i, first, last):
                    if not first and not last:
                        step.loop(i, 1, 2 if one else 4)
                    for j in range(1 if one else 2):
                        m = i if one else 2 * i + j
                        pool.wait_ge(used[1 if one else j], p + 1)
                        if first and j == 0:
                            step.link(pool.tensor_tensor(acc[:], xT[:, 0, :], xT[:, 0, :], ALU.mult))
                            continue
                        step.link(pool.tensor_tensor(sqt[:], tile(xT, m), tile(xT, m), ALU.mult))
                        ins = pool.tensor_tensor(acc[:], acc[:], sqt[:], ALU.add)
                        if last and j == (0 if one else 1):
                            ins.then_inc(squares_done, 1)
                        else:
                            step.link(ins)
                    if not first and not last:
                        step.done(ST[n][2] - 2)
                over_pairs(pool, n, body)

            def attend(layer):
                X = xa[layer]
                pool.wait_ge(X["void"]["dve"], 2)
                pool.dma_start(q_rows[layer], qs[:]).then_inc(X["q_out"], 16)
                pool.wait_ge(X["q_out"], 16)
                for b in range(NS):
                    wait(pool, X["score"], 2 * (b - 1))
                    pool.dma_start(qb[:, b % 2, :], q_rows[layer, b:b + 1, :].to_broadcast([P, D]))\
                        .then_inc(X["qb"][b % 2], 16)

            def s5():
                pool.wait_ge(consts_done, 4)
                pool.dma_start(s5_k[:, :, 0:7 * SC].rearrange("g c n -> c g n"),
                               zeros[0:SC, 0:7 * SC].unsqueeze(1).to_broadcast([SC, SG, 7 * SC]))                    .then_inc(s5_zeros_out, 16)
                pool.wait_ge(s5_fill, S5G.after("K"))
                pool.memset(sTab[:], 0.0).then_inc(s5_tab_clear, 1)

            def hgrn():
                first = number("hg_out", 1)
                pool.wait_ge(chunk_done, 2 * first_pair[ST[first][:2]])
                pool.wait_ge(used[1], first_pair[ST[first][:2]])
                step.link(pool.memset(pair_mask[:], 0.0))
                for e in range(2):
                    pool.memset(attn[e][:], 0.0)
                step.link(pool.memset(chunk_start[:], 1.0))
                step.link(pool.memset(chunk_start[:].rearrange("p (n t) -> p n t", t=HC)[:, :, 0], 0.0))
                for u, level in enumerate(LEVELS):
                    m = pair_mask[:, u, :].rearrange("p (b t) -> p b t", t=2 * level)
                    step.link(pool.memset(m[:, :, level:], 1.0))
                    step.link(pool.affine_select(out=m, in_=m, compare_op=ALU.is_ge, fill=0.0, base=0,
                                                 pattern=[[-2 * level, P // (2 * level)], [0, 2 * level]],
                                                 channel_multiplier=1))
                    step.link(pool.affine_select(out=m, in_=m, compare_op=ALU.is_ge, fill=0.0, base=level - 1,
                                                 pattern=[[2 * level, P // (2 * level)], [0, 2 * level]],
                                                 channel_multiplier=-1))
                m = pair_mask[:, len(LEVELS), :].rearrange("p (b t) -> p b t", t=8)
                step.link(pool.memset(m, 1.0))
                step.link(pool.affine_select(out=m, in_=m, compare_op=ALU.is_ge, fill=0.0, base=0,
                                             pattern=[[-8, P // 8], [0, 8]], channel_multiplier=1))
                step.link(pool.affine_select(out=m, in_=m, compare_op=ALU.is_ge, fill=0.0, base=0,
                                             pattern=[[8, P // 8], [1, 8]], channel_multiplier=-1))
                pool.nop().then_inc(hg["consts"], 1)
                for h in range(HH):
                    e = h % 2
                    pool.wait_ge(hg["exps"], EXPS * h + 1)
                    pool.tensor_tensor(inQ[e][:], inQ[e][:], hgQ[:, h, 0:SEQ], ALU.mult).then_inc(hg["scaled_pool"], 1)
                    for u, level in enumerate(LEVELS):
                        pool.wait_ge(hg["exps"], EXPS * h + 2 + u)
                        q, k, w = (t.rearrange("p (b a t) -> p b a t", a=2, t=level)
                                   for t in (hgQ[:, h, 0:SEQ], hgK[:, h, 0:SEQ], lvl[e][u][:]))
                        pool.tensor_tensor(w[:, :, 1], w[:, :, 1], q[:, :, 1], ALU.mult)
                        pool.tensor_tensor(w[:, :, 0], w[:, :, 0], k[:, :, 0], ALU.mult).then_inc(hg["scaled_pool"], 1)

            for n in range(len(ST)):
                if ST[n][0] == "glu":
                    s5()
                if ST[n][0] == "hg_out":
                    hgrn()
                if ST[n][0] == "xo":
                    attend(ST[n][1])
                if ST[n][:2] in norm_after:
                    squares(n, norm_after[ST[n][:2]])
                if ST[n][0] == "v":
                    layer = ST[n][1]
                    pool.wait_ge(kv_evac, 8 * layer + 4)
                    pool.dma_start(o_["mem_k"][layer, 0].rearrange("(t p) h d -> p t (h d)", p=P), kOut[:])\
                        .then_inc(kv_out, 16)
                    pool.wait_ge(kv_evac, 8 * layer + 8)
                    pool.dma_start(o_["mem_v"][layer, 0].rearrange("(t p) h d -> p t (h d)", p=P), vM[layer][:])\
                        .then_inc(kv_out, 16)

        @block.scalar
        def _(act):
            step = Chain(act, act_step)

            def split(p, j, kt):
                if kt is None:
                    return
                act.wait_ge(raw_arrived[j], 16 * (p + 1))
                wait(act, chunk_done, 2 * p + j - 1)
                act.activation(w_hi[:, j, 0:kt, :], raw[:, j, 0:kt, :], ACT.Copy).then_inc(hi_ready, 1)

            def root(r):
                act.wait_ge(sums_done, r + 1)
                act.activation(two(t1[:]), mis[:, 0:2, 0:HT], ACT.Sqrt, bias=eps[:, 0:1],
                               scale=1.0 / D).then_inc(root_done, 1)

            def gain_hi(m, row):
                act.activation(tile(a_hi, m), tile(xT, m), ACT.Copy,
                               scale=vec[:, bass.ds(row + m, 1)]).then_inc(a_hi_done, 1)

            act.wait_ge(consts_done, 4)
            act.wait_ge(vec_done, 1)
            act.wait_ge(in_evac, KD + 1)
            for m in range(KD):
                gain_hi(m, NORM_ROW[0])
            act.wait_ge(mem_sums, 1)
            act.activation(m_sq[:], mis[:, 2, 0:NM], ACT.Sqrt, bias=eps[:, 0:1], scale=1.0 / D)\
                .then_inc(mem_root, 1)
            split(0, 0, ST[0][3])

            def attend(layer):
                G, X = XAG[layer], xa[layer]
                for q, (what, a, owner) in enumerate(G.groups):
                    bank = mis[:, q % 4, :]
                    if what == "O":
                        h, e = a
                        act.wait_ge(X["fill"], q + 1)
                        act.activation(h_hi[:, 2 * h + e, 0:SEQ], bank, ACT.Copy).then_inc(X["o_hi"], 1)
                    if what == "V":
                        act.wait_ge(X["fill"], q + 1)
                        act.activation(h_hi[:, 0:KD, SEQ:NT], bank[:, 0:KD * NS].rearrange("p (k b) -> p k b", k=KD),
                                       ACT.Copy).then_inc(h_hi_done, KD)
                    if owner != "act":
                        continue
                    if what == "S":
                        h, e = a
                        act.wait_ge(X["max"], 2 * h + e + 1)
                        if h >= 2:
                            act.wait_ge(X["fill"], G.at("P", (h - 2, e)) + 1)
                        for t in range(2):
                            u = 2 * h + e
                            ins = act.activation(pP[:, u % 4, t, :], bank[:, t * NM:(t + 1) * NM], ACT.Exp,
                                                 bias=nmx[:, u, t:t + 1], scale=XA_SCALE, accum_out=den[:, u, t:t + 1])
                        ins.then_inc(X["void"]["act"], 1)
                    elif what == "P":
                        h, e = a
                        act.wait_ge(X["fill"], q + 1)
                        if h >= 2:
                            act.wait_ge(X["fill"], G.at("O", (h - 2, 1)) + 1)
                        act.activation(pT[:, h % 2, :, 256 * e:256 * e + 256],
                                       bank.rearrange("p (m t) -> p m t", m=2), ACT.Copy).then_inc(X["void"]["act"], 1)
                    elif what == "T":
                        act.wait_ge(X["s_max"], 1)
                        act.activation(pS[:], bank[0:NS * MH, 0:NM], ACT.Exp, bias=ssm[:, 1:2], scale=XA_SCALE,
                                       accum_out=ssm[:, 2:3]).then_inc(X["void"]["act"], 1)

            def s5():
                G = S5G
                act.wait_ge(s5_phase, 1)
                act.activation(sm[:, 4, :], sm[:, 3, :], ACT.Sin).then_inc(s5_sin, 1)
                act.activation(sm[:, 5, :], sm[:, 3, :], ACT.Sin, scale=0.5).then_inc(s5_sin, 1)
                for q, (what, a, owner) in enumerate(G.groups):
                    if q == S5_MADE:
                        root(s5_norm)
                    if owner != "act":
                        continue
                    act.wait_ge(s5_fill, q + 1)
                    bank = mis[:, q % 4, :]
                    if what == "F":
                        if a >= 2:
                            act.wait_ge(s5_f_out[a % 2], 16 * (a // 2))
                        dst, src = sFst[:, a % 2, :], bank
                    elif what == "K":
                        if a == 1:
                            for e in range(2):
                                act.wait_ge(s5_f_out[e], 16 * NJ // 4)
                            act.wait_ge(s5_tables_made, 1)
                        dst, src = sK[:, 8 * (a // 2) + a % 2:8 * (a // 2) + 8:2, :], bank[0:SC, :].rearrange("p (g n) -> p g n", g=4)
                    elif what == "X":
                        f, e = a
                        if f == 4 and e == 0:
                            G.all_emptied(act, G.first("U") + 8)
                            act.wait_ge(s5_fill, G.first("U") + 8)
                        dst = sX[:, 8 * (f % 4):8 * (f % 4) + 8, 4 * (1 - e):4 * (1 - e) + 4, :]                            .rearrange("n g s c -> n s g c")
                        src = bank[0:UC, :].rearrange("n (s g c) -> n s g c", s=4, g=8)
                    elif what == "U":
                        dst, src = sU[:, 4 * a:4 * a + 4, :], bank[:, 0:4 * UC].rearrange("p (g n) -> p g n", g=4)
                    elif what == "FU":
                        dst = sFH[:, 2 * a:2 * a + 2, :, 1:]
                        src = bank[:, 0:4 * UC].rearrange("p (j e n) -> p j e n", j=2, e=2)
                    elif what == "Y":
                        if a == 0:
                            act.wait_ge(s5_fill, G.after("X"))
                        if a == 8:
                            act.wait_ge(s5_fill, G.first("y") + 8)
                        dst = sY[:, :, 64 * (a % 8):64 * (a % 8) + 64].rearrange("n t (g c) -> n t g c", g=4)
                        src = bank[0:YC, :].rearrange("n (g t c) -> n t g c", g=4, t=CS)
                    act.activation(dst, src, ACT.Copy).then_inc(s5_void["act"], 1)
                for k in range(KD):
                    act.wait_ge(s5_void["dve"], G.before(G.first("y") + (2 * k + 2 if k < 4 else 2 * k + 10), "dve"))
                    if k >= 2:
                        act.wait_ge(h_lo_done, hidden_before(number("glu")) + k - 1)
                    t = (t3, t4)[k % 2]
                    step.link(act.activation(t[:], u32[:, k, :], ACT.Gelu_apprx_tanh))
                    if k == 0:
                        act.wait_ge(s5_state_done, 1)
                    act.activation(h_hi[:, k, :], t[:], ACT.Copy).then_inc(h_hi_done, 1)

            def hgrn():
                G, x = HG, hidden_before(number("hg_out", 1))
                act.wait_ge(hg["lb_diff"], 1)
                act.activation(lbv[:, 2:4], lbv[:, 0:2], ACT.Exp).then_inc(hg["lb_exp"], 1)
                act.wait_ge(hg["lb"], 1)
                act.wait_ge(gated, 2 * HH)

                def decays(h):
                    e = h % 2
                    act.activation(hgK[:, h, :], hgK[:, h, :], ACT.Copy, scale=lbv[:, 5, h:h + 1])
                    if h >= 2:
                        act.wait_ge(hg["decay"], DECAYS * (h - 1))
                    act.activation(bC[e][:], hgF[:, h, 0:SEQ], ACT.Ln, bias=lbv[:, 4, h:h + 1],
                                   scale=lbv[:, 5, h:h + 1]).then_inc(hg["log"], 1)
                    act.wait_ge(hg["decay"], DECAYS * h + 1)
                    if h >= 2:
                        act.wait_ge(hg["fill"], G.at("O", h - 2) + 1)
                    act.activation(ebt[e][:], bC[e][:].rearrange("p (n t) -> p n t", t=HC)[:, :, HC - 1], ACT.Exp)
                    act.activation(inQ[e][:], bC[e][:], ACT.Exp).then_inc(hg["exps"], 1)
                    for u in range(len(LEVELS)):
                        act.wait_ge(hg["decay"], DECAYS * h + 2 + u)
                        act.activation(lvl[e][u][:], lvl[e][u][:], ACT.Exp).then_inc(hg["exps"], 1)
                    act.wait_ge(hg["decay"], DECAYS * h + 2 + len(LEVELS))
                    act.activation(dgK[e][:], dgQ[e][:], ACT.Exp, scale=-1.0)
                    step.link(act.activation(dgQ[e][:], dgQ[e][:], ACT.Exp))
                    act.wait_ge(hg["decay"], DECAYS * (h + 1))
                    act.activation(outK[e][:], outK[e][:], ACT.Exp).then_inc(hg["exps"], 2)

                def outputs(h):
                    q = G.at("O", h)
                    act.wait_ge(hg["fill"], q + 1)
                    act.activation(hgF[:, h, 0:SEQ], hg_bank(q), ACT.Copy).then_inc(hg["void_act"], 1)

                decays(0)
                for h in range(HH):
                    if h:
                        outputs(h - 1)
                    for what, dst in (("V", vTok), ("K", kTok)):
                        q = G.at(what, h)
                        act.wait_ge(hg["fill"], q + 1)
                        act.activation(dst[:].rearrange("p a b -> p (a b)"), hg_bank(q), ACT.Copy)\
                            .then_inc(hg["void_act"], 1)
                    if h + 1 < HH:
                        decays(h + 1)
                outputs(HH - 1)
                for b in range(NS):
                    act.wait_ge(hg_s_in[b], 16)
                    for h in range(HH):
                        ins = act.activation(sS[:, b, h], sS[:, b, h], ACT.Copy, scale=fS[:, h, b:b + 1])
                    ins.then_inc(hg["s_decay"], 1)
                act.wait_ge(hg["void_dve"], G.before(G.after("S"), "dve"))
                act.wait_ge(hg["s_state"], 2 * NS)
                act.wait_ge(hg["s_out"], 16 * NS)
                for h in range(HH + 1):
                    if h < HH:
                        if h >= 2:
                            act.wait_ge(hg["fill"], G.at("N", (h - 2, 1)) + 1)
                        act.activation((t1, t2)[h % 2][:], hgF[:, h, :], ACT.Square).then_inc(hg["squares"], 1)
                    if h:
                        g = h - 1
                        if g >= 2:
                            act.wait_ge(h_lo_done, x + g - 1)
                        for e in range(2):
                            q = G.at("N", (g, e))
                            act.wait_ge(hg["fill"], q + 1)
                            act.activation((t3, t4)[g % 2][:, e * HT:(e + 1) * HT], hg_bank(q)[:, 0:HT], ACT.Sqrt,
                                           bias=eps[:, 0:1], scale=1.0 / P).then_inc(hg["void_act"], 1)
                        act.wait_ge(hg["normed"], g + 1)
                        act.activation(h_hi[:, g, :], hgF[:, g, :], ACT.Copy).then_inc(h_hi_done, 1)

            def stream(n):
                name, layer, pairs, kt = ST[n]
                r, after, g0 = norm_of.get((name, layer)), gain_after.get((name, layer)), gate_base(n)
                if (name, layer) == ("ffn1_in0", 0):
                    act.wait_ge(kv_out, 16 * 2 * DEPTH)
                    act.wait_ge(kv_tr, 8 * DEPTH)
                if name == "k":
                    if layer:
                        act.wait_ge(chunk_done, 2 * first_pair["k", layer])
                    for m in range(KD):
                        g = V_MEM + KD * layer + m
                        act.activation(m_hi[:, m, :], mT[:, m, :], ACT.Copy, scale=vec[:, g:g + 1])\
                            .then_inc(m_hi_done, 1)

                def body(p, i, first, last):
                    for j in range(2):
                        split(p + j, 1 - j, tiles_of(n, p, j, last))
                        if j == 0 and first and r is not None:
                            root(r)
                        if is_in(name) and j == 0:
                            act.wait_ge(used[0], p + 1)
                            act.activation(t2[:], t1[:], ACT.Silu).then_inc(gate_out, 1)
                        elif is_in(name):
                            act.wait_ge(used[1], p + 1)
                            act.activation(tile(h_hi, i), t3[:], ACT.Copy).then_inc(h_hi_done, 1)
                        if name == "glu" and j == 0:
                            act.wait_ge(chunk_done, 2 * p + 1)
                            if not first:
                                act.wait_ge(used[1], p)
                            act.activation(two(t2[:]), lslot(0), ACT.Sigmoid).then_inc(used[0], 1)
                        if name == "hg_qf" and j == 0:
                            act.wait_ge(used[0], p + 1)
                            act.activation(t2[:], tile(hgQ, i), ACT.Sigmoid).then_inc(gate_out, 1)
                        elif name == "hg_qf":
                            act.wait_ge(used[1], p + 1)
                            act.activation(tile(hgF, i), t3[:], ACT.Sigmoid)
                            act.activation(tile(hgK, i), t3[:], ACT.Sigmoid, scale=-1.0).then_inc(f_out, 1)
                        if name == "hg_vg" and j == 1:
                            act.wait_ge(used[1], p + 1)
                            act.activation(t2[:], tile(hgG, i), ACT.Sigmoid).then_inc(gate_out, 1)
                        if after is not None and is_out(name):
                            act.wait_ge(used[j], p + 1)
                            gain_hi(2 * i + j, NORM_ROW[after])
                        elif after is not None and j == 1:
                            act.wait_ge(used[1], p + 1)
                            gain_hi(i, NORM_ROW[after])
                over_pairs(act, n, body)

            for n in range(len(ST)):
                if ST[n][0] == "glu":
                    s5()
                if ST[n][0] == "hg_out":
                    hgrn()
                if ST[n][0] == "xo":
                    attend(ST[n][1])
                stream(n)
            root(NORMS - 1)

        @block.vector
        def _(dve):
            step = Chain(dve, dve_step)

            def split(p, j, kt):
                if kt is None:
                    return
                dve.wait_ge(hi_ready, 2 * p + j + 1)
                dve.tensor_tensor(w_lo[:, j, 0:kt, :], raw[:, j, 0:kt, :], w_hi[:, j, 0:kt, :].bitcast(F32),
                                  ALU.subtract).then_inc(lo_ready, 1)

            def gain_lo(m, r):
                dve.wait_ge(a_hi_done, KD * split_norms.index(r) + m + 1)
                dve.scalar_tensor_tensor(out=tile(a_lo, m), in0=tile(xT, m),
                                         scalar=vec[:, bass.ds(NORM_ROW[r] + m, 1)],
                                         in1=tile(a_hi, m).bitcast(F32), op0=ALU.mult,
                                         op1=ALU.subtract).then_inc(a_lo_done, 1)

            def reciprocal(r):
                dve.wait_ge(root_done, r + 1)
                step.link(dve.reciprocal(rstd[:], t1[:]))

            for k in range(KD):
                dve.wait_ge(in_tr, k + 1)
                dve.tensor_copy(xT[:, k, 0:SEQ], mis[:, k % 4, :]).then_inc(in_evac, 1)
            dve.wait_ge(in_tr, KD + 1)
            dve.tensor_copy(xT[:, :, SEQ:NT], mis[:, 0, 0:KD * NS].rearrange("p (k b) -> p k b", k=KD))\
                .then_inc(in_evac, 1)
            for q in range(4):
                dve.wait_ge(in_tr, KD + 2 + q)
                dve.tensor_copy(mT[:, 2 * q:2 * q + 2, :], mis[:, (q + 1) % 4, :].rearrange("p (k t) -> p k t", k=2))\
                    .then_inc(in_evac, 1)
            dve.wait_ge(vec_tr, 1)
            dve.tensor_copy(vec[:], mis[:, 1, 0:NVEC]).then_inc(vec_done, 1)
            dve.wait_ge(vec_done, 1)
            for m in range(KD):
                gain_lo(m, 0)
            dve.wait_ge(mem_root, 1)
            dve.reciprocal(m_rstd[:], m_sq[:]).then_inc(mem_rstd, 1)
            dve.wait_ge(mem_rstd, 1)
            split(0, 0, ST[0][3])

            def attend(layer):
                G, X, link = XAG[layer], xa[layer], step.link
                for q, (what, a, owner) in enumerate(G.groups):
                    bank = mis[:, q % 4, :]
                    if what == "S":
                        h, e = a
                        u = 2 * h + e
                        dve.wait_ge(X["fill"], q + 1)
                        link(dve.tensor_reduce(mx[:, u, :], bank.rearrange("p (t m) -> p t m", t=2), AX.X, ALU.max))
                        dve.tensor_scalar(nmx[:, u, :], mx[:, u, :], -XA_SCALE, None, ALU.mult).then_inc(X["max"], 1)
                        for v in range(2 * u, 2 * u + 2):
                            b, t = v // 2, v % 2
                            dve.wait_ge(X["qb"][b % 2], 16 * (b // 2 + 1))
                            dve.wait_ge(X["kc"][v % 2], 16 * (v // 2 + 1))
                            for g in range(MH):
                                c = slice(g * (D // MH), (g + 1) * (D // MH))
                                ins = dve.tensor_tensor_reduce(kc[:, v % 2, c], kc[:, v % 2, c], qb[:, b % 2, c], 1.0, 0.0, ALU.mult,
                                                               ALU.add, sT[:, t, MH * b + g:MH * b + g + 1])
                            ins.then_inc(X["score"], 1)
                        dve.wait_ge(X["void"]["act"], G.before(q + 1, "act"))
                        link(dve.reciprocal(rden[:, u, :], den[:, u, :]))
                        for t in range(2):
                            ins = dve.tensor_scalar(pP[:, u % 4, t, :], pP[:, u % 4, t, :], rden[:, u, t:t + 1], None,
                                                    ALU.mult)
                        ins.then_inc(X["prob"], 1)
                    if what == "T":
                        dve.wait_ge(X["fill"], q + 1)
                        link(dve.tensor_reduce(ssm[:, 0:1], bank[0:NS * MH, 0:NM], AX.X, ALU.max))
                        dve.tensor_scalar(ssm[:, 1:2], ssm[:, 0:1], -XA_SCALE, None, ALU.mult).then_inc(X["s_max"], 1)
                        dve.wait_ge(X["void"]["act"], G.before(q + 1, "act"))
                        link(dve.reciprocal(ssm[:, 3:4], ssm[:, 2:3]))
                        dve.tensor_scalar(pS[:], pS[:], ssm[:, 3:4], None, ALU.mult).then_inc(X["s_prob"], 1)
                    if owner != "dve":
                        continue
                    dve.wait_ge(X["fill"], q + 1)
                    if what == "Q":
                        dve.tensor_copy(qs[:, 512 * a:512 * a + 512], bank[0:NS, :]).then_inc(X["void"]["dve"], 1)
                    elif what == "P":
                        h, e = a
                        if h >= 2:
                            dve.wait_ge(X["fill"], G.at("O", (h - 2, 1)) + 1)
                        dve.tensor_copy(pT[:, h % 2, :, 256 * e:256 * e + 256],
                                        bank.rearrange("p (m t) -> p m t", m=2)).then_inc(X["void"]["dve"], 1)
                    elif what == "O":
                        h, e = a
                        dve.wait_ge(X["o_hi"], 2 * h + e + 1)
                        dve.tensor_tensor(h_lo[:, 2 * h + e, 0:SEQ], bank, h_hi[:, 2 * h + e, 0:SEQ].bitcast(F32),
                                          ALU.subtract).then_inc(X["void"]["dve"], 1)
                    elif what == "W":
                        dve.tensor_copy(pW[:], bank[:, 0:2 * NS * MH].rearrange("p (t c) -> p t c", t=2))\
                            .then_inc(X["void"]["dve"], 1)
                    elif what == "V":
                        dve.wait_ge(h_hi_done, hidden_before(number("xo", layer)) + KD)
                        dve.tensor_tensor(h_lo[:, 0:KD, SEQ:NT], bank[:, 0:KD * NS].rearrange("p (k b) -> p k b", k=KD),
                                          h_hi[:, 0:KD, SEQ:NT].bitcast(F32), ALU.subtract).then_inc(h_lo_done, KD)

            def expm1(x, k, r, q, s2, out_e, out_x):
                link = step.link
                link(dve.tensor_scalar(x, x, -87.0, 88.0, ALU.max, ALU.min))
                link(dve.tensor_scalar(k, x, 1.0 / math.log(2.0), 12582912.0, ALU.mult, ALU.add))
                link(dve.tensor_scalar(k, k, 12582912.0, None, ALU.subtract))
                link(dve.scalar_tensor_tensor(out=r, in0=k, scalar=-0.693359375, in1=x, op0=ALU.mult, op1=ALU.add))
                link(dve.scalar_tensor_tensor(out=r, in0=k, scalar=2.12194440e-4, in1=r, op0=ALU.mult, op1=ALU.add))
                link(dve.tensor_scalar(q, r, 1.0 / 40320, None, ALU.mult))
                for f in (5040, 720, 120, 24, 6, 2, 1):
                    link(dve.scalar_tensor_tensor(out=q, in0=q, scalar=1.0 / f, in1=r, op0=ALU.add, op1=ALU.mult))
                link(dve.tensor_scalar(smi[:], k, 127.0, 8388608.0, ALU.add, ALU.mult))
                two_k = smi[:].bitcast(F32)
                link(dve.tensor_tensor(q, q, two_k, ALU.mult))
                if out_x is not None:
                    link(dve.tensor_tensor(out_x, q, two_k, ALU.add))
                if out_e is not None:
                    link(dve.scalar_tensor_tensor(out=out_e, in0=two_k, scalar=-1.0, in1=q, op0=ALU.add, op1=ALU.add))

            def s5():
                G, link = S5G, step.link
                dve.wait_ge(s5_rows, 48)
                dve.tensor_copy(prow[64:96, :].rearrange("j (g p) -> j g p", g=2),
                                ldrow[64:96, :].unsqueeze(2).to_broadcast([32, 2, 64])).then_inc(s5_small, 1)
                dve.wait_ge(s5_fill, 1)
                dve.tensor_copy(par[:], mis[:, 0, 0:96]).then_inc(s5_void["dve"], 1)
                dve.wait_ge(s5_void["dve"], 1)
                for e in range(2):
                    dve.wait_ge(s5_fill, 2 + e)
                    dve.tensor_copy(cT[:, e].rearrange("p j c -> p (j c)"), mis[:, 1 + e, :])\
                        .then_inc(s5_void["dve"], 1)
                dve.wait_ge(s5_void["dve"], 3)
                ar, ai, ld = par[:, 0:32], par[:, 32:64], par[:, 64:96]
                v = [sm[:, q, :] for q in range(12)]
                expm1(ld, v[0], v[1], v[2], None, None, v[11])
                link(dve.tensor_tensor(v[0], ar, v[11], ALU.mult))
                link(dve.tensor_tensor(v[1], ai, v[11], ALU.mult))
                link(dve.tensor_scalar(v[2], v[1], 1.0 / (2 * math.pi), 12582912.0, ALU.mult, ALU.add))
                link(dve.tensor_scalar(v[2], v[2], 12582912.0, None, ALU.subtract))
                c1 = 6.28125
                c2 = float(np.float32(round((2 * math.pi - c1) * 2 ** 20) / 2 ** 20))
                c3 = 2 * math.pi - c1 - c2
                for c in (c1, c2, c3):
                    link(dve.scalar_tensor_tensor(out=v[1], in0=v[2], scalar=-c, in1=v[1], op0=ALU.mult, op1=ALU.add))
                dve.tensor_scalar(v[3], v[1], -3.1415925, 3.1415925, ALU.max, ALU.min).then_inc(s5_phase, 1)
                expm1(v[0], v[2], v[6], v[7], None, v[8], v[9])
                dve.wait_ge(s5_sin, 2)
                link(dve.tensor_tensor(v[10], v[5], v[5], ALU.mult))
                link(dve.tensor_scalar(v[10], v[10], -2.0, None, ALU.mult))
                dve.memset(pw[:, 0, 0, :], 1.0)
                dve.memset(pw[:, 1, 0, :], 0.0)
                link(dve.tensor_scalar(v[2], v[10], 1.0, None, ALU.add))
                link(dve.tensor_tensor(pw[:, 0, 1, :], v[9], v[2], ALU.mult))
                link(dve.tensor_tensor(pw[:, 1, 1, :], v[9], v[4], ALU.mult))
                link(dve.tensor_tensor(v[8], v[8], v[2], ALU.mult))
                link(dve.tensor_tensor(v[8], v[8], v[10], ALU.add))
                link(dve.tensor_tensor(v[0], ar, ar, ALU.mult))
                link(dve.tensor_tensor(v[1], ai, ai, ALU.mult))
                link(dve.tensor_tensor(v[0], v[0], v[1], ALU.add))
                link(dve.reciprocal(v[0], v[0]))
                for out, a, b, op in ((v[6], v[8], pw[:, 1, 1, :], ALU.add), (v[7], pw[:, 1, 1, :], v[8], ALU.subtract)):
                    link(dve.tensor_tensor(v[1], a, ar, ALU.mult))
                    link(dve.tensor_tensor(v[2], b, ai, ALU.mult))
                    link(dve.tensor_tensor(v[1], v[1], v[2], op))
                    link(dve.tensor_tensor(out, v[1], v[0], ALU.mult))

                def times(out_r, out_i, ar_, ai_, br_, bi_, tmp, neg=False):
                    link(dve.tensor_tensor(out_r, ar_, br_, ALU.mult))
                    link(dve.tensor_tensor(tmp, ai_, bi_, ALU.mult))
                    link(dve.tensor_tensor(out_r, out_r, tmp, ALU.subtract))
                    link(dve.tensor_tensor(out_i, ar_, bi_, ALU.mult))
                    link(dve.tensor_tensor(tmp, ai_, br_, ALU.mult))
                    if neg:
                        link(dve.scalar_tensor_tensor(out=out_i, in0=out_i, scalar=-1.0, in1=tmp, op0=ALU.mult,
                                                      op1=ALU.subtract))
                    else:
                        link(dve.tensor_tensor(out_i, out_i, tmp, ALU.add))

                for n in (1, 2, 4):
                    def by(e, d):
                        return pw[:, e, d, :].unsqueeze(1).to_broadcast([P, n, NJ])
                    times(pw[:, 0, n + 1:2 * n + 1, :], pw[:, 1, n + 1:2 * n + 1, :], pw[:, 0, 1:n + 1, :],
                          pw[:, 1, 1:n + 1, :], by(0, n), by(1, n), sTmp[:, 0:n * NJ].rearrange("p (n j) -> p n j", n=n))
                for e in range(2):
                    link(dve.tensor_copy(cw[:, e, 1, :], pw[:, e, CS, :]))
                for n in (1, 2, 4):
                    def by(e, d):
                        return cw[:, e, d, :].unsqueeze(1).to_broadcast([P, n, NJ])
                    times(cw[:, 0, n + 1:2 * n + 1, :], cw[:, 1, n + 1:2 * n + 1, :], cw[:, 0, 1:n + 1, :],
                          cw[:, 1, 1:n + 1, :], by(0, n), by(1, n), sTmp[:, 0:n * NJ].rearrange("p (n j) -> p n j", n=n))
                dve.wait_ge(s5_bc, 16 * (4 + 2 * 4 * 2 * 8))
                col = [v[q].unsqueeze(2).to_broadcast([P, NJ, SC]) for q in (6, 7)]
                times(bBar[:, 0], bBar[:, 1], bRaw[:, 0], bRaw[:, 1], col[0], col[1],
                      sTmp[:, 0:NJ * SC].rearrange("p (j c) -> p j c", j=NJ))

                def table(out, n, m, neg):
                    tmp = sTmp[:, 0:SC * n * NJ].rearrange("p (j d c) -> p j d c", j=NJ, d=n)
                    pv = [pw[:, e, 0:n, :].rearrange("p d j -> p j d").unsqueeze(3).to_broadcast([P, NJ, n, SC])
                          for e in range(2)]
                    mv = [m[:, e].unsqueeze(2).to_broadcast([P, NJ, n, SC]) for e in range(2)]
                    times(out[:, 0], out[:, 1], pv[0], pv[1], mv[0], mv[1], tmp, neg)

                table(sF, CS, bBar, False)
                dve.nop().then_inc(s5_tables_f, 1)
                table(sG, CS + 1, cT, True)
                dve.nop().then_inc(s5_tables_made, 1)

                for q, (what, a, owner) in enumerate(G.groups):
                    if q == S5_MADE:
                        reciprocal(s5_norm)
                        G.all_emptied(dve, q)
                        dve.wait_ge(s5_tab_out, 16 * 3)
                        for k in range(KD):
                            dve.scalar_tensor_tensor(out=u32[:, k, :], in0=xT[:, k, :],
                                                     scalar=vec[:, NORM_ROW[s5_norm] + k:NORM_ROW[s5_norm] + k + 1],
                                                     in1=rstd[:], op0=ALU.mult, op1=ALU.mult).then_inc(s5_u, 1)
                        for e in range(2):
                            link(dve.memset(sZ[:, e, :, NC:UC], 0.0))
                    if what == "X" and a[1] == 0:
                        f = a[0]
                        dve.wait_ge(s5_u, f + 1 + (f == 0) * (KD - 1))
                        if f >= 2:
                            dve.wait_ge(s5_fill, q - 2)
                        link(dve.tensor_copy(sZ[:, f % 2, :, 0:NC],
                                             u32[:, f, 0:SEQ].rearrange("p (n s) -> p s n", s=CS)))
                        dve.tensor_copy(sZ[:, f % 2, 0, NC:YC], u32[:, f, SEQ:NT])
                        dve.tensor_copy(sZ[:, f % 2, CS - 1, YC:UC], u32[:, f, SEQ:NT]).then_inc(s5_z, 1)
                    if owner != "dve" or q < 3:
                        continue
                    if what == "hfin":
                        scan()
                    dve.wait_ge(s5_fill, q + 1)
                    bank = mis[:, q % 4, :]
                    if what == "y":
                        f, e = a
                        d = vec[:, V_D + f:V_D + f + 1]
                        if e == 0:
                            dve.scalar_tensor_tensor(out=u32[:, f, SEQ:NT], in0=u32[:, f, SEQ:NT], scalar=d,
                                                     in1=bank[:, NC:YC], op0=ALU.mult, op1=ALU.add)
                        seg = u32[:, f, 0:SEQ].rearrange("p (n s) -> p n s", s=CS)[:, :, 4 * e:4 * e + 4]
                        dve.scalar_tensor_tensor(
                            out=seg, in0=seg, scalar=d,
                            in1=bank[:, 0:4 * YC].rearrange("p (t n) -> p n t", t=4)[:, 0:NC, :],
                            op0=ALU.mult, op1=ALU.add).then_inc(s5_void["dve"], 1)
                        continue
                    if what == "K":
                        if a == 0:
                            for e in range(2):
                                dve.wait_ge(s5_f_out[e], 16 * NJ // 4)
                        dst, src = sK[:, 8 * (a // 2) + a % 2:8 * (a // 2) + 8:2, :], bank[0:SC, :].rearrange("p (g n) -> p g n", g=4)
                    elif what == "h0":
                        dst, src = hs0[:], bank.rearrange("p (e b j) -> p e b j", e=2, b=NS)
                    elif what == "U":
                        dst, src = sU[:, 4 * a:4 * a + 4, :], bank[:, 0:4 * UC].rearrange("p (g n) -> p g n", g=4)
                    elif what == "FU":
                        dst = sFH[:, 2 * a:2 * a + 2, :, 1:]
                        src = bank[:, 0:4 * UC].rearrange("p (j e n) -> p j e n", j=2, e=2)
                    elif what == "hfin":
                        dst, src = frow[:], bank[0:64, 0:P]
                    elif what == "hs1":
                        dst, src = hrow[:].rearrange("p e f n -> p (e f n)"), bank
                    elif what == "Y":
                        if a == 9:
                            dve.wait_ge(s5_fill, G.first("y") + 8)
                        dst = sY[:, :, 64 * (a % 8):64 * (a % 8) + 64].rearrange("n t (g c) -> n t g c", g=4)
                        src = bank[0:YC, :].rearrange("n (g t c) -> n t g c", g=4, t=CS)
                    dve.tensor_copy(dst, src).then_inc(s5_void["dve"], 1)
                    if what == "hfin" or what == "hs1":
                        dve.wait_ge(s5_void["dve"], G.before(q + 1, "dve"))
                        dve.nop().then_inc(s5_fin, 1)
                h0 = hidden_before(number("glu"))
                dve.wait_ge(s5_state_out, 16 * 6)
                dve.nop().then_inc(s5_state_done, 1)
                for k in range(KD):
                    dve.wait_ge(h_hi_done, h0 + k + 1)
                    dve.tensor_tensor(h_lo[:, k, :], (t3, t4)[k % 2][:], h_hi[:, k, :].bitcast(F32), ALU.subtract)\
                        .then_inc(h_lo_done, 1)

            def scan():
                G, link = S5G, step.link
                G.all_emptied(dve, G.after("FU"))
                link(dve.memset(sFH[:, :, :, 0], 0.0))
                H = sFH[:, :, :, 1:NC + 1].rearrange("p j e (b m) -> p j e b m", m=CB)
                blocks = NC // CB

                def add_product(out, x, fac, shape):
                    n = int(np.prod(shape))
                    tmp = [t[:, 0:n] if len(shape) == 1 else t[:, 0:n].rearrange(
                        "p (j b) -> p j b" if len(shape) == 2 else "p (j b m) -> p j b m", j=NJ,
                        **({"b": shape[1]} if len(shape) == 3 else {})) for t in sc]
                    for f, (a, b) in enumerate((((0, 0), (1, 1)), ((0, 1), (1, 0)))):
                        dve.tensor_tensor(tmp[0], fac[a[0]], x[a[1]], ALU.mult)
                        link(dve.tensor_tensor(tmp[1], fac[b[0]], x[b[1]], ALU.mult))
                        link(dve.tensor_tensor(out[f], out[f], tmp[0], ALU.add))
                        link(dve.tensor_tensor(out[f], out[f], tmp[1], ALU.add if f else ALU.subtract))

                for m in range(1, CB):
                    add_product([H[:, :, e, :, m] for e in range(2)], [H[:, :, e, :, m - 1] for e in range(2)],
                                [cw[:, e, 1, :].unsqueeze(2).to_broadcast([P, NJ, blocks]) for e in range(2)],
                                (NJ, blocks))
                for b in range(1, blocks):
                    add_product([H[:, :, e, b, CB - 1] for e in range(2)], [H[:, :, e, b - 1, CB - 1] for e in range(2)],
                                [cw[:, e, CB, :] for e in range(2)], (NJ,))
                shape = [P, NJ, blocks - 1, CB - 1]
                add_product([H[:, :, e, 1:, 0:CB - 1] for e in range(2)],
                            [H[:, :, e, 0:blocks - 1, CB - 1:CB].to_broadcast(shape) for e in range(2)],
                            [cw[:, e, 1:CB, :].rearrange("p m j -> p j m").unsqueeze(2).to_broadcast(shape)
                             for e in range(2)], tuple(shape[1:]))
                link(dve.tensor_copy(hfin[:], sFH[:, :, :, NC].rearrange("p j e -> p e j")))

                def lam(e):
                    return pw[:, e, 1, :].unsqueeze(1).to_broadcast([P, NS, NJ])
                for e in range(2):
                    link(dve.tensor_tensor(hs1[:, e], hs0[:, e], lam(0), ALU.mult))
                    link(dve.tensor_tensor(hst[:, e], hs0[:, 1 - e], lam(1), ALU.mult))
                    link(dve.tensor_tensor(hs1[:, e], hs1[:, e], hst[:, e], ALU.add if e else ALU.subtract))
                    link(dve.tensor_tensor(hs1[:, e], hs1[:, e],
                                           sFH[:, :, e, 1 + YC:1 + UC].rearrange("p j b -> p b j"), ALU.add))
                    link(dve.tensor_copy(sFH[:, :, e, NC:YC], hs0[:, e].rearrange("p b j -> p j b")))
                dve.nop().then_inc(s5_scanned, 1)

            def hgrn():
                G, link, x = HG, step.link, hidden_before(number("hg_out", 1))
                l0, l1 = vec[:, V_LB:V_LB + HH], vec[:, V_LB + HH:V_LB + 2 * HH]
                link(dve.tensor_tensor(lbv[:, 4], l0, l1, ALU.max))
                link(dve.tensor_tensor(lbv[:, 0], l0, lbv[:, 4], ALU.subtract))
                dve.tensor_tensor(lbv[:, 1], l1, lbv[:, 4], ALU.subtract).then_inc(hg["lb_diff"], 1)
                dve.wait_ge(hg["lb_exp"], 1)
                link(dve.tensor_tensor(lbv[:, 4], lbv[:, 2], lbv[:, 3], ALU.add))
                link(dve.reciprocal(lbv[:, 4], lbv[:, 4]))
                link(dve.tensor_tensor(lbv[:, 5], lbv[:, 2], lbv[:, 4], ALU.mult))
                link(dve.tensor_tensor(lbv[:, 4], lbv[:, 3], lbv[:, 4], ALU.mult))
                dve.nop().then_inc(hg["lb"], 1)
                link(dve.tensor_tensor(fS[:], hgF[:, :, SEQ:NT], lbv[:, 5].unsqueeze(2).to_broadcast([P, HH, NS]), ALU.mult))
                link(dve.tensor_tensor(fS[:], fS[:], lbv[:, 4].unsqueeze(2).to_broadcast([P, HH, NS]), ALU.add))
                dve.wait_ge(hg["consts"], 1)

                def decays(h):
                    e = h % 2
                    b = bC[e][:]
                    dve.wait_ge(hg["log"], h + 1)
                    link(dve.tensor_scalar(b, b, -20.0, None, ALU.max))
                    if h >= 2:
                        dve.wait_ge(hg["fill"], G.at("O", h - 2) + 1)
                    link(dve.tensor_tensor_scan(b, chunk_start[:], b, 0.0, ALU.mult, ALU.add))
                    dve.nop().then_inc(hg["decay"], 1)
                    for u, level in enumerate(LEVELS):
                        c, w = (t.rearrange("p (b a t) -> p b a t", a=2, t=level) for t in (b, lvl[e][u][:]))
                        edge = c[:, :, 0, level - 1:level].to_broadcast([P, SEQ // (2 * level), level])
                        dve.tensor_tensor(w[:, :, 1], c[:, :, 1], edge, ALU.subtract)
                        dve.tensor_tensor(w[:, :, 0], edge, c[:, :, 0], ALU.subtract).then_inc(hg["decay"], 1)
                    c, w = (t.rearrange("p (b t) -> p b t", t=8) for t in (b, dgQ[e][:]))
                    dve.tensor_tensor(w, c, c[:, :, 3:4].to_broadcast([P, SEQ // 8, 8]), ALU.subtract)\
                        .then_inc(hg["decay"], 1)
                    c, w = (t.rearrange("p (b t) -> p b t", t=HC) for t in (b, outK[e][:]))
                    dve.tensor_tensor(w, c[:, :, HC - 1:HC].to_broadcast([P, NHC, HC]), c, ALU.subtract)\
                        .then_inc(hg["decay"], 1)

                def scaled(h):
                    e = h % 2
                    dve.wait_ge(hg["exps"], EXPS * (h + 1))
                    dve.tensor_tensor(dgQ[e][:], dgQ[e][:], hgQ[:, h, 0:SEQ], ALU.mult)
                    dve.tensor_tensor(dgK[e][:], dgK[e][:], hgK[:, h, 0:SEQ], ALU.mult).then_inc(hg["scaled_dve"], 1)
                    dve.tensor_tensor(outK[e][:], outK[e][:], hgK[:, h, 0:SEQ], ALU.mult).then_inc(hg["scaled_dve"], 1)

                decays(0)
                scaled(0)
                for h in range(HH):
                    e = h % 2
                    if h >= 2:
                        dve.wait_ge(hg["fill"], G.at("O", h - 2) + 1)
                    for u in range(len(LEVELS) + 1):
                        q = G.at("A", (h, u))
                        dve.wait_ge(hg["fill"], q + 1)
                        if u:
                            dve.wait_ge(hg["void_dve"], G.before(q, "dve"))
                        dve.copy_predicated(attn[e][:], pair_mask[:, u:u + 1, :].bitcast(I32).to_broadcast([P, 4, P]),
                                            hg_bank(q).rearrange("p (a t) -> p a t", a=4)).then_inc(hg["void_dve"], 1)
                    if h + 1 < HH:
                        decays(h + 1)
                    dve.wait_ge(hg["fill"], G.at("D", (h, 1)) + 1)
                    dve.wait_ge(hg["void_act"], G.before(G.at("V", h), "act"))
                    for n in range(NHC):
                        add = hg_bank(G.at("D", (h, n % 2)))[:, (n // 2) * P:(n // 2 + 1) * P]
                        if n == 0:
                            link(dve.tensor_copy(hS[:, 0], add))
                            continue
                        if n == NHC - 1 and h:
                            dve.wait_ge(hg["state_out"], 16 * h)
                        link(dve.scalar_tensor_tensor(out=hS[:, n], in0=hS[:, n - 1], scalar=ebt[e][:, n:n + 1], in1=add,
                                                      op0=ALU.mult, op1=ALU.add))
                    dve.nop().then_inc(hg["state"], 1)
                    dve.nop().then_inc(hg["void_dve"], 2)
                    if h + 1 < HH:
                        scaled(h + 1)
                for b in range(NS):
                    dve.wait_ge(hg["s_decay"], b + 1)
                    for f in range(2):
                        q = G.at("B", (b, f))
                        dve.wait_ge(hg["fill"], q + 1)
                        for u in range(4):
                            h = 4 * f + u
                            ins = dve.scalar_tensor_tensor(out=sS[:, b, h], in0=hg_bank(q)[:, u * P:(u + 1) * P],
                                                           scalar=hgK[:, h, SEQ + b:SEQ + b + 1], in1=sS[:, b, h],
                                                           op0=ALU.mult, op1=ALU.add)
                        link(ins)
                        dve.nop().then_inc(hg["void_dve"], 1)
                        dve.nop().then_inc(hg["s_state"], 1)
                q = G.at("S", 0)
                dve.wait_ge(hg["fill"], q + 1)
                dve.tensor_copy(hgF[:, :, SEQ:NT], hg_bank(q)[:, 0:HH * NS].rearrange("p (h b) -> p h b", h=HH))\
                    .then_inc(hg["void_dve"], 1)
                for h in range(HH):
                    t = (t3, t4)[h % 2]
                    dve.wait_ge(hg["void_act"], G.before(G.at("N", (h, 1)) + 1, "act"))
                    link(dve.reciprocal(t[:], t[:]))
                    link(dve.scalar_tensor_tensor(out=t[:], in0=t[:], scalar=vec[:, V_HG:V_HG + 1], in1=hgG[:, h, :],
                                                  op0=ALU.mult, op1=ALU.mult))
                    dve.tensor_tensor(hgF[:, h, :], hgF[:, h, :], t[:], ALU.mult).then_inc(hg["normed"], 1)
                    dve.wait_ge(h_hi_done, x + h + 1)
                    dve.tensor_tensor(h_lo[:, h, :], hgF[:, h, :], h_hi[:, h, :].bitcast(F32), ALU.subtract)\
                        .then_inc(h_lo_done, 1)

            def evac_kv(layer, which):
                dst = kOut if which == 0 else vM[layer]
                if which == 0 and layer:
                    dve.wait_ge(kv_out, 16 * 2 * layer)
                for t in range(2):
                    for half in range(2):
                        q = 8 * layer + 4 * which + 2 * t + half
                        dve.wait_ge(kv_tr, q + 1)
                        dve.tensor_copy(dst[:, t, half * 512:(half + 1) * 512], mis[:, 2 + q % 2, :])\
                            .then_inc(kv_evac, 1)

            def stream(n):
                name, layer, pairs, kt = ST[n]
                r, after, g0 = norm_of.get((name, layer)), gain_after.get((name, layer)), gate_base(n)
                h0 = hidden_before(n)
                if name == "k":
                    for m in range(KD):
                        g = V_MEM + KD * layer + m
                        dve.wait_ge(m_hi_done, KD * layer + m + 1)
                        dve.scalar_tensor_tensor(out=m_lo[:, m, :], in0=mT[:, m, :], scalar=vec[:, g:g + 1],
                                                 in1=m_hi[:, m, :].bitcast(F32), op0=ALU.mult,
                                                 op1=ALU.subtract).then_inc(m_lo_done, 1)

                def hidden_lo(i):
                    dve.wait_ge(h_hi_done, h0 + i + 1)
                    dve.tensor_tensor(tile(h_lo, i), t3[:], tile(h_hi, i).bitcast(F32), ALU.subtract)\
                        .then_inc(h_lo_done, 1)

                def gate(i):
                    dve.wait_ge(gate_out, g0 + i + 1)
                    dve.tensor_tensor(tile(hgG, i), tile(hgG, i), t2[:], ALU.mult).then_inc(gated, 1)

                def body(p, i, first, last):
                    inner = not first and not last
                    if inner:
                        step.loop(i, 1, 1 if is_in(name) or name == "glu" else 0)
                    for j in range(2):
                        split(p + j, 1 - j, tiles_of(n, p, j, last))
                        if j == 0 and first and r is not None:
                            reciprocal(r)
                        if name == "glu" and j == 0:
                            continue
                        dve.wait_ge(chunk_done, 2 * p + j + 1)
                        m = 2 * i + j
                        if name in ("k", "v"):
                            dst = kT[layer] if name == "k" else vT
                            dve.tensor_tensor(tile(dst, m), lslot(j, NM), m_rstd[:], ALU.mult).then_inc(used[j], 1)
                        elif is_in(name) and j == 0:
                            wait(dve, gate_out, g0 + i)
                            dve.tensor_tensor(two(t1[:]), lslot(0), two(rstd[:]), ALU.mult).then_inc(used[0], 1)
                            if not first:
                                hidden_lo(i - 1)
                        elif is_in(name):
                            step.link(dve.tensor_tensor(two(t4[:]), lslot(1), two(rstd[:]), ALU.mult))
                            dve.wait_ge(gate_out, g0 + i + 1)
                            dve.tensor_tensor(t3[:], t4[:], t2[:], ALU.mult).then_inc(used[1], 1)
                            if last:
                                hidden_lo(i)
                        elif name == "glu":
                            dve.wait_ge(used[0], p + 1)
                            step.link(dve.tensor_tensor(two(t3[:]), lslot(1), two(t2[:]), ALU.mult))
                            dve.tensor_tensor(tile(xT, i), tile(xT, i), t3[:], ALU.add).then_inc(used[1], 1)
                            if not first and after is not None:
                                gain_lo(i - 1, after)
                            if last and after is not None:
                                gain_lo(i, after)
                        elif name == "xq":
                            dve.tensor_tensor(twotile(qT, m), lslot(j), two(rstd[:]), ALU.mult).then_inc(used[j], 1)
                        elif name == "hg_qf" and j == 0:
                            dve.tensor_tensor(twotile(hgQ, i), lslot(0), two(rstd[:]), ALU.mult).then_inc(used[0], 1)
                        elif name == "hg_qf":
                            wait(dve, f_out, i)
                            dve.tensor_tensor(two(t3[:]), lslot(1), two(rstd[:]), ALU.mult).then_inc(used[1], 1)
                            dve.wait_ge(gate_out, g0 + i + 1)
                            dve.tensor_tensor(tile(hgQ, i), tile(hgQ, i), t2[:], ALU.mult).then_inc(gated, 1)
                        elif name == "hg_vg" and j == 0:
                            if not first:
                                gate(i - 1)
                            dve.tensor_tensor(twotile(hgV, i), lslot(0), two(rstd[:]), ALU.mult).then_inc(used[0], 1)
                        elif name == "hg_vg":
                            dve.tensor_tensor(twotile(hgG, i), lslot(1), two(rstd[:]), ALU.mult).then_inc(used[1], 1)
                            if last:
                                gate(i)
                        else:
                            scale = 0.5 if name[:3] == "ffn" else 1.0
                            dve.scalar_tensor_tensor(out=twotile(xT, m), in0=lslot(j), scalar=scale,
                                                     in1=twotile(xT, m), op0=ALU.mult, op1=ALU.add)\
                                .then_inc(used[j], 1)
                            if after is not None:
                                if not (first and j == 0):
                                    gain_lo(m - 1, after)
                                if last and j == 1:
                                    gain_lo(m, after)
                    if inner:
                        step.done(pairs - 2)
                over_pairs(dve, n, body)
                if name in ("k", "v"):
                    evac_kv(layer, 0 if name == "k" else 1)

            for n in range(len(ST)):
                if ST[n][0] == "glu":
                    s5()
                if ST[n][0] == "hg_out":
                    hgrn()
                if ST[n][0] == "xo":
                    attend(ST[n][1])
                stream(n)
            reciprocal(NORMS - 1)
            for m in range(KD):
                dve.scalar_tensor_tensor(out=yT[:, m, :], in0=xT[:, m, :], scalar=vec[:, V_FIN + m:V_FIN + m + 1],
                                         in1=rstd[:], op0=ALU.mult, op1=ALU.mult).then_inc(y_normed, 1)
            for q in range(10):
                t, half = q // 2, q % 2
                dve.wait_ge(y_tr, q + 1)
                dst = yout[:, t, half * 512:(half + 1) * 512] if t < 4 else ysout[:, half * 512:(half + 1) * 512]
                dve.tensor_copy(dst, mis[0:P if t < 4 else NS, 2 + q % 2, :]).then_inc(y_evac, 1)

        @block.tensor
        def _(pe):
            pe.wait_ge(consts_done, 4)
            pe.wait_ge(loaded, 48)
            for k in range(KD):
                wait(pe, in_evac, k - 3)
                for t in range(4):
                    ins = pe.transpose(mis[:, k % 4, t * P:(t + 1) * P], xin[:, t, k * P:(k + 1) * P], ident[:])
                ins.then_inc(in_tr, 1)
            pe.wait_ge(in_evac, KD - 3)
            for k in range(KD):
                ins = pe.transpose(mis[:, 0, k * NS:(k + 1) * NS], xsin[:, k * P:(k + 1) * P], ident[0:NS, 0:NS])
            ins.then_inc(in_tr, 1)
            for q in range(4):
                pe.wait_ge(in_evac, KD + 1 + q - 3)
                for u in range(4):
                    k, t = 2 * q + u // 2, u % 2
                    ins = pe.transpose(mis[:, (q + 1) % 4, u * P:(u + 1) * P], min_[:, t, k * P:(k + 1) * P], ident[:])
                ins.then_inc(in_tr, 1)
            pe.wait_ge(vrows_loaded, 16 * 9)
            pe.wait_ge(in_evac, KD + 2)
            pe.transpose(mis[:, 1, 0:P], vrows[:], ident[:]).then_inc(vec_tr, 1)
            pe.wait_ge(mem_squares, 1)
            pe.wait_ge(in_evac, KD + 3)
            pe.matmul(mis[:, 2, 0:NM], ones[:], m_acc[:], start=True, stop=True).then_inc(mem_sums, 1)

            def sums(r):
                pe.wait_ge(squares_done, r + 1)
                for half in range(2):
                    ins = pe.matmul(mis[:, half, 0:HT], ones[:], acc[:, half * HT:(half + 1) * HT],
                                    start=True, stop=True)
                ins.then_inc(sums_done, 1)

            def attend(layer):
                G, X = XAG[layer], xa[layer]
                for j in range(2):
                    pe.wait_ge(used[j], first_pair["xo", layer])
                for q, (what, a, owner) in enumerate(G.groups):
                    bank = mis[:, q % 4, :]
                    if q == 0:
                        pe.wait_ge(root_done, norm_of["xq", layer] + 1)
                    G.reuse(pe, q)
                    if what == "Q":
                        for u in range(4):
                            ins = pe.transpose(bank[0:NS, u * P:(u + 1) * P], qT[:, 4 * a + u, SEQ:NT], ident[:])
                    elif what == "S":
                        h, e = a
                        for t in range(2):
                            c = (2 * e + t) * P
                            for k in range(2):
                                ins = pe.matmul(bank[:, t * NM:(t + 1) * NM], qT[:, 2 * h + k, c:c + P],
                                                kT[layer][:, 2 * h + k, :], start=k == 0, stop=k == 1)
                    elif what == "P":
                        h, e = a
                        u = 2 * h + e
                        pe.wait_ge(X["prob"], u + 1)
                        for m in range(2):
                            for t in range(2):
                                ins = pe.transpose(bank[:, (2 * m + t) * P:(2 * m + t + 1) * P],
                                                   pP[:, u % 4, t, m * P:(m + 1) * P], ident[:])
                    elif what == "O":
                        h, e = a
                        if e == 0:
                            G.all_emptied(pe, G.at("P", (h, 1)) + 1)
                        for m in range(2):
                            ins = pe.matmul(bank, vM[layer][:, m, (2 * h + e) * P:(2 * h + e + 1) * P],
                                            pT[:, h % 2, m, :], start=m == 0, stop=m == 1)
                    elif what == "T":
                        pe.wait_ge(X["score"], 2 * NS)
                        for t in range(2):
                            ins = pe.transpose(bank[0:NS * MH, t * P:(t + 1) * P], sT[:, t, :], ident[:])
                    elif what == "W":
                        pe.wait_ge(X["s_prob"], 1)
                        for t in range(2):
                            ins = pe.transpose(bank[:, t * NS * MH:(t + 1) * NS * MH], pS[:, t * P:(t + 1) * P],
                                               ident[0:NS * MH, 0:NS * MH])
                    else:
                        G.all_emptied(pe, q)
                        for b in range(NS):
                            pe.wait_ge(X["vc"][b % 4], 16 * (b // 4 + 1))
                            for k in range(KD):
                                c = MH * b + k // 2
                                for t in range(2):
                                    ins = pe.matmul(bank[:, k * NS + b:k * NS + b + 1], vc[b % 4][:, t, k * P:(k + 1) * P],
                                                    pW[:, t, c:c + 1], start=t == 0, stop=t == 1)
                            if b < NS - 1:
                                ins.then_inc(X["pv"], 1)
                    ins.then_inc(X["fill"], 1)

            def s5():
                G = S5G
                for q, (what, a, owner) in enumerate(G.groups):
                    if what == "h0":
                        G.all_emptied(pe, q)
                        sums(s5_norm)
                        pe.wait_ge(root_done, s5_norm + 1)
                        pe.wait_ge(s5_state_in, 64)
                    G.reuse(pe, q)
                    bank = mis[:, q % 4, :]
                    if what == "par":
                        pe.wait_ge(s5_small, 1)
                        ins = pe.transpose(bank[:, 0:96], prow[:], ident[0:96, 0:96])
                    elif what == "c":
                        pe.wait_ge(s5_bc, 16 * (4 + 2 * 4 * 2 * 8))
                        for b in range(4):
                            ins = pe.transpose(bank[:, b * P:(b + 1) * P], cRaw[:, a, b, :], ident[:])
                    elif what == "F":
                        pe.wait_ge(s5_tables_f, 1)
                        for u in range(4):
                            j, e = 2 * a + u // 2, u % 2
                            ins = pe.transpose(bank[:, u * P:(u + 1) * P],
                                               sF[:, e, j].rearrange("p d c -> p (d c)"), ident[:])
                    elif what == "K":
                        if a == 0:
                            pe.wait_ge(s5_tables_made, 1)
                        for u in range(4):
                            g = 8 * (a // 2) + 2 * u + a % 2
                            rows = slice(64 * (g % 2), 64 * (g % 2) + 64)
                            for e in range(2):
                                ins = pe.matmul(bank[0:SC, u * P:(u + 1) * P], sF[rows, e, g // 2, 0, :],
                                                sG[rows, e, g // 2, 0:CS, :], start=e == 0, stop=e == 1)
                    elif what == "h0":
                        for e in range(2):
                            for f in range(2):
                                ins = pe.transpose(bank[:, (2 * e + f) * P:(2 * e + f + 1) * P], hrow[:, e, f, :], ident[:])
                    elif what == "X":
                        f, e = a
                        pe.wait_ge(s5_z, f + 1)
                        for u in range(4):
                            step_ = 4 * e + 3 - u
                            ins = pe.transpose(bank[0:UC, u * P:(u + 1) * P], sZ[:, f % 2, step_, :], ident[:])
                    elif what == "U":
                        if a % 8 == 0:
                            G.all_emptied(pe, q)
                        for u in range(4):
                            g = (4 * a + u) % 32
                            ins = pe.transpose(bank[:, u * UC:(u + 1) * UC], sX[:, g, :, :].rearrange("n s c -> n (s c)"),
                                               ident[0:UC, 0:UC])
                    elif what == "FU":
                        if a == 0:
                            G.all_emptied(pe, q)
                        pe.wait_ge(s5_tabf_in[a % 2], 16 * (a // 2 + 1))
                        for u in range(4):
                            j, e = 2 * a + u // 2, u % 2
                            for g in range(2):
                                c = (u // 2) * 256 + e * P + 64 * g
                                ins = pe.matmul(bank[64 * g:64 * g + 64, u * UC:(u + 1) * UC],
                                                sTabF[:, a % 2, c:c + 64], sU[:, 2 * j + g, :], start=True, stop=True)
                    elif what == "hfin":
                        pe.wait_ge(s5_scanned, 1)
                        ins = pe.transpose(bank[0:64, 0:P], hfin[:].rearrange("p e j -> p (e j)"), ident[:])
                    elif what == "hs1":
                        for e in range(2):
                            for f in range(2):
                                ins = pe.transpose(bank[:, (2 * e + f) * P:(2 * e + f + 1) * P],
                                                   hs1[:, e, 4 * f:4 * f + 4, :].rearrange("p b j -> p (b j)"), ident[:])
                    elif what == "Y":
                        for v in range(2):
                            j = 2 * a + v
                            pe.wait_ge(s5_tab_in[j % 2], 16 * 4 * (j // 2 + 1))
                            for g in range(2):
                                dst = bank[0:YC, (2 * v + g) * P:(2 * v + g + 1) * P]
                                pe.matmul(dst, sU[:, 2 * j + g, 0:YC], sTab[:, j % 2, g * P:(g + 1) * P],
                                          start=True, stop=False)
                                for e in range(2):
                                    c = 256 * (1 + g) + e * P
                                    ins = pe.matmul(dst, sFH[:, j, e, 0:YC], sTab[:, j % 2, c:c + P],
                                                    start=False, stop=e == 1)
                            if v == 0:
                                ins.then_inc(s5_tab_used, 1)
                    elif what == "y":
                        f, e = a
                        if f % 4 == 0 and e == 0:
                            G.all_emptied(pe, q)
                        for u in range(4):
                            ins = pe.transpose(bank[:, u * YC:(u + 1) * YC],
                                               sY[:, 4 * e + u, (f % 4) * P:(f % 4 + 1) * P], ident[0:YC, 0:YC])
                    ins.then_inc(s5_fill, 1)

            def hgrn():
                G = HG
                for j in range(2):
                    pe.wait_ge(used[j], first_pair["hg_out", 1])
                pe.wait_ge(gated, 2 * HH)
                for q, (what, a, owner) in enumerate(G.groups):
                    G.reuse(pe, q)
                    bank = hg_bank(q)
                    if what == "A":
                        h, u = a
                        e = h % 2
                        if u < len(LEVELS):
                            pe.wait_ge(hg["scaled_pool"], (1 + len(LEVELS)) * h + 2 + u)
                            k_, q_ = lvl[e][u], lvl[e][u]
                        else:
                            pe.wait_ge(hg["scaled_dve"], 2 * h + 1)
                            k_, q_ = dgK[e], dgQ[e]
                        for t in range(4):
                            c = slice(t * P, (t + 1) * P)
                            ins = pe.matmul(bank[:, c], k_[:, c], q_[:, c], start=True, stop=True)
                    elif what == "O":
                        h, e = a, a % 2
                        pe.wait_ge(hg["void_dve"], G.before(G.at("A", (h, len(LEVELS))) + 1, "dve"))
                        pe.wait_ge(hg["void_act"], G.before(G.at("V", h) + 1, "act"))
                        pe.wait_ge(hg["state"], h + 1)
                        for t in range(4):
                            pe.matmul(bank[:, t * P:(t + 1) * P], vTok[:, t, :], attn[e][:, t, :], start=True, stop=False,
                                      skip_group_check=True)
                            for n in range(2 * t, 2 * t + 2):
                                if n:
                                    c = slice(n * HC, (n + 1) * HC)
                                    ins = pe.matmul(bank[:, c], hS[:, n - 1, :], inQ[e][:, c], start=False, stop=True,
                                                    skip_group_check=True)
                    elif what == "V" or what == "K":
                        h, e = a, a % 2
                        if what == "K":
                            pe.wait_ge(hg["scaled_dve"], 2 * h + 2)
                        for t in range(4):
                            c = slice(t * P, (t + 1) * P)
                            ins = pe.transpose(bank[:, c], hgV[:, h, c] if what == "V" else outK[e][:, c], ident[:])
                    elif what == "D":
                        h, odd = a
                        pe.wait_ge(hg["void_act"], G.before(G.at("K", h) + 1, "act"))
                        rows = slice(HC * odd, HC * (odd + 1))
                        for t in range(4):
                            ins = pe.matmul(bank[:, t * P:(t + 1) * P], kTok[rows, t, :], vTok[rows, t, :],
                                            start=True, stop=True)
                    elif what == "B":
                        b, f = a
                        for u in range(4):
                            h = 4 * f + u
                            ins = pe.matmul(bank[:, u * P:(u + 1) * P],
                                            hgV[:, h, SEQ + b:SEQ + b + 1].to_broadcast([P, P]), ident[:],
                                            start=True, stop=True)
                    elif what == "S":
                        for b in range(NS):
                            pe.wait_ge(hg["s_state"], 2 * (b + 1))
                            for h in range(HH):
                                ins = pe.matmul(bank[:, h * NS + b:h * NS + b + 1], sS[:, b, h, :],
                                                hgQ[:, h, SEQ + b:SEQ + b + 1], start=True, stop=True)
                    else:
                        h, e = a
                        pe.wait_ge(hg["squares"], h + 1)
                        ins = pe.matmul(bank[:, 0:HT], ones[:], (t1, t2)[h % 2][:, e * HT:(e + 1) * HT],
                                        start=True, stop=True)
                    ins.then_inc(hg["fill"], 1)
                G.all_emptied(pe, len(G.groups))

            def transposes_kv(layer, which):
                src = kT[layer] if which == 0 else vT
                n = next(n for n, s_ in enumerate(ST) if s_[:2] == ("v" if which else "k", layer))
                for j in range(2):
                    pe.wait_ge(used[j], first_pair[ST[n][0], layer] + ST[n][2])
                for t in range(2):
                    for half in range(2):
                        q = 8 * layer + 4 * which + 2 * t + half
                        wait(pe, kv_evac, q - 1)
                        if q == 0:
                            pe.wait_ge(mem_root, 1)
                        for u in range(4):
                            ins = pe.transpose(mis[:, 2 + q % 2, u * P:(u + 1) * P],
                                               src[:, 4 * half + u, t * P:(t + 1) * P], ident[:])
                        ins.then_inc(kv_tr, 1)

            def stream(n):
                name, layer, pairs, kt = ST[n]
                r = norm_of.get((name, layer))
                mem = name in ("k", "v")
                hidden = from_hidden(name)
                x_hi, x_lo = (m_hi, m_lo) if mem else (h_hi, h_lo) if hidden else (a_hi, a_lo)
                if hidden:
                    x_done, x0 = h_lo_done, hidden_before(n)
                elif mem:
                    x_done, x0 = m_lo_done, KD * layer
                else:
                    r_in = next(norm_of[k_] for k_ in reversed([s_[:2] for s_ in ST[:n + 1]]) if k_ in norm_of)
                    x_done, x0 = a_lo_done, KD * split_norms.index(r_in)

                def body(p, i, first, last):
                    for j in range(2):
                        pe.wait_ge(lo_ready, 2 * p + j + 1)
                        wait(pe, used[j], p)
                        for k in range(kt):
                            if first and j == 0:
                                pe.wait_ge(x_done, x0 + k + 1)
                            for u, (w, x) in enumerate(((w_hi, x_hi), (w_hi, x_lo), (w_lo, x_hi))):
                                start, stop = k == 0 and u == 0, k == kt - 1 and u == 2
                                if mem:
                                    ins = pe.matmul(lslot(j, NM), w[:, j, k, :], x[:, k, :], start=start, stop=stop)
                                    continue
                                for half in range(2):
                                    ins = pe.matmul(lin[:, j, half, 0:HT], w[:, j, k, :],
                                                    x[:, k, half * HT:(half + 1) * HT], start=start, stop=stop)
                        ins.then_inc(chunk_done, 1)
                        if first and j == 0 and r is not None:
                            sums(r)
                over_pairs(pe, n, body)
                if mem:
                    transposes_kv(layer, 0 if name == "k" else 1)

            for n in range(len(ST)):
                if ST[n][0] == "glu":
                    s5()
                if ST[n][0] == "hg_out":
                    hgrn()
                if ST[n][0] == "xo":
                    attend(ST[n][1])
                stream(n)
            sums(NORMS - 1)
            for q in range(10):
                t, half = q // 2, q % 2
                wait(pe, y_evac, q - 1)
                cols = P if t < 4 else NS
                for u in range(4):
                    pe.wait_ge(y_normed, 4 * half + u + 1)
                    ins = pe.transpose(mis[0:cols, 2 + q % 2, u * P:(u + 1) * P],
                                       yT[:, 4 * half + u, t * P:t * P + cols], ident[:])
                ins.then_inc(y_tr, 1)


_INS = ["x_prompt", "x_sample", "mem_prompt", "state_s5_re", "state_s5_im", "state_hgrn", "cache_mem_k", "cache_mem_v",
        "ffn1_norm", "ffn1_w_in", "ffn1_w_out", "mix_norm", "xattn_norm", "mem_norm", "xattn_w_q", "xattn_w_kv",
        "xattn_w_o", "ffn2_norm", "ffn2_w_in", "ffn2_w_out", "s5_a_re", "s5_a_im", "s5_log_dt", "s5_b_re", "s5_b_im",
        "s5_c_re", "s5_c_im", "s5_d", "s5_w_glu", "hg_w_in", "hg_lb_logits", "hg_norm", "hg_w_out", "final_norm"]
_OUTS = [("y_prompt", (1, SEQ, D)), ("y_sample", (NS, 1, D)), ("s5_re_p", (1, 1, SG, SP_)), ("s5_im_p", (1, 1, SG, SP_)),
         ("s5_re_s", (1, NS, SG, SP_)), ("s5_im_s", (1, NS, SG, SP_)), ("hg_p", (1, 1, HH, P, P)),
         ("hg_s", (1, NS, HH, P, P)), ("mem_k", (DEPTH, 1, NM, MH, D // MH)), ("mem_v", (DEPTH, 1, NM, MH, D // MH))]


def kernel(**inputs):
    import numpy as _np
    import concourse.bacc as _bacc
    from concourse import mybir as _mybir
    from concourse.bass_utils import run_bass_kernel_spmd as _run

    nc = _bacc.Bacc("TRN2", target_bir_lowering=False, num_devices=1)
    arrays, ins, outs = {}, {}, {}
    for name in _INS:
        a = _np.ascontiguousarray(inputs[name])
        arrays[f"in_{name}_dram"] = a
        ins[name] = nc.dram_tensor(f"in_{name}_dram", a.shape, _mybir.dt.from_np(a.dtype), kind="ExternalInput").ap()
    for name, shape in _OUTS:
        outs[name] = nc.dram_tensor(f"out_{name}_dram", shape, F32, kind="ExternalOutput").ap()
    trunk_kernel(nc, ins, outs)
    r = _run(nc, [arrays], core_ids=[0])
    return tuple(r.results[0][f"out_{name}_dram"] for name, _ in _OUTS)
```

```python
import math
import numpy as np
import concourse.bass as bass
from concourse import mybir

F32 = mybir.dt.float32
F32R = mybir.dt.float32r
I32 = mybir.dt.int32
ALU = mybir.AluOpType
ACT = mybir.ActivationFunctionType
AX = mybir.AxisListType

P = 128
D = 1024
KD = D // P
SEQ = 512
NS = 8
NT = SEQ + NS
HT = NT // 2
DEPTH = 2
FFN = 2816
FH = FFN // P // 2
NM = 256
MH = 4
EPS = 1e-6
SG, SC, SP_, CS = 64, 16, 64, 8
NJ = SG // 2
NC = SEQ // CS
CB = 8
UC = NC + 2 * NS
YC = NC + NS
HH = 8
HC = 64
NHC = SEQ // HC
LEVELS = (32, 16, 8)

V_FFN1, V_MIX, V_XA, V_MEM, V_FFN2, V_FIN, V_D, V_LB, V_HG = 0, 16, 32, 48, 64, 80, 88, 96, 112
NVEC = 113


class Chain:

    def __init__(self, eng, sem):
        self.eng, self.sem, self.n, self.off = eng, sem, 0, 0

    def link(self, ins):
        ins.then_inc(self.sem, 1)
        self.n += 1
        self.eng.wait_ge(self.sem, self.off + self.n)

    def loop(self, i, first, per):
        self.off = (i - first) * per
        self.start, self.per = self.n, per

    def done(self, turns):
        assert self.n == self.start + self.per, (self.n - self.start, self.per)
        self.n = self.start + self.per * turns
        self.off = 0


BLOCKS = [("ffn1", 0), ("s5", 0), ("xattn", 0), ("ffn2", 0), ("ffn1", 1), ("hgrn", 1), ("xattn", 1), ("ffn2", 1)]
GAIN_ROW = {"ffn1": V_FFN1, "s5": V_MIX, "hgrn": V_MIX, "xattn": V_XA, "ffn2": V_FFN2}


class Groups:

    def __init__(self, groups, filled, emptied, banks=4):
        self.groups, self.filled, self.emptied, self.banks = groups, filled, emptied, banks

    def before(self, q, engine):
        return sum(g[2] == engine for g in self.groups[:q])

    def reuse(self, eng, q):
        if q >= self.banks:
            owner = self.groups[q - self.banks][2]
            eng.wait_ge(self.emptied[owner], self.before(q - self.banks + 1, owner))

    def all_emptied(self, eng, q):
        for owner, semaphore in self.emptied.items():
            if self.before(q, owner):
                eng.wait_ge(semaphore, self.before(q, owner))

    def emptied_of(self, eng, what, a):
        q = self.at(what, a)
        eng.wait_ge(self.emptied[self.groups[q][2]], self.before(q + 1, self.groups[q][2]))

    def first(self, what):
        return next(q for q, g in enumerate(self.groups) if g[0] == what)

    def at(self, what, a):
        return next(q for q, g in enumerate(self.groups) if g[:2] == (what, a))

    def after(self, what):
        return 1 + max(q for q, g in enumerate(self.groups) if g[0] == what)


def streams():
    out = []
    for layer in range(DEPTH):
        out += [("k", layer, 4, KD), ("v", layer, 4, KD)]
    for block, layer in BLOCKS:
        if block in ("ffn1", "ffn2"):
            for half in range(2):
                out += [(f"{block}_in{half}", layer, FH, KD), (f"{block}_out{half}", layer, 4, FH)]
        elif block == "s5":
            out += [("glu", layer, 8, KD)]
        elif block == "hgrn":
            out += [("hg_qf", layer, 8, KD), ("hg_vg", layer, 8, KD), ("hg_out", layer, 4, KD)]
        else:
            out += [("xq", layer, 4, KD), ("xo", layer, 4, KD)]
    return out


LAST = {"ffn1": "ffn1_out1", "ffn2": "ffn2_out1", "s5": "glu", "hgrn": "hg_out", "xattn": "xo"}
FIRST = {"ffn1": "ffn1_in0", "ffn2": "ffn2_in0", "hgrn": "hg_qf", "xattn": "xq"}


def trunk_kernel(nc, i_, o_):
    ST = streams()
    first_pair, at_pair = {}, 0
    for name, layer, pairs, _ in ST:
        first_pair[name, layer] = at_pair
        at_pair += pairs
    ALL_PAIRS = at_pair
    NORM_ROW = [GAIN_ROW[b] + KD * l for b, l in BLOCKS] + [V_FIN]
    NORMS = len(NORM_ROW)
    norm_of = {(FIRST[b], l): r for r, (b, l) in enumerate(BLOCKS) if b in FIRST}
    norm_after = {(LAST[b], l): r + 1 for r, (b, l) in enumerate(BLOCKS)}
    split_norms = [r for r, (b, l) in enumerate(BLOCKS) if b in FIRST]
    gain_after = {k: r for k, r in norm_after.items() if r in split_norms}

    def at(name, shape, dtype, offset):
        return nc.alloc_sbuf_tensor_at(name, shape, dtype, offset=offset)

    base = (nc.sbuf_base + 63) // 64 * 64
    TILE = NT * 4
    off = base
    o_x = off; off += KD * TILE
    o_ah = off; off += KD * TILE
    o_al = off; off += KD * TILE
    CH = FH * P * 4
    o_raw = off; off += 2 * CH
    o_wh = off; off += 2 * CH
    o_wl = off; off += 2 * CH
    o_hid = off; off += 2 * FH * TILE
    o_small = off; off += 16640
    o_s0 = off; off += 33536
    o_kv = off; off += DEPTH * 16384
    assert off <= nc.sbuf_usable_end, (off, nc.sbuf_usable_end)
    assert 3 * KD * TILE <= 33536 + 16384

    xT = at("xT", [P, KD, NT], F32, o_x)
    a_hi = at("a_hi", [P, KD, NT], F32R, o_ah)
    a_lo = at("a_lo", [P, KD, NT], F32R, o_al)
    raw = at("raw", [P, 2, FH, P], F32, o_raw)
    w_hi = at("w_hi", [P, 2, FH, P], F32R, o_wh)
    w_lo = at("w_lo", [P, 2, FH, P], F32R, o_wl)
    h_hi = at("h_hi", [P, FH, NT], F32R, o_hid)
    h_lo = at("h_lo", [P, FH, NT], F32R, o_hid + FH * TILE)
    s = o_small
    ident = at("ident", [P, P], F32, s); s += 512
    ones = at("ones", [P, P], F32, s); s += 512
    zeros = at("zeros", [P, P], F32, s); s += 512
    eps = at("eps", [P, 1], F32, s); s += 32
    vec = at("vec", [P, NVEC], F32, s); s += 480
    assert s == o_small + 2048
    rstd = at("rstd", [P, NT], F32, s); s += TILE
    t1 = at("t1", [P, NT], F32, s); s += TILE
    t2 = at("t2", [P, NT], F32, s); s += TILE
    t3 = at("t3", [P, NT], F32, s); s += TILE
    t4 = at("t4", [P, NT], F32, s); s += TILE
    sqt = at("sqt", [P, NT], F32, s); s += TILE
    acc = at("acc", [P, NT], F32, s); s += TILE
    assert s <= o_small + 16640
    kT = [at(f"kT{l}", [P, KD, NM], F32, o_kv + l * 16384) for l in range(DEPTH)]
    vM = [at(f"vM{l}", [P, 2, D], F32, o_kv + l * 16384 + 8192) for l in range(DEPTH)]

    xin = at("xin", [P, 4, D], F32, o_hid)
    xsin = at("xsin", [NS, D], F32, o_hid + 16384)
    min_ = at("min_", [P, 2, D], F32, o_hid + 20480)
    vrows = at("vrows", [P, P], F32, o_hid + 28672)
    kOut = at("kOut", [P, 2, D], F32, o_hid)
    vT = at("vT", [P, KD, NM], F32, o_hid + 8192)
    mT = at("mT", [P, KD, NM], F32, o_s0)
    m_hi = at("m_hi", [P, KD, NM], F32R, o_s0 + 8192)
    m_lo = at("m_lo", [P, KD, NM], F32R, o_s0 + 16384)
    m_rstd = at("m_rstd", [P, NM], F32, o_s0 + 24576)
    m_acc = at("m_acc", [P, NM], F32, o_s0 + 25600)
    m_sq = at("m_sq", [P, NM], F32, o_s0 + 26624)
    qT = at("qT", [P, KD, NT], F32, o_s0)
    pP = at("pP", [P, 4, 2, NM], F32, o_ah + 16384)
    pT = at("pT", [P, 2, 2, SEQ], F32, o_ah + 24576)
    kc = [at(f"kc{q}", [P, D], F32, o_hid + 2 * TILE + 4096 * (q // 2) + (FH * TILE if q % 2 else 0)) for q in range(8)]
    kc += [at(f"kc{8 + q}", [P, D], F32, o_ah + 4096 * q) for q in range(4)]
    vc = [at(f"vc{q}", [P, 2, D], F32, (o_s0 + 16640, o_s0 + 24832, o_small + 2048 + TILE, o_ah, o_ah + 8192)[q])
          for q in range(5)]
    K_SLOT = [v if v < 12 else v - 4 for v in range(2 * NS)]
    V_SLOT = [b if b < 5 else b - 5 for b in range(NS)]
    oS = at("oS", [NS, D], F32, o_ah + 16384)
    c = o_hid + 2 * TILE + 4 * 4096
    pZ = at("pZ", [P, 2, MH, NS, NS], F32, c); c += 2048
    assert c <= o_hid + FH * TILE
    c += FH * TILE - 2048
    sT = at("sT", [P, 2, NS * MH], F32, c); c += 256
    pS = at("pS", [NS * MH, NM], F32, c); c += 1024
    mx = at("mx", [P, 8, 2], F32, c); c += 64
    nmx = at("nmx", [P, 8, 2], F32, c); c += 64
    den = at("den", [P, 8, 2], F32, c); c += 64
    rden = at("rden", [P, 8, 2], F32, c); c += 64
    ssm = at("ssm", [NS * MH, 4], F32, c); c += 32
    assert c <= o_hid + 2 * FH * TILE
    hgQ = at("hgQ", [P, KD, NT], F32, o_hid)
    hgK = at("hgK", [P, KD, NT], F32, o_hid + KD * TILE)
    hgF = at("hgF", [P, KD, NT], F32, o_s0)
    hgV = at("hgV", [P, KD, NT], F32, o_s0 + KD * TILE)
    hgG = at("hgG", [P, KD, NT], F32, o_s0 + 2 * KD * TILE)
    lvl = [[at(f"lvl{e}{u}", [P, SEQ], F32, o_ah + 16384 * e + 2048 * u) for u in range(len(LEVELS))]
           for e in range(2)]
    dgQ = [at(f"dgQ{e}", [P, SEQ], F32, o_ah + 16384 * e + 6144) for e in range(2)]
    dgK = [at(f"dgK{e}", [P, SEQ], F32, o_ah + 16384 * e + 8192) for e in range(2)]
    inQ = [at(f"inQ{e}", [P, SEQ], F32, o_ah + 16384 * e + 10240) for e in range(2)]
    outK = [at(f"outK{e}", [P, SEQ], F32, o_ah + 16384 * e + 12288) for e in range(2)]
    ebt = [at(f"ebt{e}", [P, NHC], F32, o_ah + 16384 * e + 14336) for e in range(2)]
    sS = at("sS", [P, NS, HH, P], F32, o_ah)
    hS = at("hS", [P, NHC, P], F32, o_small + 2048 + TILE)
    bC = [at(f"bC{e}", [P, SEQ], F32, o_small + 2048 + TILE * (3 + e)) for e in range(2)]
    c = o_hid + 2 * KD * TILE
    attn = [at(f"attn{e}", [P, 4, P], F32, c + 2048 * e) for e in range(2)]; c += 4096
    vTok = at("vTok", [P, 4, P], F32, c); c += 2048
    kTok = at("kTok", [P, 4, P], F32, c); c += 2048
    pair_mask = at("pair_mask", [P, 4, P], F32, c); c += 2048
    lbv = at("lbv", [P, 6, HH], F32, c); c += 192
    fS = at("fS", [P, HH, NS], F32, c); c += 256
    one = at("one", [P, 2 * HH], F32, c); c += 64
    chunk_start = at("chunk_start", [P, SEQ], F32, o_small + 2048 + TILE * 5)
    assert c <= o_hid + 2 * FH * TILE
    sX = at("sX", [UC, SG // 2, CS, SC], F32, o_hid)
    sY = at("sY", [YC, CS, 512], F32, o_hid)
    sFH = at("sFH", [P, NJ, 2, 1 + UC], F32, o_hid + 16384)
    c = o_s0
    bRaw = at("bRaw", [P, 2, NJ, SC], F32, c); c += 4096
    cRaw = at("cRaw", [P, 2, 8, P], F32, c); c += 8192
    sTmp = at("sTmp", [P, 3072], F32, o_s0)
    bBar = at("bBar", [P, 2, NJ, SC], F32, c); c += 4096
    cT = at("cT", [P, 2, NJ, SC], F32, c)
    prow = at("prow", [96, P], F32, c)
    ldrow = at("ldrow", [96, 2], F32, c + 512); c += 4096
    bZ = at("bZ", [P, 2, NJ, 2, SC], F32, c)
    bTmp = at("bTmp", [P, NJ * SC], F32, c); c += 8192
    par = at("par", [P, 96], F32, c); c += 384
    pw = at("pw", [P, 2, CS + 1, NJ], F32, c); c += 2304
    sm = at("sm", [P, 12, NJ], F32, c); c += 1536
    smi = at("smi", [P, NJ], I32, c); c += 128
    assert c <= o_s0 + 33536
    c = o_ah + 5120
    hs0 = at("hs0", [P, 2, NS, NJ], F32, c); c += 2048
    hs1 = at("hs1", [P, 2, NS, NJ], F32, c); c += 2048
    hst = at("hst", [P, 2, NS, NJ], F32, c); c += 2048
    hrow = at("hrow", [P, 2, 2, P], F32, c); c += 2048
    frow = at("frow", [64, P], F32, c); c += 512
    hfin = at("hfin", [P, 2, NJ], F32, c); c += 256
    assert c <= o_al
    c = o_hid + 42240
    cw = at("cw", [P, 2, CB + 1, NJ], F32, c); c += 2304
    lam1 = at("lam1", [P, 2, NJ], F32, c); c += 256
    ncw = at("ncw", [P, 2, NJ], F32, c); c += 256
    assert c <= o_hid + 2 * FH * TILE
    sc = [at(f"sc{e}", [P, NJ // 2 * NC], F32, o_small + 2048 + TILE + 4096 * e) for e in range(2)]
    sG = at("sG", [P, 2, NJ, CS + 1, SC], F32, o_hid)
    sF = at("sF", [P, 2, NJ, CS, SC], F32, o_ah)
    sFst = at("sFst", [P, 2, 512], F32, o_hid + 36864)
    sGt = [at(f"sGt{e}", [P, NJ // 4 * (CS + 1) * SC], F32, o_small + 2048 + 4608 * e) for e in range(2)]
    sK = at("sK", [2 * SC, NJ, P], F32, o_ah)
    u32 = at("u32", [P, KD, NT], F32, o_al)
    sZ = at("sZ", [P, 2, CS, UC], F32, o_hid + 37120)
    sU = at("sU", [P, SG, UC], F32, o_s0)
    sTab = at("sTab", [P, 2, 2, 256], F32, o_s0 + 20480)
    sTabG = at("sTabG", [P, 2, 2, 512], F32, o_s0 + 24576)
    sTabF = at("sTabF", [P, 2, 512], F32, o_small + 2048 + 5 * TILE)
    s5_fg = nc.dram_tensor("s5_fg", (NJ, P, 512), F32, kind="Internal").ap()
    s5_t = nc.dram_tensor("s5_t", (P, SG, P), F32, kind="Internal").ap()
    yT = at("yT", [P, KD, NT], F32, o_ah)
    yout = at("yout", [P, 4, D], F32, o_hid)
    ysout = at("ysout", [NS, D], F32, o_hid + 16384)

    lin = nc.alloc_psum_tensor("lin", [P, 2, 2, 512], F32)
    mis = nc.alloc_psum_tensor("mis", [P, 4, 512], F32)

    def lslot(j, n=NT):
        return lin[:, j, :, 0:HT] if n == NT else lin[:, j, 0, 0:n]

    def two(ap):
        return ap.rearrange("p (a b) -> p a b", a=2)

    def tile(t, m):
        return t[:, bass.ds(m, 1), :].rearrange("p o n -> p (o n)")

    def twotile(t, m):
        return t[:, bass.ds(m, 1), :].rearrange("p o (a b) -> p (o a) b", a=2)

    def sem(name):
        return nc.alloc_semaphore(name)

    mem_loaded, loaded = sem("mem_loaded"), sem("loaded")
    vrows_loaded = sem("vrows_loaded")
    raw_arrived = [sem("raw_arrived0"), sem("raw_arrived1")]
    hi_ready = sem("hi_ready")
    lo_ready = sem("lo_ready")
    chunk_done = sem("chunk_done")
    used = [sem("used0"), sem("used1")]
    a_hi_done = sem("a_hi_done")
    a_lo_done = sem("a_lo_done")
    squares_done = sem("squares_done")
    sums_done = sem("sums_done")
    root_done = sem("root_done")
    gate_out = sem("gate_out")
    h_hi_done = sem("h_hi_done")
    h_lo_done = sem("h_lo_done")
    dve_step, act_step, pool_step = sem("dve_step"), sem("act_step"), sem("pool_step")
    f_out = sem("f_out")
    gated = sem("gated")
    s5_rows, s5_bc, s5_small = sem("s5_rows"), sem("s5_bc"), sem("s5_small")
    s5_sin, s5_phase, s5_square, s5_inverse = sem("s5_sin"), sem("s5_phase"), sem("s5_square"), sem("s5_inverse")
    s5_powers, s5_g0, s5_coef_kept, s5_t_out = sem("s5_powers"), sem("s5_g0"), sem("s5_coef_kept"), sem("s5_t_out")
    s5_tables_made = sem("s5_tables_made")
    s5_fill, s5_void = sem("s5_fill"), {"dve": sem("s5_void_dve"), "act": sem("s5_void_act")}
    s5_f_out = [sem("s5_f_out0"), sem("s5_f_out1")]
    s5_tab_out, s5_zeros_out = sem("s5_tab_out"), sem("s5_zeros_out")
    s5_state_in, s5_state_out = sem("s5_state_in"), sem("s5_state_out")
    s5_z, s5_scanned, s5_fin = sem("s5_z"), sem("s5_scanned"), sem("s5_fin")
    s5_tab_in = [sem("s5_tab_in0"), sem("s5_tab_in1")]
    s5_tabf_in = [sem("s5_tabf_in0"), sem("s5_tabf_in1")]
    s5_tables_f = sem("s5_tables_f")
    s5_tab_clear = sem("s5_tab_clear")
    s5_state_done = sem("s5_state_done")
    xa = []
    for l in range(DEPTH):
        xa.append(dict(fill=sem(f"xa_fill{l}"), void={"dve": sem(f"xa_void_dve{l}"), "act": sem(f"xa_void_act{l}")},
                       max=sem(f"xa_max{l}"), prob=sem(f"xa_prob{l}"), zeros=sem(f"xa_zeros{l}"), pv=sem(f"xa_pv{l}"),
                       s_max=sem(f"xa_s_max{l}"), s_prob=sem(f"xa_s_prob{l}"), o_hi=sem(f"xa_o_hi{l}"),
                       rows=sem(f"xa_rows{l}"), clear=sem(f"xa_clear{l}")))
    keys_in = [sem(f"keys_in{q}") for q in range(12)]
    values_in = [sem(f"values_in{q}") for q in range(5)]
    hg = {name: sem("hg_" + name) for name in
          ("fill", "void_dve", "void_act", "lb_diff", "lb_exp", "lb", "consts", "log", "decay", "exps", "scaled_pool",
           "scaled_dve", "state", "state_out", "s_decay", "s_state", "s_out", "squares", "squares_read",
           "inverse", "normed")}
    hg_s_in = [sem(f"hg_s_in{b}") for b in range(NS)]
    consts_done = sem("consts_done")
    vec_tr, vec_done = sem("vec_tr"), sem("vec_done")
    in_tr, in_evac = sem("in_tr"), sem("in_evac")
    mem_squares, mem_sums, mem_root, mem_rstd = sem("mem_squares"), sem("mem_sums"), sem("mem_root"), sem("mem_rstd")
    m_hi_done, m_lo_done = sem("m_hi_done"), sem("m_lo_done")
    kv_tr, kv_evac, kv_out = sem("kv_tr"), sem("kv_evac"), sem("kv_out")
    y_normed, y_tr, y_evac, y_out = sem("y_normed"), sem("y_tr"), sem("y_evac"), sem("y_out")

    def weights(n, i, j):
        name, layer, _, kt = ST[n]
        if name in ("k", "v"):
            w, c = i_["xattn_w_kv"][layer], (2 * i + j) * P + (D if name == "v" else 0)
        elif name[:3] == "ffn" and name[4:7] == "_in":
            half = int(name[7])
            w, c = i_[f"ffn{name[3]}_w_in"][layer], (i + half * FH) * P + j * FFN
        elif name[:3] == "ffn":
            half = int(name[8])
            w = i_[f"ffn{name[3]}_w_out"][layer][half * FH * P:(half + 1) * FH * P, :]
            c = (2 * i + j) * P
        elif name == "glu":
            return i * P, i_["s5_w_glu"][0].rearrange("(k p) (a n) -> p k a n", p=P, a=2)[:, :, 1 - j, :]
        elif name == "hg_qf":
            w, c = i_["hg_w_in"][0], i * P + j * D
        elif name == "hg_vg":
            w, c = i_["hg_w_in"][0], i * P + (2 + j) * D
        elif name == "hg_out":
            w, c = i_["hg_w_out"][0], (2 * i + j) * P
        elif name == "xq":
            w, c = i_["xattn_w_q"][layer], (2 * i + j) * P
        else:
            w, c = i_["xattn_w_o"][layer], (2 * i + j) * P
        return c, w.rearrange("(k p) n -> p k n", p=P)

    def over_pairs(eng, n, body):
        name, layer, pairs, _ = ST[n]
        p0 = first_pair[name, layer]
        body(p0, 0, True, False)
        with eng.Fori(0, pairs - 2) as i:
            body(p0 + 1 + i, 1 + i, False, False)
        body(p0 + pairs - 1, pairs - 1, False, True)

    def tiles_of(n, p, j, last):
        if j == 0 or not last:
            return ST[n][3]
        return ST[n + 1][3] if n + 1 < len(ST) else None

    def from_hidden(name):
        return FH if name[:3] == "ffn" and "_out" in name else KD if name in ("glu", "xo", "hg_out") else 0

    def hidden_before(n):
        return sum(from_hidden(s_[0]) for s_ in ST[:n])

    def number(name, layer=0):
        return next(n for n, s_ in enumerate(ST) if s_[:2] == (name, layer))

    def gate_base(n):
        per = {"ffn1_in0": FH, "ffn1_in1": FH, "ffn2_in0": FH, "ffn2_in1": FH, "hg_qf": 8, "hg_vg": 8}
        return sum(per.get(s_[0], 0) for s_ in ST[:n])

    def is_in(name):
        return name[:3] == "ffn" and "_in" in name

    def is_out(name):
        return (name[:3] == "ffn" and "_out" in name) or name in ("xo", "hg_out")

    def wait(eng, semaphore, value):
        if isinstance(value, int) and value <= 0:
            return
        eng.wait_ge(semaphore, value)

    def arrivals(slots, n, layer):
        return 16 * (layer * slots.count(slots[n]) + slots[:n + 1].count(slots[n]))

    def bank_of(q):
        q %= 8
        return mis[:, q, :] if q < 4 else lin[:, (q - 4) // 2, q % 2, :]

    made = []
    for h in range(MH):
        for e in range(2):
            made += [("B", (2 * h + e, f), "dve") for f in range(2)] + [("S", (h, e), "act")]
        if h:
            made += [("O", (h - 1, e), "dve") for e in range(2)]
        if h == MH - 1:
            made += [("T", 0, "act")]
        made += [("P", (h, e), "act" if e else "dve") for e in range(2)]
    made += [("W", 0, "dve")] + [("O", (MH - 1, e), "dve") for e in range(2)] + [("V", 0, "dve")]
    XAG = [Groups(made, xa[l]["fill"], xa[l]["void"], banks=6) for l in range(DEPTH)]

    def xa_bank(q):
        q %= 6
        return mis[:, q, :] if q < 4 else lin[:, 0, q - 4, :]

    XA_SCALE = 1.0 / math.sqrt(D // MH)

    made = []
    for h in range(HH + 1):
        if h < HH:
            made += [("A", (h, u), "dve") for u in range(len(LEVELS) + 1)]
        if h:
            made += [("O", h - 1, "act")]
        if h < HH:
            made += [("V", h, "act"), ("K", h, "act"), ("D", (h, 0), "dve"), ("D", (h, 1), "dve")]
    made += [("B", (b, e), "dve") for b in range(NS) for e in range(2)]
    made += [("S", 0, "dve")]
    made += [("N", e, "act") for e in range(2)]
    made += [("R", (h, e), "dve") for h in range(HH) for e in range(2)]
    HG = Groups(made, hg["fill"], {"dve": hg["void_dve"], "act": hg["void_act"]}, banks=8)

    EXPS, DECAYS = 3 + len(LEVELS), 3 + len(LEVELS)

    made = [("par", 0, "dve")] + [("c", (e, f), "dve") for e in range(2) for f in range(2)]
    S5_EARLY = len(made)
    made += [("F", q, "act") for q in range(NJ // 2)]
    made += [("K", q, "act" if q % 2 else "dve") for q in range(NJ // 4)]
    S5_MADE = len(made)
    for hf in range(2):
        made += [("X", (4 * hf + f, e), "act") for f in range(4) for e in range(2)]
        made += [("U", 8 * hf + q, "act" if hf or q % 2 == 0 else "dve") for q in range(8)]
        made += [("FU", 8 * hf + q, "act" if hf or q % 2 == 0 else "dve") for q in range(8)]
        if hf == 0:
            made += [("h0", 0, "dve")]
    for hf in range(2):
        made += [("Y", 8 * hf + q, "dve" if q % 2 and hf else "act") for q in range(8)]
        if hf == 0:
            made += [("hfin", 0, "dve"), ("hs1", 0, "dve")]
        made += [("y", (4 * hf + f, e), "dve") for f in range(4) for e in range(2)]
    S5G = Groups(made, s5_fill, s5_void, banks=8)
    s5_norm = next((r for r, (b, l) in enumerate(BLOCKS) if b == "s5"), None)

    def times(eng, link, out_r, out_i, ar_, ai_, br_, bi_, tmp):
        link(eng.tensor_tensor(out_r, ar_, br_, ALU.mult))
        link(eng.tensor_tensor(tmp, ai_, bi_, ALU.mult))
        link(eng.tensor_tensor(out_r, out_r, tmp, ALU.subtract))
        link(eng.tensor_tensor(out_i, ar_, bi_, ALU.mult))
        link(eng.tensor_tensor(tmp, ai_, br_, ALU.mult))
        link(eng.tensor_tensor(out_i, out_i, tmp, ALU.add))

    def powers(eng, link, p_):
        for n in (1, 2, 4):
            by = [p_[:, e, n, :].unsqueeze(1).to_broadcast([P, n, NJ]) for e in range(2)]
            times(eng, link, p_[:, 0, n + 1:2 * n + 1, :], p_[:, 1, n + 1:2 * n + 1, :], p_[:, 0, 1:n + 1, :],
                  p_[:, 1, 1:n + 1, :], by[0], by[1], (bTmp if p_ is pw else sTmp)[:, 0:n * NJ]
                  .rearrange("p (n j) -> p n j", n=n))

    def table_part(eng, link, out, n, m, parts, j0, j1, tmp):
        shape = [P, j1 - j0, n, SC]
        pv = [pw[:, e, 0:n, j0:j1].rearrange("p d j -> p j d").unsqueeze(3).to_broadcast(shape) for e in range(2)]
        mv = [m[:, e, j0:j1].unsqueeze(2).to_broadcast(shape) for e in range(2)]
        tmp = tmp[:, 0:(j1 - j0) * n * SC].rearrange("p (j d c) -> p j d c", j=j1 - j0, d=n)
        for part in parts:
            o = out[:, min(part, 1), j0:j1]
            link(eng.tensor_tensor(o, pv[0], mv[min(part, 1)], ALU.mult))
            link(eng.tensor_tensor(tmp, pv[1], mv[1 - min(part, 1)], ALU.mult))
            if part == 2:
                link(eng.scalar_tensor_tensor(out=o, in0=o, scalar=-1.0, in1=tmp, op0=ALU.mult, op1=ALU.subtract))
            else:
                link(eng.tensor_tensor(o, o, tmp, ALU.add if part else ALU.subtract))

    block = nc.Block()
    with block:
        @block.sync
        def _(sp):
            sp.dma_start(min_[:], i_["mem_prompt"][0].rearrange("(t p) d -> p t d", p=P)).then_inc(mem_loaded, 16)
            sp.dma_start(xin[:], i_["x_prompt"][0].rearrange("(t p) d -> p t d", p=P)).then_inc(loaded, 16)
            sp.dma_start(xsin[:], i_["x_sample"].rearrange("b o d -> (b o) d")).then_inc(loaded, 16)

            def keys(layer, v):
                sp.dma_start(kc[K_SLOT[v]][:], i_["cache_mem_k"][layer, v // 2, v % 2 * P:(v % 2 + 1) * P]
                             .rearrange("p h d -> p (h d)")).then_inc(keys_in[K_SLOT[v]], 16)

            def values(layer, b):
                sp.dma_start(vc[V_SLOT[b]][:], i_["cache_mem_v"][layer, b].rearrange("(t p) h d -> p t (h d)", p=P))\
                    .then_inc(values_in[V_SLOT[b]], 16)

            def early_caches(layer, i):
                if i == 0:
                    sp.wait_ge(chunk_done, 2 * first_pair["xq", layer] + 1)
                for v in ((0, 1), (2, 3, 4), (5, 6, 7), ())[i]:
                    keys(layer, v)
                if i == 3:
                    values(layer, 0)

            def caches(layer):
                G, X = XAG[layer], xa[layer]
                sp.wait_ge(chunk_done, 2 * first_pair["xo", layer])
                for v in range(8, 12):
                    keys(layer, v)
                values(layer, 1)
                values(layer, 2)
                for v in range(12, 16):
                    G.emptied_of(sp, "B", ((v - 4) // 2, 1))
                    keys(layer, v)
                for b in range(3, NS):
                    if b < 5:
                        G.emptied_of(sp, "B", (b + 3, 1))
                    else:
                        sp.wait_ge(X["pv"], b - 4)
                    values(layer, b)

            def s5_parameters():
                for j in range(2):
                    sp.wait_ge(used[j], first_pair["ffn1_in0", 0])
                sp.wait_ge(kv_tr, 8 * DEPTH)
                for q, name in enumerate(("s5_a_re", "s5_a_im")):
                    sp.dma_start(prow[32 * q:32 * q + 32, :], i_[name][0].rearrange("(j g) p -> j (g p)", g=2))\
                        .then_inc(s5_rows, 16)
                sp.dma_start(ldrow[64:96, :], i_["s5_log_dt"][0].rearrange("(j g) -> j g", g=2)).then_inc(s5_rows, 16)
                for q, name in enumerate(("s5_b_re", "s5_b_im")):
                    b = i_[name][0].rearrange("(j g) p c -> g p j c", g=2)
                    for g in range(2):
                        sp.dma_start(bRaw[64 * g:64 * g + 64, q], b[g]).then_inc(s5_bc, 16)
                for q, name in enumerate(("s5_c_re", "s5_c_im")):
                    for e in range(2):
                        sp.dma_start(cRaw[:, q, :, 64 * e:64 * e + 64],
                                     i_[name][0].rearrange("(t g) c p -> (g c) t p", t=8)).then_inc(s5_bc, 16)

            def s5_tables(sp):
                for q in range(NJ // 2):
                    S = S5G.first("F") + q
                    sp.wait_ge(s5_void["act"], S5G.before(S + 1, "act"))
                    sp.dma_start(s5_fg[2 * q:2 * q + 2, :, 0:256].rearrange("j p n -> p j n"),
                                 sFst[:, q % 2, :].rearrange("p (j n) -> p j n", j=2)).then_inc(s5_f_out[q % 2], 16)
                sp.wait_ge(s5_tables_made, 1)
                sp.wait_ge(s5_g0, 1)
                for e in range(2):
                    sp.dma_start(s5_fg[:, :, 256 + P * e:256 + P * (e + 1)].rearrange("j p n -> p j n"),
                                 sG[:, e, :, 1:, :].rearrange("p j d c -> p j (d c)")).then_inc(s5_tab_out, 16)
                S5G.all_emptied(sp, S5G.after("K"))
                sp.wait_ge(s5_zeros_out, 16 * (CS - 1))
                for d in range(CS):
                    for g in range(2):
                        dst = s5_t[SC * d:SC * (d + 1), g::2, SC * (CS - 1 - d):]
                        sp.dma_start(dst, sK[SC * g:SC * (g + 1), :, 0:SC * (d + 1)]).then_inc(s5_t_out, 16)
                sp.wait_ge(s5_tab_out, 16 * 2)
                sp.wait_ge(s5_f_out[0], 16 * NJ // 4)
                sp.wait_ge(s5_f_out[1], 16 * NJ // 4)
                sp.wait_ge(s5_coef_kept, 1)
                for q in range(NJ // 2):
                    if q == 2:
                        sp.wait_ge(s5_t_out, 16 * 2 * CS)
                        for part, name in enumerate(("state_s5_re", "state_s5_im")):
                            rows = i_[name][0].rearrange("b (j g) p -> (b j) (g p)", g=2)
                            for e in range(2):
                                sp.dma_start(hrow[:, part, e, :], rows[e * P:(e + 1) * P, :]).then_inc(s5_state_in, 16)
                    if q >= 2:
                        sp.wait_ge(s5_fill, S5G.at("FU", q - 2) + 1)
                    sp.dma_start(sTabF[:, q % 2, :].rearrange("p (j n) -> p j n", j=2),
                                 s5_fg[2 * q:2 * q + 2, :, 0:256].rearrange("j p n -> p j n"))\
                        .then_inc(s5_tabf_in[q % 2], 16)
                sp.wait_ge(s5_tab_clear, 1)
                for q in range(NJ // 2):
                    if q >= 2:
                        sp.wait_ge(s5_fill, S5G.at("Y", q - 2) + 1)
                    sp.dma_start(sTab[:, q % 2].rearrange("p v n -> p (v n)"),
                                 s5_t[:, 4 * q:4 * q + 4, :].rearrange("p g n -> p (g n)"))\
                        .then_inc(s5_tab_in[q % 2], 16)
                    for g in range(2):
                        sp.dma_start(sTabG[64 * g:64 * g + 64, q % 2, :, 256 * g:256 * (g + 1)],
                                     s5_fg[2 * q:2 * q + 2, 64 * g:64 * g + 64, 256:512].rearrange("j p n -> p j n"))\
                            .then_inc(s5_tab_in[q % 2], 16)
                sp.wait_ge(s5_fin, 1)
                sp.dma_start(o_["s5_re_p"][0, 0].rearrange("(j g) p -> j (g p)", g=2), frow[0:32, :])\
                    .then_inc(s5_state_out, 16)
                sp.dma_start(o_["s5_im_p"][0, 0].rearrange("(j g) p -> j (g p)", g=2), frow[32:64, :])\
                    .then_inc(s5_state_out, 16)
                sp.wait_ge(s5_fin, 2)
                for q, name in enumerate(("s5_re_s", "s5_im_s")):
                    rows = o_[name][0].rearrange("b (j g) p -> (b j) (g p)", g=2)
                    for e in range(2):
                        sp.dma_start(rows[e * P:(e + 1) * P, :], hrow[:, q, e, :]).then_inc(s5_state_out, 16)
                sp.wait_ge(s5_state_out, 16 * 6)

            def states():
                for h in range(HH):
                    sp.wait_ge(hg["state"], h + 1)
                    sp.dma_start(o_["hg_p"][0, 0, h], hS[:, NHC - 1, :]).then_inc(hg["state_out"], 16)
                for b in range(NS):
                    sp.wait_ge(hg["fill"], HG.at("O", HH - 2 if b < NS // 2 else HH - 1) + 1)
                    sp.dma_start(sS[:, b], i_["state_hgrn"][0, b].rearrange("h k v -> k h v")).then_inc(hg_s_in[b], 16)
                for b in range(NS):
                    sp.wait_ge(hg["s_state"], 2 * (b + 1))
                    sp.dma_start(o_["hg_s"][0, b].rearrange("h k v -> k h v"), sS[:, b]).then_inc(hg["s_out"], 16)
                sp.wait_ge(hg["s_out"], 16 * NS)

            def stream(n):
                def body(p, i, first, last):
                    for j in range(2):
                        column, src = weights(n, i, j)
                        if ST[n][0] == "glu" and not (first or last):
                            if j == 0:
                                sp.wait_ge(lo_ready, 2 * p)
                        else:
                            wait(sp, lo_ready, 2 * p + j - 1)
                        sp.dma_start(raw[:, j, 0:ST[n][3], :], src[:, :, bass.ds(column, P)])\
                            .then_inc(raw_arrived[j], 16)
                        if first and j == 0 and ST[n][0] == "glu":
                            s5_tables(sp)
                        if first and j == 1 and ST[n][:2] == ("ffn1_in0", 0) and s5_norm is not None:
                            s5_parameters()
                        if first and j == 0 and ST[n][0] == "xo":
                            caches(ST[n][1])
                        if first and j == 0 and ST[n][0] == "hg_out":
                            states()
                if ST[n][0] == "xq":
                    for i in range(ST[n][2]):
                        body(first_pair[ST[n][:2]] + i, i, i == 0, i == ST[n][2] - 1)
                        early_caches(ST[n][1], i)
                    return
                over_pairs(sp, n, body)

            for n in range(len(ST)):
                stream(n)
            for t in range(4):
                sp.wait_ge(y_evac, 2 * (t + 1))
                sp.dma_start(o_["y_prompt"][0, t * P:(t + 1) * P, :], yout[:, t, :]).then_inc(y_out, 16)
            sp.wait_ge(y_evac, 10)
            sp.dma_start(o_["y_sample"].rearrange("b o d -> (b o) d"), ysout[:]).then_inc(y_out, 16)
            sp.wait_ge(y_out, 16 * 5)
            sp.wait_ge(kv_out, 16 * 2 * DEPTH)
            if any(s_[0] == "hg_out" for s_ in ST):
                sp.wait_ge(hg["state_out"], 16 * HH)

        @block.gpsimd
        def _(pool):
            step = Chain(pool, pool_step)
            pool.memset(ones[:], 1.0).then_inc(consts_done, 1)
            pool.memset(eps[:], EPS).then_inc(consts_done, 1)
            step.link(pool.memset(ident[:], 0.0))
            pool.affine_select(out=ident[:], in_=ident[:], compare_op=ALU.not_equal, fill=1.0, base=0,
                               pattern=[[-1, P]], channel_multiplier=1).then_inc(consts_done, 1)
            pool.memset(zeros[:], 0.0).then_inc(consts_done, 1)
            step.link(pool.memset(vrows[:], 0.0))
            for name, row in (("ffn1_norm", V_FFN1), ("mix_norm", V_MIX), ("xattn_norm", V_XA), ("mem_norm", V_MEM),
                              ("ffn2_norm", V_FFN2), ("hg_lb_logits", V_LB)):
                pool.dma_start(vrows[row:row + 2 * KD, :], i_[name].rearrange("l (k p) -> (l k) p", p=P))\
                    .then_inc(vrows_loaded, 16)
            pool.dma_start(vrows[V_FIN:V_FIN + KD, :], i_["final_norm"].rearrange("(k p) -> k p", p=P))\
                .then_inc(vrows_loaded, 16)
            pool.dma_start(vrows[V_D:V_D + KD, :], i_["s5_d"][0].rearrange("(k g) c -> k (g c)", k=KD))\
                .then_inc(vrows_loaded, 16)
            pool.dma_start(vrows[V_HG:V_HG + 1, :], i_["hg_norm"]).then_inc(vrows_loaded, 16)

            pool.wait_ge(in_evac, 4)
            step.link(pool.tensor_tensor(m_acc[:], mT[:, 0, :], mT[:, 0, :], ALU.mult))
            for m in range(1, KD):
                step.link(pool.tensor_tensor(m_sq[:], mT[:, m, :], mT[:, m, :], ALU.mult))
                ins = pool.tensor_tensor(m_acc[:], m_acc[:], m_sq[:], ALU.add)
                if m < KD - 1:
                    step.link(ins)
                else:
                    ins.then_inc(mem_squares, 1)

            pool.wait_ge(consts_done, 4)
            for d in range(CS - 1):
                n = SC * (CS - 1 - d)
                pool.dma_start(s5_t[SC * d:SC * (d + 1), :, 0:n],
                               zeros[0:SC, 0:n].unsqueeze(1).to_broadcast([SC, SG, n]))\
                    .then_inc(s5_zeros_out, 16)
            pool.wait_ge(in_evac, 4 + KD + 1)
            step.link(pool.tensor_tensor(acc[:], xT[:, 0, :], xT[:, 0, :], ALU.mult))
            for m in range(1, KD):
                step.link(pool.tensor_tensor(sqt[:], xT[:, m, :], xT[:, m, :], ALU.mult))
                ins = pool.tensor_tensor(acc[:], acc[:], sqt[:], ALU.add)
                if m < KD - 1:
                    step.link(ins)
                else:
                    ins.then_inc(squares_done, 1)

            def squares(n, r):
                one = ST[n][0] == "glu"
                pool.wait_ge(sums_done, r)

                def body(p, i, first, last):
                    if not first and not last:
                        step.loop(i, 1, 2 if one else 4)
                    for j in range(1 if one else 2):
                        m = i if one else 2 * i + j
                        pool.wait_ge(used[1 if one else j], p + 1)
                        if first and j == 0:
                            step.link(pool.tensor_tensor(acc[:], xT[:, 0, :], xT[:, 0, :], ALU.mult))
                            continue
                        step.link(pool.tensor_tensor(sqt[:], tile(xT, m), tile(xT, m), ALU.mult))
                        ins = pool.tensor_tensor(acc[:], acc[:], sqt[:], ALU.add)
                        if last and j == (0 if one else 1):
                            ins.then_inc(squares_done, 1)
                        else:
                            step.link(ins)
                    if not first and not last:
                        step.done(ST[n][2] - 2)
                over_pairs(pool, n, body)

            def attend(layer):
                pool.wait_ge(chunk_done, 2 * first_pair["xq", layer] + 1)
                pool.memset(pZ[:], 0.0).then_inc(xa[layer]["zeros"], 1)

            def fused(out, in0, scalar, in1, op0, op1):
                step.link(pool.tensor_scalar(bTmp[:, 0:NJ], in0, scalar, None, op0))
                step.link(pool.tensor_tensor(out, bTmp[:, 0:NJ], in1, op1))

            def expm1(x, k, r, q, s2, out_e, out_x):
                link = step.link
                link(pool.tensor_scalar(x, x, -87.0, 88.0, ALU.max, ALU.min))
                link(pool.tensor_scalar(k, x, 1.0 / math.log(2.0), 12582912.0, ALU.mult, ALU.add))
                link(pool.tensor_scalar(k, k, 12582912.0, None, ALU.subtract))
                fused(r, k, -0.693359375, x, ALU.mult, ALU.add)
                fused(r, k, 2.12194440e-4, r, ALU.mult, ALU.add)
                link(pool.tensor_scalar(q, r, 1.0 / 40320, None, ALU.mult))
                for f in (5040, 720, 120, 24, 6, 2, 1):
                    fused(q, q, 1.0 / f, r, ALU.add, ALU.mult)
                link(pool.tensor_scalar(smi[:], k, 127.0, 8388608.0, ALU.add, ALU.mult))
                two_k = smi[:].bitcast(F32)
                link(pool.tensor_tensor(q, q, two_k, ALU.mult))
                if out_x is not None:
                    link(pool.tensor_tensor(out_x, q, two_k, ALU.add))
                if out_e is not None:
                    fused(out_e, two_k, -1.0, q, ALU.add, ALU.add)

            def s5_discretize():
                link = step.link
                pool.wait_ge(s5_rows, 48)
                pool.wait_ge(squares_done, 1)
                pool.tensor_copy(prow[64:96, :].rearrange("j (g p) -> j g p", g=2),
                                 ldrow[64:96, :].unsqueeze(2).to_broadcast([32, 2, 64])).then_inc(s5_small, 1)
                pool.wait_ge(s5_void["dve"], 1)
                ar, ai, ld = par[:, 0:32], par[:, 32:64], par[:, 64:96]
                v = [sm[:, q, :] for q in range(12)]
                expm1(ld, v[0], v[1], v[2], None, None, v[11])
                link(pool.tensor_tensor(v[0], ar, v[11], ALU.mult))
                link(pool.tensor_tensor(v[1], ai, v[11], ALU.mult))
                link(pool.tensor_tensor(v[6], ar, ar, ALU.mult))
                link(pool.tensor_tensor(ld, ai, ai, ALU.mult))
                pool.tensor_tensor(ld, ld, v[6], ALU.add).then_inc(s5_square, 1)
                link(pool.tensor_scalar(v[2], v[1], 1.0 / (2 * math.pi), 12582912.0, ALU.mult, ALU.add))
                link(pool.tensor_scalar(v[2], v[2], 12582912.0, None, ALU.subtract))
                c1 = 6.28125
                c2 = float(np.float32(round((2 * math.pi - c1) * 2 ** 20) / 2 ** 20))
                c3 = 2 * math.pi - c1 - c2
                for c in (c1, c2, c3):
                    fused(v[1], v[2], -c, v[1], ALU.mult, ALU.add)
                pool.tensor_scalar(v[3], v[1], -3.1415925, 3.1415925, ALU.max, ALU.min).then_inc(s5_phase, 1)
                expm1(v[0], v[2], v[6], v[7], None, v[8], v[9])
                pool.wait_ge(s5_sin, 2)
                link(pool.tensor_tensor(v[10], v[5], v[5], ALU.mult))
                link(pool.tensor_scalar(v[10], v[10], -2.0, None, ALU.mult))
                pool.memset(pw[:, 0, 0, :], 1.0)
                pool.memset(pw[:, 1, 0, :], 0.0)
                link(pool.tensor_scalar(v[2], v[10], 1.0, None, ALU.add))
                link(pool.tensor_tensor(pw[:, 0, 1, :], v[9], v[2], ALU.mult))
                link(pool.tensor_tensor(pw[:, 1, 1, :], v[9], v[4], ALU.mult))
                link(pool.tensor_tensor(v[8], v[8], v[2], ALU.mult))
                link(pool.tensor_tensor(v[8], v[8], v[10], ALU.add))
                pool.wait_ge(s5_inverse, 1)
                for out, a, b, op in ((v[6], v[8], pw[:, 1, 1, :], ALU.add), (v[7], pw[:, 1, 1, :], v[8], ALU.subtract)):
                    link(pool.tensor_tensor(v[1], a, ar, ALU.mult))
                    link(pool.tensor_tensor(v[2], b, ai, ALU.mult))
                    link(pool.tensor_tensor(v[1], v[1], v[2], op))
                    link(pool.tensor_tensor(out, v[1], ld, ALU.mult))

                powers(pool, link, pw)
                pool.wait_ge(s5_bc, 16 * 8)
                col = [v[q].unsqueeze(2).to_broadcast([P, NJ, SC]) for q in (6, 7)]
                times(pool, link, bBar[:, 0], bBar[:, 1], bRaw[:, 0], bRaw[:, 1], col[0], col[1],
                      bTmp[:].rearrange("p (j c) -> p j c", j=NJ))
                pool.nop().then_inc(s5_powers, 1)
                link(pool.memset(bZ[:], 0.0))
                for g in range(2):
                    rows = slice(64 * g, 64 * g + 64)
                    for e in range(2):
                        link(pool.tensor_copy(bZ[rows, e, :, g, :], bBar[rows, e]))
                pool.wait_ge(chunk_done, 2 * first_pair["ffn1_out1", 0])
                G = S5G
                G.all_emptied(pool, S5_EARLY)
                for j0 in range(0, NJ, NJ // 2):
                    table_part(pool, link, sF, CS, bBar, (0, 1), j0, j0 + NJ // 2, sTmp)
                pool.nop().then_inc(s5_tables_f, 1)

            def s5():
                pool.wait_ge(chunk_done, 2 * first_pair["glu", 0])
                for j0 in range(0, NJ // 2, NJ // 4):
                    table_part(pool, step.link, sG, CS + 1, cT, (0,), j0, j0 + NJ // 4, sGt[0])
                pool.nop().then_inc(s5_g0, 1)
                pool.wait_ge(s5_coef_kept, 1)
                pool.wait_ge(s5_fill, S5G.after("K"))
                pool.memset(sTabG[:], 0.0).then_inc(s5_tab_clear, 1)

            def hgrn():
                first = number("hg_out", 1)
                pool.wait_ge(chunk_done, 2 * first_pair[ST[first][:2]])
                pool.wait_ge(used[1], first_pair[ST[first][:2]])
                step.link(pool.memset(pair_mask[:], 0.0))
                for e in range(2):
                    pool.memset(attn[e][:], 0.0)
                step.link(pool.memset(chunk_start[:], 1.0))
                step.link(pool.memset(chunk_start[:].rearrange("p (n t) -> p n t", t=HC)[:, :, 0], 0.0))
                for u, level in enumerate(LEVELS):
                    m = pair_mask[:, u, :].rearrange("p (b t) -> p b t", t=2 * level)
                    step.link(pool.memset(m[:, :, level:], 1.0))
                    step.link(pool.affine_select(out=m, in_=m, compare_op=ALU.is_ge, fill=0.0, base=0,
                                                 pattern=[[-2 * level, P // (2 * level)], [0, 2 * level]],
                                                 channel_multiplier=1))
                    step.link(pool.affine_select(out=m, in_=m, compare_op=ALU.is_ge, fill=0.0, base=level - 1,
                                                 pattern=[[2 * level, P // (2 * level)], [0, 2 * level]],
                                                 channel_multiplier=-1))
                m = pair_mask[:, len(LEVELS), :].rearrange("p (b t) -> p b t", t=8)
                step.link(pool.memset(m, 1.0))
                step.link(pool.affine_select(out=m, in_=m, compare_op=ALU.is_ge, fill=0.0, base=0,
                                             pattern=[[-8, P // 8], [0, 8]], channel_multiplier=1))
                step.link(pool.affine_select(out=m, in_=m, compare_op=ALU.is_ge, fill=0.0, base=0,
                                             pattern=[[8, P // 8], [1, 8]], channel_multiplier=-1))
                step.link(pool.memset(one[:], 0.0))
                step.link(pool.memset(one[:, HH:HH + 1], 1.0))
                pool.nop().then_inc(hg["consts"], 1)
                for h in range(HH):
                    e = h % 2
                    for u, level in enumerate(LEVELS):
                        pool.wait_ge(hg["exps"], EXPS * h + 1 + u)
                        q, k, w = (t.rearrange("p (b a t) -> p b a t", a=2, t=level)
                                   for t in (hgQ[:, h, 0:SEQ], hgK[:, h, 0:SEQ], lvl[e][u][:]))
                        pool.tensor_tensor(w[:, :, 1], w[:, :, 1], q[:, :, 1], ALU.mult)
                        pool.tensor_tensor(w[:, :, 0], w[:, :, 0], k[:, :, 0], ALU.mult).then_inc(hg["scaled_pool"], 1)
                    pool.wait_ge(hg["exps"], EXPS * h + 2 + len(LEVELS))
                    pool.tensor_tensor(outK[e][:], outK[e][:], hgK[:, h, 0:SEQ], ALU.mult).then_inc(hg["scaled_pool"], 1)
                    pool.wait_ge(hg["exps"], EXPS * (h + 1))
                    pool.tensor_tensor(inQ[e][:], inQ[e][:], hgQ[:, h, 0:SEQ], ALU.mult).then_inc(hg["scaled_pool"], 1)

            for n in range(len(ST)):
                if ST[n][:2] == ("ffn1_in0", 0) and s5_norm is not None:
                    s5_discretize()
                if ST[n][0] == "glu":
                    s5()
                if ST[n][0] == "hg_out":
                    hgrn()
                if ST[n][0] == "xo":
                    attend(ST[n][1])
                if ST[n][:2] in norm_after:
                    squares(n, norm_after[ST[n][:2]])
                if ST[n][0] == "v":
                    layer = ST[n][1]
                    pool.wait_ge(kv_evac, 8 * layer + 4)
                    pool.dma_start(o_["mem_k"][layer, 0].rearrange("(t p) h d -> p t (h d)", p=P), kOut[:])\
                        .then_inc(kv_out, 16)
                    pool.wait_ge(kv_evac, 8 * layer + 8)
                    pool.dma_start(o_["mem_v"][layer, 0].rearrange("(t p) h d -> p t (h d)", p=P), vM[layer][:])\
                        .then_inc(kv_out, 16)

        @block.scalar
        def _(act):
            step = Chain(act, act_step)

            def split(p, j, kt):
                if kt is None:
                    return
                act.wait_ge(raw_arrived[j], 16 * (p + 1))
                wait(act, chunk_done, 2 * p + j - 1)
                act.activation(w_hi[:, j, 0:kt, :], raw[:, j, 0:kt, :], ACT.Copy).then_inc(hi_ready, 1)

            def root(r):
                act.wait_ge(sums_done, r + 1)
                act.activation(two(t1[:]), mis[:, 0:2, 0:HT], ACT.Sqrt, bias=eps[:, 0:1],
                               scale=1.0 / D).then_inc(root_done, 1)

            def gain_hi(m, row):
                act.activation(tile(a_hi, m), tile(xT, m), ACT.Copy,
                               scale=vec[:, bass.ds(row + m, 1)]).then_inc(a_hi_done, 1)

            act.wait_ge(consts_done, 4)
            act.wait_ge(vec_done, 1)
            act.wait_ge(in_evac, 4)
            split(0, 0, ST[0][3])

            def attend(layer):
                G, X = XAG[layer], xa[layer]
                for q, (what, a, owner) in enumerate(G.groups):
                    bank = xa_bank(q)
                    if what == "O":
                        h, e = a
                        act.wait_ge(X["fill"], q + 1)
                        if h:
                            G.emptied_of(act, "B", (2 * h + 1, 1))
                        act.activation(h_hi[:, 2 * h + e, 0:SEQ], bank, ACT.Copy).then_inc(X["o_hi"], 1)
                    if what == "V":
                        act.wait_ge(X["fill"], q + 1)
                        act.activation(h_hi[:, 0:KD, SEQ:NT], bank[:, 0:KD * NS].rearrange("p (k b) -> p k b", k=KD),
                                       ACT.Copy).then_inc(h_hi_done, KD)
                    if owner != "act":
                        continue
                    if what == "S":
                        h, e = a
                        act.wait_ge(X["max"], 2 * h + e + 1)
                        if h >= 2:
                            act.wait_ge(X["fill"], G.at("P", (h - 2, e)) + 1)
                        for t in range(2):
                            u = 2 * h + e
                            ins = act.activation(pP[:, u % 4, t, :], bank[:, t * NM:(t + 1) * NM], ACT.Exp,
                                                 bias=nmx[:, u, t:t + 1], scale=XA_SCALE, accum_out=den[:, u, t:t + 1])
                        ins.then_inc(X["void"]["act"], 1)
                    elif what == "P":
                        h, e = a
                        act.wait_ge(X["fill"], q + 1)
                        if h >= 2:
                            act.wait_ge(X["fill"], G.at("O", (h - 2, 1)) + 1)
                        act.activation(pT[:, h % 2, :, 256 * e:256 * e + 256],
                                       bank.rearrange("p (m t) -> p m t", m=2), ACT.Copy).then_inc(X["void"]["act"], 1)
                    elif what == "T":
                        act.wait_ge(X["s_max"], 1)
                        act.activation(pS[:], bank[0:NS * MH, 0:NM], ACT.Exp, bias=ssm[:, 1:2], scale=XA_SCALE,
                                       accum_out=ssm[:, 2:3]).then_inc(X["void"]["act"], 1)

            def s5_sines():
                act.wait_ge(s5_phase, 1)
                act.activation(sm[:, 4, :], sm[:, 3, :], ACT.Sin).then_inc(s5_sin, 1)
                act.activation(sm[:, 5, :], sm[:, 3, :], ACT.Sin, scale=0.5).then_inc(s5_sin, 1)

            def s5():
                G = S5G
                for q, (what, a, owner) in enumerate(G.groups):
                    if q == G.first("K"):
                        act.wait_ge(sums_done, s5_norm + 1)
                        act.activation(two(sqt[:]), mis[:, 0:2, 0:HT], ACT.Sqrt, bias=eps[:, 0:1],
                                       scale=1.0 / D).then_inc(root_done, 1)
                    if owner != "act":
                        continue
                    act.wait_ge(s5_fill, q + 1)
                    bank = bank_of(q)
                    if what == "F":
                        if a >= 2:
                            act.wait_ge(s5_f_out[a % 2], 16 * (a // 2))
                        dst, src = sFst[:, a % 2, :], bank
                    elif what == "K":
                        dst, src = sK[:, 4 * a:4 * a + 4, :], bank[0:2 * SC, :].rearrange("p (j n) -> p j n", j=4)
                    elif what == "X":
                        f, e = a
                        if f == 0 and e == 0:
                            act.wait_ge(s5_tab_out, 16 * 2)
                        if f == 4 and e == 0:
                            G.all_emptied(act, G.first("U") + 8)
                            act.wait_ge(s5_fill, G.first("U") + 8)
                        dst = sX[:, 8 * (f % 4):8 * (f % 4) + 8, 4 * (1 - e):4 * (1 - e) + 4, :]\
                            .rearrange("n g s c -> n s g c")
                        src = bank[0:UC, :].rearrange("n (s g c) -> n s g c", s=4, g=8)
                    elif what == "U":
                        dst, src = sU[:, 4 * a:4 * a + 4, :], bank[:, 0:4 * UC].rearrange("p (g n) -> p g n", g=4)
                    elif what == "FU":
                        dst = sFH[:, 2 * a:2 * a + 2, :, 1:]
                        src = bank[:, 0:4 * UC].rearrange("p (j e n) -> p j e n", j=2, e=2)
                    elif what == "Y":
                        if a == 0:
                            act.wait_ge(s5_fill, G.after("X"))
                        if a == 8:
                            act.wait_ge(s5_fill, G.first("y") + 8)
                        dst = sY[:, :, 64 * (a % 8):64 * (a % 8) + 64].rearrange("n t (g c) -> n t g c", g=4)
                        src = bank[0:YC, :].rearrange("n (g t c) -> n t g c", g=4, t=CS)
                    act.activation(dst, src, ACT.Copy).then_inc(s5_void["act"], 1)
                for k in range(KD):
                    act.wait_ge(s5_void["dve"], G.before(G.first("y") + (2 * k + 2 if k < 4 else 2 * k + 10), "dve"))
                    if k >= 2:
                        act.wait_ge(h_lo_done, hidden_before(number("glu")) + k - 1)
                    t = (t3, t4)[k % 2]
                    step.link(act.activation(t[:], u32[:, k, :], ACT.Gelu_apprx_tanh))
                    if k == 0:
                        act.wait_ge(s5_state_done, 1)
                    act.activation(h_hi[:, k, :], t[:], ACT.Copy).then_inc(h_hi_done, 1)

            def hgrn():
                G, x = HG, hidden_before(number("hg_out", 1))
                act.wait_ge(hg["lb_diff"], 1)
                act.activation(lbv[:, 2:4], lbv[:, 0:2], ACT.Exp).then_inc(hg["lb_exp"], 1)
                act.wait_ge(hg["lb"], 1)
                act.wait_ge(gated, 2 * HH)

                def decays(h):
                    e = h % 2
                    act.activation(hgK[:, h, :], hgK[:, h, :], ACT.Copy, scale=lbv[:, 5, h:h + 1])
                    if h >= 2:
                        act.wait_ge(hg["decay"], DECAYS * (h - 1))
                    act.activation(bC[e][:], hgF[:, h, 0:SEQ], ACT.Ln, bias=lbv[:, 4, h:h + 1],
                                   scale=lbv[:, 5, h:h + 1]).then_inc(hg["log"], 1)
                    act.wait_ge(hg["decay"], DECAYS * h + 1)
                    act.activation(ebt[e][:], bC[e][:].rearrange("p (n t) -> p n t", t=HC)[:, :, HC - 1], ACT.Exp)
                    for u in range(len(LEVELS)):
                        act.wait_ge(hg["decay"], DECAYS * h + 2 + u)
                        act.activation(lvl[e][u][:], lvl[e][u][:], ACT.Exp).then_inc(hg["exps"], 1)
                    act.wait_ge(hg["decay"], DECAYS * h + 2 + len(LEVELS))
                    act.activation(dgK[e][:], dgQ[e][:], ACT.Exp, scale=-1.0)
                    act.activation(dgQ[e][:], dgQ[e][:], ACT.Exp).then_inc(hg["exps"], 1)
                    act.wait_ge(hg["decay"], DECAYS * (h + 1))
                    act.activation(outK[e][:], outK[e][:], ACT.Exp).then_inc(hg["exps"], 1)

                def from_start(h):
                    if h >= 2:
                        act.wait_ge(hg["fill"], G.at("O", h - 2) + 1)
                    act.activation(inQ[h % 2][:], bC[h % 2][:], ACT.Exp).then_inc(hg["exps"], 1)

                def outputs(h):
                    q = G.at("O", h)
                    act.wait_ge(hg["fill"], q + 1)
                    act.activation(hgF[:, h, 0:SEQ], bank_of(q), ACT.Copy).then_inc(hg["void_act"], 1)

                decays(0)
                from_start(0)
                for h in range(HH):
                    if h + 1 < HH:
                        decays(h + 1)
                    if h:
                        outputs(h - 1)
                    for what, dst in (("V", vTok), ("K", kTok)):
                        q = G.at(what, h)
                        act.wait_ge(hg["fill"], q + 1)
                        act.activation(dst[:].rearrange("p a b -> p (a b)"), bank_of(q), ACT.Copy)\
                            .then_inc(hg["void_act"], 1)
                    if h + 1 < HH:
                        from_start(h + 1)
                outputs(HH - 1)
                for b in range(NS):
                    act.wait_ge(hg_s_in[b], 16)
                    for h in range(HH):
                        ins = act.activation(sS[:, b, h], sS[:, b, h], ACT.Copy, scale=fS[:, h, b:b + 1])
                    ins.then_inc(hg["s_decay"], 1)
                act.wait_ge(hg["void_dve"], G.before(G.after("S"), "dve"))
                for h in range(HH):
                    if h >= 2:
                        act.wait_ge(hg["squares_read"], h - 1)
                    act.activation((t1, t2)[h % 2][:], hgF[:, h, :], ACT.Square).then_inc(hg["squares"], 1)
                for e in range(2):
                    q = G.at("N", e)
                    act.wait_ge(hg["fill"], q + 1)
                    act.activation(t3[0:HH, e * HT:(e + 1) * HT], bank_of(q)[0:HH, 0:HT], ACT.Sqrt,
                                   bias=eps[0:HH, 0:1], scale=1.0 / P).then_inc(hg["void_act"], 1)
                for h in range(HH):
                    act.wait_ge(hg["normed"], h + 1)
                    if h == 0:
                        act.wait_ge(hg["s_state"], 2 * NS)
                    act.activation(h_hi[:, h, :], hgF[:, h, :], ACT.Copy).then_inc(h_hi_done, 1)

            def stream(n):
                name, layer, pairs, kt = ST[n]
                r, after, g0 = norm_of.get((name, layer)), gain_after.get((name, layer)), gate_base(n)
                if (name, layer) == ("ffn1_in0", 0):
                    act.wait_ge(kv_out, 16 * 2 * DEPTH)
                    act.wait_ge(kv_tr, 8 * DEPTH)
                if name == "k":
                    if layer:
                        act.wait_ge(chunk_done, 2 * first_pair["k", layer])
                    for m in range(KD):
                        g = V_MEM + KD * layer + m
                        act.activation(m_hi[:, m, :], mT[:, m, :], ACT.Copy, scale=vec[:, g:g + 1])\
                            .then_inc(m_hi_done, 1)

                def body(p, i, first, last):
                    for j in range(2):
                        split(p + j, 1 - j, tiles_of(n, p, j, last))
                        if j == 0 and first and r is not None:
                            root(r)
                        if j == 0 and first and n == 0:
                            act.wait_ge(mem_sums, 1)
                            act.activation(m_sq[:], mis[:, 2, 0:NM], ACT.Sqrt, bias=eps[:, 0:1], scale=1.0 / D)\
                                .then_inc(mem_root, 1)
                        if n == 1:
                            if first and j == 0:
                                act.wait_ge(in_evac, 4 + KD + 1)
                            gain_hi(2 * i + j, NORM_ROW[0])
                        if is_in(name) and j == 0:
                            act.wait_ge(used[0], p + 1)
                            act.activation(t2[:], t1[:], ACT.Silu).then_inc(gate_out, 1)
                        elif is_in(name):
                            act.wait_ge(used[1], p + 1)
                            act.activation(tile(h_hi, i), t3[:], ACT.Copy).then_inc(h_hi_done, 1)
                        if name == "glu" and j == 0:
                            act.wait_ge(chunk_done, 2 * p + 1)
                            if not first:
                                act.wait_ge(used[1], p)
                            act.activation(two(t2[:]), lslot(0), ACT.Sigmoid).then_inc(used[0], 1)
                        if name == "hg_qf" and j == 0:
                            act.wait_ge(used[0], p + 1)
                            act.activation(t2[:], tile(hgQ, i), ACT.Sigmoid).then_inc(gate_out, 1)
                        elif name == "hg_qf":
                            act.wait_ge(used[1], p + 1)
                            act.activation(tile(hgF, i), t3[:], ACT.Sigmoid)
                            act.activation(tile(hgK, i), t3[:], ACT.Sigmoid, scale=-1.0).then_inc(f_out, 1)
                        if name == "hg_vg" and j == 1:
                            act.wait_ge(used[1], p + 1)
                            act.activation(t2[:], tile(hgG, i), ACT.Sigmoid).then_inc(gate_out, 1)
                        if after is not None and is_out(name):
                            act.wait_ge(used[j], p + 1)
                            gain_hi(2 * i + j, NORM_ROW[after])
                        elif after is not None and j == 1:
                            act.wait_ge(used[1], p + 1)
                            gain_hi(i, NORM_ROW[after])
                over_pairs(act, n, body)

            for n in range(len(ST)):
                if ST[n][:2] == ("ffn1_in1", 0) and s5_norm is not None:
                    s5_sines()
                if ST[n][0] == "glu":
                    s5()
                if ST[n][0] == "hg_out":
                    hgrn()
                if ST[n][0] == "xo":
                    attend(ST[n][1])
                stream(n)
            root(NORMS - 1)

        @block.vector
        def _(dve):
            step = Chain(dve, dve_step)

            def split(p, j, kt):
                if kt is None:
                    return
                dve.wait_ge(hi_ready, 2 * p + j + 1)
                dve.tensor_tensor(w_lo[:, j, 0:kt, :], raw[:, j, 0:kt, :], w_hi[:, j, 0:kt, :].bitcast(F32),
                                  ALU.subtract).then_inc(lo_ready, 1)

            def gain_lo(m, r):
                dve.wait_ge(a_hi_done, KD * split_norms.index(r) + m + 1)
                dve.scalar_tensor_tensor(out=tile(a_lo, m), in0=tile(xT, m),
                                         scalar=vec[:, bass.ds(NORM_ROW[r] + m, 1)],
                                         in1=tile(a_hi, m).bitcast(F32), op0=ALU.mult,
                                         op1=ALU.subtract).then_inc(a_lo_done, 1)

            def reciprocal(r):
                dve.wait_ge(root_done, r + 1)
                step.link(dve.reciprocal(rstd[:], t1[:]))

            for q in range(4):
                dve.wait_ge(in_tr, q + 1)
                dve.tensor_copy(mT[:, 2 * q:2 * q + 2, :], mis[:, q, :].rearrange("p (k t) -> p k t", k=2))\
                    .then_inc(in_evac, 1)
            for k in range(KD):
                if k == 4:
                    dve.wait_ge(vec_tr, 1)
                    dve.tensor_copy(vec[:], lin[:, 0, 0, 0:NVEC]).then_inc(vec_done, 1)
                dve.wait_ge(in_tr, 4 + k + 1)
                dve.tensor_copy(xT[:, k, 0:SEQ], mis[:, k % 4, :]).then_inc(in_evac, 1)
            dve.wait_ge(in_tr, 4 + KD + 1)
            dve.tensor_copy(xT[:, :, SEQ:NT], mis[:, 0, 0:KD * NS].rearrange("p (k b) -> p k b", k=KD))\
                .then_inc(in_evac, 1)
            dve.wait_ge(vec_done, 1)
            split(0, 0, ST[0][3])

            def attend(layer):
                G, X, link = XAG[layer], xa[layer], step.link
                dve.wait_ge(used[1], first_pair["xo", layer])
                dve.memset(lin[0:NS, 1], 0.0).then_inc(X["clear"], 1)
                for q, (what, a, owner) in enumerate(G.groups):
                    bank = xa_bank(q)
                    if what == "B":
                        b, f = a
                        dve.wait_ge(X["fill"], q + 1)
                        for t in range(2):
                            v = 2 * b + t
                            dve.wait_ge(keys_in[K_SLOT[v]], arrivals(K_SLOT, v, layer))
                            for g in range(2):
                                c = 4 * b + 2 * f + g
                                k_ = kc[K_SLOT[v]][:, (2 * f + g) * NM:(2 * f + g + 1) * NM]
                                ins = dve.tensor_tensor_reduce(k_, k_, bank[:, g * NM:(g + 1) * NM], 1.0, 0.0,
                                                               ALU.mult, ALU.add, sT[:, t, c:c + 1])
                        ins.then_inc(X["void"]["dve"], 1)
                        continue
                    if what == "S":
                        h, e = a
                        u = 2 * h + e
                        dve.wait_ge(X["fill"], q + 1)
                        link(dve.tensor_reduce(mx[:, u, :], bank.rearrange("p (t m) -> p t m", t=2), AX.X, ALU.max))
                        dve.tensor_scalar(nmx[:, u, :], mx[:, u, :], -XA_SCALE, None, ALU.mult).then_inc(X["max"], 1)
                        dve.wait_ge(X["void"]["act"], G.before(q + 1, "act"))
                        link(dve.reciprocal(rden[:, u, :], den[:, u, :]))
                        for t in range(2):
                            ins = dve.tensor_scalar(pP[:, u % 4, t, :], pP[:, u % 4, t, :], rden[:, u, t:t + 1], None,
                                                    ALU.mult)
                        ins.then_inc(X["prob"], 1)
                    if what == "T":
                        dve.wait_ge(X["fill"], q + 1)
                        link(dve.tensor_reduce(ssm[:, 0:1], bank[0:NS * MH, 0:NM], AX.X, ALU.max))
                        dve.tensor_scalar(ssm[:, 1:2], ssm[:, 0:1], -XA_SCALE, None, ALU.mult).then_inc(X["s_max"], 1)
                        dve.wait_ge(X["void"]["act"], G.before(q + 1, "act"))
                        link(dve.reciprocal(ssm[:, 3:4], ssm[:, 2:3]))
                        dve.tensor_scalar(pS[:], pS[:], ssm[:, 3:4], None, ALU.mult).then_inc(X["s_prob"], 1)
                    if owner != "dve":
                        continue
                    if what == "V":
                        dve.wait_ge(X["pv"], NS)
                        dve.tensor_copy(oS[:].rearrange("b (a n) -> b a n", a=2), lin[0:NS, 1]).then_inc(X["rows"], 1)
                    dve.wait_ge(X["fill"], q + 1)
                    if what == "P":
                        h, e = a
                        if h >= 2:
                            dve.wait_ge(X["fill"], G.at("O", (h - 2, 1)) + 1)
                        dve.tensor_copy(pT[:, h % 2, :, 256 * e:256 * e + 256],
                                        bank.rearrange("p (m t) -> p m t", m=2)).then_inc(X["void"]["dve"], 1)
                    elif what == "O":
                        h, e = a
                        dve.wait_ge(X["o_hi"], 2 * h + e + 1)
                        dve.tensor_tensor(h_lo[:, 2 * h + e, 0:SEQ], bank, h_hi[:, 2 * h + e, 0:SEQ].bitcast(F32),
                                          ALU.subtract).then_inc(X["void"]["dve"], 1)
                    elif what == "W":
                        dve.wait_ge(X["zeros"], 1)
                        dve.tensor_copy(pZ[:].rearrange("p t h b c -> p t h (b c)")[:, :, :, ::NS + 1],
                                        bank[:, 0:2 * NS * MH].rearrange("p (t b h) -> p t h b", t=2, h=MH))\
                            .then_inc(X["void"]["dve"], 1)
                    elif what == "V":
                        dve.wait_ge(h_hi_done, hidden_before(number("xo", layer)) + KD)
                        dve.tensor_tensor(h_lo[:, 0:KD, SEQ:NT], bank[:, 0:KD * NS].rearrange("p (k b) -> p k b", k=KD),
                                          h_hi[:, 0:KD, SEQ:NT].bitcast(F32), ALU.subtract).then_inc(h_lo_done, KD)

            def s5_parameters(part):
                G = S5G
                if part == 0:
                    dve.wait_ge(s5_fill, 1)
                    dve.tensor_copy(par[:], bank_of(0)[:, 0:96]).then_inc(s5_void["dve"], 1)
                    return
                for q in range(1, S5_EARLY):
                    e, f = G.groups[q][1]
                    dve.wait_ge(s5_fill, q + 1)
                    for g in range(2):
                        rows = slice(64 * g, 64 * g + 64)
                        ins = dve.tensor_copy(cT[rows, e, 16 * f:16 * f + 16, :], bank_of(q)[rows, :]
                                              .rearrange("p (j g c) -> p j g c", g=2, c=SC)[:, :, g, :])
                    ins.then_inc(s5_void["dve"], 1)

            def s5():
                G, link = S5G, step.link
                dve.wait_ge(chunk_done, 2 * first_pair["glu", 0])
                dve.wait_ge(s5_powers, 1)
                for j0 in range(0, NJ, NJ // 4):
                    table_part(dve, link, sG, CS + 1, cT, (0, 2) if j0 >= NJ // 2 else (2,), j0, j0 + NJ // 4, sGt[1])
                dve.nop().then_inc(s5_tables_made, 1)
                for q, (what, a, owner) in enumerate(G.groups):
                    if q == G.first("K"):
                        dve.wait_ge(s5_g0, 1)
                        dve.wait_ge(root_done, s5_norm + 1)
                        link(dve.reciprocal(rstd[:], sqt[:]))
                        for e in range(2):
                            link(dve.tensor_copy(cw[:, e, 1, :], pw[:, e, CS, :]))
                            link(dve.tensor_copy(lam1[:, e, :], pw[:, e, 1, :]))
                        powers(dve, link, cw)
                        for e, m in enumerate((1, CB)):
                            link(dve.tensor_scalar(ncw[:, e, :], cw[:, 1, m, :], -1.0, None, ALU.mult))
                        dve.nop().then_inc(s5_coef_kept, 1)
                        for e in range(2):
                            dve.wait_ge(s5_f_out[e], 16 * NJ // 4)
                        for e in range(2):
                            link(dve.memset(sZ[:, e, :, NC:UC], 0.0))
                    if what == "X" and a[1] == 0:
                        f = a[0]
                        link(dve.scalar_tensor_tensor(
                            out=u32[:, f, :], in0=xT[:, f, :], in1=rstd[:], op0=ALU.mult, op1=ALU.mult,
                            scalar=vec[:, NORM_ROW[s5_norm] + f:NORM_ROW[s5_norm] + f + 1]))
                        if f >= 2:
                            dve.wait_ge(s5_fill, q - 2)
                        link(dve.tensor_copy(sZ[:, f % 2, :, 0:NC],
                                             u32[:, f, 0:SEQ].rearrange("p (n s) -> p s n", s=CS)))
                        dve.tensor_copy(sZ[:, f % 2, 0, NC:YC], u32[:, f, SEQ:NT])
                        dve.tensor_copy(sZ[:, f % 2, CS - 1, YC:UC], u32[:, f, SEQ:NT]).then_inc(s5_z, 1)
                    if (what, a) == ("U", 8):
                        scan(0)
                    if owner != "dve" or q < S5_EARLY:
                        continue
                    if what == "hfin":
                        scan(1)
                    dve.wait_ge(s5_fill, q + 1)
                    if what == "h0":
                        dve.wait_ge(s5_t_out, 16 * 2 * CS)
                    bank = bank_of(q)
                    if what == "y":
                        f, e = a
                        d = vec[:, V_D + f:V_D + f + 1]
                        if e == 0:
                            dve.scalar_tensor_tensor(out=u32[:, f, SEQ:NT], in0=u32[:, f, SEQ:NT], scalar=d,
                                                     in1=bank[:, NC:YC], op0=ALU.mult, op1=ALU.add)
                        seg = u32[:, f, 0:SEQ].rearrange("p (n s) -> p n s", s=CS)[:, :, 4 * e:4 * e + 4]
                        dve.scalar_tensor_tensor(
                            out=seg, in0=seg, scalar=d,
                            in1=bank[:, 0:4 * YC].rearrange("p (t n) -> p n t", t=4)[:, 0:NC, :],
                            op0=ALU.mult, op1=ALU.add).then_inc(s5_void["dve"], 1)
                        continue
                    if what == "K":
                        dst, src = sK[:, 4 * a:4 * a + 4, :], bank[0:2 * SC, :].rearrange("p (j n) -> p j n", j=4)
                    elif what == "h0":
                        dst, src = hs0[:], bank.rearrange("p (e b j) -> p e b j", e=2, b=NS)
                    elif what == "U":
                        dst, src = sU[:, 4 * a:4 * a + 4, :], bank[:, 0:4 * UC].rearrange("p (g n) -> p g n", g=4)
                    elif what == "FU":
                        dst = sFH[:, 2 * a:2 * a + 2, :, 1:]
                        src = bank[:, 0:4 * UC].rearrange("p (j e n) -> p j e n", j=2, e=2)
                    elif what == "hfin":
                        dst, src = frow[:], bank[0:64, 0:P]
                    elif what == "hs1":
                        dst, src = hrow[:].rearrange("p e f n -> p (e f n)"), bank
                    elif what == "Y":
                        if a == 9:
                            dve.wait_ge(s5_fill, G.first("y") + 8)
                        dst = sY[:, :, 64 * (a % 8):64 * (a % 8) + 64].rearrange("n t (g c) -> n t g c", g=4)
                        src = bank[0:YC, :].rearrange("n (g t c) -> n t g c", g=4, t=CS)
                    dve.tensor_copy(dst, src).then_inc(s5_void["dve"], 1)
                    if what == "hfin" or what == "hs1":
                        dve.wait_ge(s5_void["dve"], G.before(q + 1, "dve"))
                        dve.nop().then_inc(s5_fin, 1)
                h0 = hidden_before(number("glu"))
                dve.wait_ge(s5_state_out, 16 * 6)
                dve.nop().then_inc(s5_state_done, 1)
                for k in range(KD):
                    dve.wait_ge(h_hi_done, h0 + k + 1)
                    dve.tensor_tensor(h_lo[:, k, :], (t3, t4)[k % 2][:], h_hi[:, k, :].bitcast(F32), ALU.subtract)\
                        .then_inc(h_lo_done, 1)

            def scan(half):
                G, link = S5G, step.link
                blocks, nj = NC // CB, NJ // 2
                if half == 0:
                    G.all_emptied(dve, G.at("h0", 0) + 1)
                    link(dve.memset(sFH[:, :, :, 0], 0.0))
                else:
                    G.all_emptied(dve, G.after("FU"))
                j_ = slice(half * nj, (half + 1) * nj)
                H = sFH[:, j_, :, 1:NC + 1].rearrange("p j e (b m) -> p j e b m", m=CB)

                def step_on(out, x, m):
                    n = x.shape[3]
                    a, b = (t[:, 0:nj * 2 * n].rearrange("p (j e n) -> p j e n", e=2, n=n) for t in sc)
                    re, im = (cw[:, e, m, j_].unsqueeze(2) for e in range(2))
                    dve.tensor_tensor(a, re.unsqueeze(3).to_broadcast([P, nj, 2, n]), x, ALU.mult)
                    dve.tensor_tensor(b[:, :, 0], ncw[:, m // CB, j_].unsqueeze(2).to_broadcast([P, nj, n]),
                                      x[:, :, 1], ALU.mult)
                    link(dve.tensor_tensor(b[:, :, 1], im.to_broadcast([P, nj, n]), x[:, :, 0], ALU.mult))
                    link(dve.tensor_tensor(out, out, a, ALU.add))
                    link(dve.tensor_tensor(out, out, b, ALU.add))

                for m in range(1, CB):
                    step_on(H[:, :, :, :, m], H[:, :, :, :, m - 1], 1)
                for b in range(1, blocks):
                    step_on(H[:, :, :, b:b + 1, CB - 1], H[:, :, :, b - 1:b, CB - 1], CB)

                def add_product(out, x, fac, shape):
                    tmp = [t[:, 0:int(np.prod(shape))].rearrange("p (j b m) -> p j b m", j=nj, b=shape[1]) for t in sc]
                    for f, (a, b) in enumerate((((0, 0), (1, 1)), ((0, 1), (1, 0)))):
                        dve.tensor_tensor(tmp[0], fac[a[0]], x[a[1]], ALU.mult)
                        link(dve.tensor_tensor(tmp[1], fac[b[0]], x[b[1]], ALU.mult))
                        link(dve.tensor_tensor(out[f], out[f], tmp[0], ALU.add))
                        link(dve.tensor_tensor(out[f], out[f], tmp[1], ALU.add if f else ALU.subtract))

                shape = [P, nj, blocks - 1, CB - 1]
                add_product([H[:, :, e, 1:, 0:CB - 1] for e in range(2)],
                            [H[:, :, e, 0:blocks - 1, CB - 1:CB].to_broadcast(shape) for e in range(2)],
                            [cw[:, e, 1:CB, j_].rearrange("p m j -> p j m").unsqueeze(2).to_broadcast(shape)
                             for e in range(2)], tuple(shape[1:]))
                link(dve.tensor_copy(hfin[:, :, j_], sFH[:, j_, :, NC].rearrange("p j e -> p e j")))

                def lam(e):
                    return lam1[:, e, j_].unsqueeze(1).to_broadcast([P, NS, nj])
                for e in range(2):
                    link(dve.tensor_tensor(hs1[:, e, :, j_], hs0[:, e, :, j_], lam(0), ALU.mult))
                    link(dve.tensor_tensor(hst[:, e, :, j_], hs0[:, 1 - e, :, j_], lam(1), ALU.mult))
                    link(dve.tensor_tensor(hs1[:, e, :, j_], hs1[:, e, :, j_], hst[:, e, :, j_],
                                           ALU.add if e else ALU.subtract))
                    link(dve.tensor_tensor(hs1[:, e, :, j_], hs1[:, e, :, j_],
                                           sFH[:, j_, e, 1 + YC:1 + UC].rearrange("p j b -> p b j"), ALU.add))
                    link(dve.tensor_copy(sFH[:, j_, e, NC:YC], hs0[:, e, :, j_].rearrange("p b j -> p j b")))
                dve.nop().then_inc(s5_scanned, 1)

            def hgrn():
                G, link, x = HG, step.link, hidden_before(number("hg_out", 1))
                l0, l1 = vec[:, V_LB:V_LB + HH], vec[:, V_LB + HH:V_LB + 2 * HH]
                link(dve.tensor_tensor(lbv[:, 4], l0, l1, ALU.max))
                link(dve.tensor_tensor(lbv[:, 0], l0, lbv[:, 4], ALU.subtract))
                dve.tensor_tensor(lbv[:, 1], l1, lbv[:, 4], ALU.subtract).then_inc(hg["lb_diff"], 1)
                dve.wait_ge(hg["lb_exp"], 1)
                link(dve.tensor_tensor(lbv[:, 4], lbv[:, 2], lbv[:, 3], ALU.add))
                link(dve.reciprocal(lbv[:, 4], lbv[:, 4]))
                link(dve.tensor_tensor(lbv[:, 5], lbv[:, 2], lbv[:, 4], ALU.mult))
                link(dve.tensor_tensor(lbv[:, 4], lbv[:, 3], lbv[:, 4], ALU.mult))
                dve.nop().then_inc(hg["lb"], 1)
                link(dve.tensor_tensor(fS[:], hgF[:, :, SEQ:NT],
                                       lbv[:, 5].unsqueeze(2).to_broadcast([P, HH, NS]), ALU.mult))
                link(dve.tensor_tensor(fS[:], fS[:], lbv[:, 4].unsqueeze(2).to_broadcast([P, HH, NS]), ALU.add))
                dve.wait_ge(hg["consts"], 1)

                def decays(h):
                    e = h % 2
                    b = bC[e][:]
                    dve.wait_ge(hg["log"], h + 1)
                    link(dve.tensor_scalar(b, b, -20.0, None, ALU.max))
                    if h >= 2:
                        dve.wait_ge(hg["fill"], G.at("K", h - 2) + 1)
                    link(dve.tensor_tensor_scan(b, chunk_start[:], b, 0.0, ALU.mult, ALU.add))
                    dve.nop().then_inc(hg["decay"], 1)
                    for u, level in enumerate(LEVELS):
                        c, w = (t.rearrange("p (b a t) -> p b a t", a=2, t=level) for t in (b, lvl[e][u][:]))
                        edge = c[:, :, 0, level - 1:level].to_broadcast([P, SEQ // (2 * level), level])
                        dve.tensor_tensor(w[:, :, 1], c[:, :, 1], edge, ALU.subtract)
                        dve.tensor_tensor(w[:, :, 0], edge, c[:, :, 0], ALU.subtract).then_inc(hg["decay"], 1)
                    c, w = (t.rearrange("p (b t) -> p b t", t=8) for t in (b, dgQ[e][:]))
                    dve.tensor_tensor(w, c, c[:, :, 3:4].to_broadcast([P, SEQ // 8, 8]), ALU.subtract)\
                        .then_inc(hg["decay"], 1)
                    c, w = (t.rearrange("p (b t) -> p b t", t=HC) for t in (b, outK[e][:]))
                    dve.tensor_tensor(w, c[:, :, HC - 1:HC].to_broadcast([P, NHC, HC]), c, ALU.subtract)\
                        .then_inc(hg["decay"], 1)

                def scaled(h):
                    e = h % 2
                    dve.wait_ge(hg["exps"], EXPS * h + 1 + len(LEVELS))
                    dve.tensor_tensor(dgQ[e][:], dgQ[e][:], hgQ[:, h, 0:SEQ], ALU.mult)
                    dve.tensor_tensor(dgK[e][:], dgK[e][:], hgK[:, h, 0:SEQ], ALU.mult).then_inc(hg["scaled_dve"], 1)

                decays(0)
                scaled(0)
                for h in range(HH):
                    e = h % 2
                    if h + 1 < HH:
                        decays(h + 1)
                    if h >= 2:
                        dve.wait_ge(hg["fill"], G.at("O", h - 2) + 1)
                    for u in range(len(LEVELS) + 1):
                        q = G.at("A", (h, u))
                        dve.wait_ge(hg["fill"], q + 1)
                        if u:
                            dve.wait_ge(hg["void_dve"], G.before(q, "dve"))
                        dve.copy_predicated(attn[e][:], pair_mask[:, u:u + 1, :].bitcast(I32).to_broadcast([P, 4, P]),
                                            bank_of(q).rearrange("p (a t) -> p a t", a=4)).then_inc(hg["void_dve"], 1)
                    if h + 1 < HH:
                        scaled(h + 1)
                    dve.wait_ge(hg["fill"], G.at("D", (h, 1)) + 1)
                    dve.wait_ge(hg["void_act"], G.before(G.at("V", h), "act"))
                    for n in range(NHC):
                        add = bank_of(G.at("D", (h, n % 2)))[:, (n // 2) * P:(n // 2 + 1) * P]
                        if n == 0:
                            link(dve.tensor_copy(hS[:, 0], add))
                            continue
                        if n == NHC - 1 and h:
                            dve.wait_ge(hg["state_out"], 16 * h)
                        link(dve.scalar_tensor_tensor(out=hS[:, n], in0=hS[:, n - 1], scalar=ebt[e][:, n:n + 1], in1=add,
                                                      op0=ALU.mult, op1=ALU.add))
                    dve.nop().then_inc(hg["state"], 1)
                    dve.nop().then_inc(hg["void_dve"], 2)
                for b in range(NS):
                    dve.wait_ge(hg["s_decay"], b + 1)
                    for f in range(2):
                        q = G.at("B", (b, f))
                        dve.wait_ge(hg["fill"], q + 1)
                        for u in range(4):
                            h = 4 * f + u
                            ins = dve.scalar_tensor_tensor(out=sS[:, b, h], in0=bank_of(q)[:, u * P:(u + 1) * P],
                                                           scalar=hgK[:, h, SEQ + b:SEQ + b + 1], in1=sS[:, b, h],
                                                           op0=ALU.mult, op1=ALU.add)
                        link(ins)
                        dve.nop().then_inc(hg["void_dve"], 1)
                        dve.nop().then_inc(hg["s_state"], 1)
                q = G.at("S", 0)
                dve.wait_ge(hg["fill"], q + 1)
                dve.tensor_copy(hgF[:, :, SEQ:NT], bank_of(q)[:, 0:HH * NS].rearrange("p (h b) -> p h b", h=HH))\
                    .then_inc(hg["void_dve"], 1)
                def low(h):
                    dve.wait_ge(h_hi_done, x + h + 1)
                    dve.tensor_tensor(h_lo[:, h, :], hgF[:, h, :], h_hi[:, h, :].bitcast(F32), ALU.subtract)\
                        .then_inc(h_lo_done, 1)

                for h in range(HH):
                    dve.wait_ge(hg["squares"], h + 1)
                    link(dve.scalar_tensor_tensor(out=hgF[:, h, :], in0=hgG[:, h, :], scalar=vec[:, V_HG:V_HG + 1],
                                                  in1=hgF[:, h, :], op0=ALU.mult, op1=ALU.mult))
                dve.wait_ge(hg["void_act"], G.before(G.at("N", 1) + 1, "act"))
                dve.reciprocal(t3[0:HH, :], t3[0:HH, :]).then_inc(hg["inverse"], 1)
                for h in range(HH):
                    for e in range(2):
                        q = G.at("R", (h, e))
                        dve.wait_ge(hg["fill"], q + 1)
                        o = hgF[:, h, e * HT:(e + 1) * HT]
                        dve.tensor_tensor(o, o, bank_of(q)[:, 0:HT], ALU.mult).then_inc(hg["void_dve"], 1)
                    dve.wait_ge(hg["void_dve"], G.before(q + 1, "dve"))
                    dve.nop().then_inc(hg["normed"], 1)
                    if h:
                        low(h - 1)
                low(HH - 1)

            def evac_kv(layer, which):
                dst = kOut if which == 0 else vM[layer]
                if which == 0 and layer:
                    dve.wait_ge(kv_out, 16 * 2 * layer)
                for t in range(2):
                    for half in range(2):
                        q = 8 * layer + 4 * which + 2 * t + half
                        dve.wait_ge(kv_tr, q + 1)
                        dve.tensor_copy(dst[:, t, half * 512:(half + 1) * 512], mis[:, 2 + q % 2, :])\
                            .then_inc(kv_evac, 1)

            def stream(n):
                name, layer, pairs, kt = ST[n]
                r, after, g0 = norm_of.get((name, layer)), gain_after.get((name, layer)), gate_base(n)
                h0 = hidden_before(n)
                if name == "k":
                    for m in range(KD):
                        g = V_MEM + KD * layer + m
                        dve.wait_ge(m_hi_done, KD * layer + m + 1)
                        dve.scalar_tensor_tensor(out=m_lo[:, m, :], in0=mT[:, m, :], scalar=vec[:, g:g + 1],
                                                 in1=m_hi[:, m, :].bitcast(F32), op0=ALU.mult,
                                                 op1=ALU.subtract).then_inc(m_lo_done, 1)

                def hidden_lo(i):
                    dve.wait_ge(h_hi_done, h0 + i + 1)
                    dve.tensor_tensor(tile(h_lo, i), t3[:], tile(h_hi, i).bitcast(F32), ALU.subtract)\
                        .then_inc(h_lo_done, 1)

                def gate(i):
                    dve.wait_ge(gate_out, g0 + i + 1)
                    dve.tensor_tensor(tile(hgG, i), tile(hgG, i), t2[:], ALU.mult).then_inc(gated, 1)

                def body(p, i, first, last):
                    inner = not first and not last
                    if inner:
                        step.loop(i, 1, 1 if is_in(name) or name == "glu" else 0)
                    for j in range(2):
                        split(p + j, 1 - j, tiles_of(n, p, j, last))
                        if j == 0 and first and r is not None:
                            reciprocal(r)
                        if j == 0 and first and n == 0:
                            dve.wait_ge(mem_root, 1)
                            dve.reciprocal(m_rstd[:], m_sq[:]).then_inc(mem_rstd, 1)
                            dve.wait_ge(mem_rstd, 1)
                        if n == 1:
                            gain_lo(2 * i + j, 0)
                        if name == "glu" and j == 0:
                            continue
                        dve.wait_ge(chunk_done, 2 * p + j + 1)
                        m = 2 * i + j
                        if name in ("k", "v"):
                            dst = kT[layer] if name == "k" else vT
                            dve.tensor_tensor(tile(dst, m), lslot(j, NM), m_rstd[:], ALU.mult).then_inc(used[j], 1)
                        elif is_in(name) and j == 0:
                            wait(dve, gate_out, g0 + i)
                            dve.tensor_tensor(two(t1[:]), lslot(0), two(rstd[:]), ALU.mult).then_inc(used[0], 1)
                            if not first:
                                hidden_lo(i - 1)
                        elif is_in(name):
                            step.link(dve.tensor_tensor(two(t4[:]), lslot(1), two(rstd[:]), ALU.mult))
                            dve.wait_ge(gate_out, g0 + i + 1)
                            dve.tensor_tensor(t3[:], t4[:], t2[:], ALU.mult).then_inc(used[1], 1)
                            if last:
                                hidden_lo(i)
                        elif name == "glu":
                            dve.wait_ge(used[0], p + 1)
                            step.link(dve.tensor_tensor(two(t3[:]), lslot(1), two(t2[:]), ALU.mult))
                            dve.tensor_tensor(tile(xT, i), tile(xT, i), t3[:], ALU.add).then_inc(used[1], 1)
                            if not first and after is not None:
                                gain_lo(i - 1, after)
                            if last and after is not None:
                                gain_lo(i, after)
                        elif name == "xq":
                            dve.tensor_tensor(twotile(qT, m), lslot(j), two(rstd[:]), ALU.mult).then_inc(used[j], 1)
                        elif name == "hg_qf" and j == 0:
                            dve.tensor_tensor(twotile(hgQ, i), lslot(0), two(rstd[:]), ALU.mult).then_inc(used[0], 1)
                        elif name == "hg_qf":
                            wait(dve, f_out, i)
                            dve.tensor_tensor(two(t3[:]), lslot(1), two(rstd[:]), ALU.mult).then_inc(used[1], 1)
                            dve.wait_ge(gate_out, g0 + i + 1)
                            dve.tensor_tensor(tile(hgQ, i), tile(hgQ, i), t2[:], ALU.mult).then_inc(gated, 1)
                        elif name == "hg_vg" and j == 0:
                            if not first:
                                gate(i - 1)
                            dve.tensor_tensor(twotile(hgV, i), lslot(0), two(rstd[:]), ALU.mult).then_inc(used[0], 1)
                        elif name == "hg_vg":
                            dve.tensor_tensor(twotile(hgG, i), lslot(1), two(rstd[:]), ALU.mult).then_inc(used[1], 1)
                            if last:
                                gate(i)
                        else:
                            scale = 0.5 if name[:3] == "ffn" else 1.0
                            dve.scalar_tensor_tensor(out=twotile(xT, m), in0=lslot(j), scalar=scale,
                                                     in1=twotile(xT, m), op0=ALU.mult, op1=ALU.add)\
                                .then_inc(used[j], 1)
                            if after is not None:
                                if not (first and j == 0):
                                    gain_lo(m - 1, after)
                                if last and j == 1:
                                    gain_lo(m, after)
                    if inner:
                        step.done(pairs - 2)
                over_pairs(dve, n, body)
                if name in ("k", "v"):
                    evac_kv(layer, 0 if name == "k" else 1)

            for n in range(len(ST)):
                if ST[n][:2] == ("ffn1_out0", 0) and s5_norm is not None:
                    s5_parameters(0)
                if ST[n][:2] == ("ffn1_in1", 0) and s5_norm is not None:
                    dve.wait_ge(s5_square, 1)
                    dve.reciprocal(par[:, 64:96], par[:, 64:96]).then_inc(s5_inverse, 1)
                if ST[n][:2] == ("ffn1_out1", 0) and s5_norm is not None:
                    s5_parameters(1)
                if ST[n][0] == "glu":
                    s5()
                if ST[n][0] == "hg_out":
                    hgrn()
                if ST[n][0] == "xo":
                    attend(ST[n][1])
                stream(n)
            reciprocal(NORMS - 1)
            for m in range(KD):
                dve.scalar_tensor_tensor(out=yT[:, m, :], in0=xT[:, m, :], scalar=vec[:, V_FIN + m:V_FIN + m + 1],
                                         in1=rstd[:], op0=ALU.mult, op1=ALU.mult).then_inc(y_normed, 1)
            for q in range(10):
                t, half = q // 2, q % 2
                dve.wait_ge(y_tr, q + 1)
                dst = yout[:, t, half * 512:(half + 1) * 512] if t < 4 else ysout[:, half * 512:(half + 1) * 512]
                dve.tensor_copy(dst, mis[0:P if t < 4 else NS, 2 + q % 2, :]).then_inc(y_evac, 1)

        @block.tensor
        def _(pe):
            pe.wait_ge(consts_done, 4)
            pe.wait_ge(mem_loaded, 16)
            for q in range(4):
                for u in range(4):
                    k, t = 2 * q + u // 2, u % 2
                    ins = pe.transpose(mis[:, q, u * P:(u + 1) * P], min_[:, t, k * P:(k + 1) * P], ident[:])
                ins.then_inc(in_tr, 1)
            pe.wait_ge(loaded, 32)
            for k in range(KD):
                if k == 4:
                    pe.wait_ge(vrows_loaded, 16 * 9)
                    pe.transpose(lin[:, 0, 0, 0:P], vrows[:], ident[:]).then_inc(vec_tr, 1)
                pe.wait_ge(in_evac, k + 1)
                for t in range(4):
                    ins = pe.transpose(mis[:, k % 4, t * P:(t + 1) * P], xin[:, t, k * P:(k + 1) * P], ident[:])
                ins.then_inc(in_tr, 1)
            pe.wait_ge(in_evac, 4 + KD - 3)
            for k in range(KD):
                ins = pe.transpose(mis[:, 0, k * NS:(k + 1) * NS], xsin[:, k * P:(k + 1) * P], ident[0:NS, 0:NS])
            ins.then_inc(in_tr, 1)
            pe.wait_ge(vec_done, 1)

            def memory_sums():
                pe.wait_ge(mem_squares, 1)
                pe.wait_ge(in_evac, 4 + KD - 1)
                pe.matmul(mis[:, 2, 0:NM], ones[:], m_acc[:], start=True, stop=True).then_inc(mem_sums, 1)

            def sums(r):
                pe.wait_ge(squares_done, r + 1)
                for half in range(2):
                    ins = pe.matmul(mis[:, half, 0:HT], ones[:], acc[:, half * HT:(half + 1) * HT],
                                    start=True, stop=True)
                ins.then_inc(sums_done, 1)

            def attend(layer):
                G, X = XAG[layer], xa[layer]
                for j in range(2):
                    pe.wait_ge(used[j], first_pair["xo", layer])
                for q, (what, a, owner) in enumerate(G.groups):
                    bank = xa_bank(q)
                    if q == 0:
                        pe.wait_ge(root_done, norm_of["xq", layer] + 1)
                    G.reuse(pe, q)
                    if what == "B":
                        b, f = a
                        for u in range(4):
                            ins = pe.matmul(bank[:, u * P:(u + 1) * P],
                                            qT[:, 4 * f + u, SEQ + b:SEQ + b + 1].to_broadcast([P, P]), ident[:],
                                            start=True, stop=True)
                    elif what == "S":
                        h, e = a
                        for t in range(2):
                            c = (2 * e + t) * P
                            for k in range(2):
                                ins = pe.matmul(bank[:, t * NM:(t + 1) * NM], qT[:, 2 * h + k, c:c + P],
                                                kT[layer][:, 2 * h + k, :], start=k == 0, stop=k == 1)
                    elif what == "P":
                        h, e = a
                        u = 2 * h + e
                        pe.wait_ge(X["prob"], u + 1)
                        for m in range(2):
                            for t in range(2):
                                ins = pe.transpose(bank[:, (2 * m + t) * P:(2 * m + t + 1) * P],
                                                   pP[:, u % 4, t, m * P:(m + 1) * P], ident[:])
                    elif what == "O":
                        h, e = a
                        if e == 0:
                            G.all_emptied(pe, G.at("P", (h, 1)) + 1)
                        for m in range(2):
                            ins = pe.matmul(bank, vM[layer][:, m, (2 * h + e) * P:(2 * h + e + 1) * P],
                                            pT[:, h % 2, m, :], start=m == 0, stop=m == 1)
                    elif what == "T":
                        G.emptied_of(pe, "B", (NS - 1, 1))
                        for t in range(2):
                            ins = pe.transpose(bank[0:NS * MH, t * P:(t + 1) * P], sT[:, t, :], ident[:])
                    elif what == "W":
                        pe.wait_ge(X["s_prob"], 1)
                        for t in range(2):
                            ins = pe.transpose(bank[:, t * NS * MH:(t + 1) * NS * MH], pS[:, t * P:(t + 1) * P],
                                               ident[0:NS * MH, 0:NS * MH])
                    else:
                        G.emptied_of(pe, "W", 0)
                        pe.wait_ge(X["clear"], 1)
                        for b in range(NS):
                            pe.wait_ge(values_in[V_SLOT[b]], arrivals(V_SLOT, b, layer))
                            for h in range(MH):
                                for t in range(2):
                                    ins = pe.matmul(lin[0:NS, 1, h // 2, h % 2 * NM:(h % 2 + 1) * NM],
                                                    pZ[:, t, h, b, :], vc[V_SLOT[b]][:, t, h * NM:(h + 1) * NM],
                                                    start=False, stop=b == NS - 1 and t == 1,
                                                    skip_group_check=True)
                            ins.then_inc(X["pv"], 1)
                        pe.wait_ge(X["rows"], 1)
                        for k in range(KD):
                            ins = pe.transpose(bank[:, k * NS:(k + 1) * NS], oS[:, k * P:(k + 1) * P], ident[0:NS, 0:NS])
                    ins.then_inc(X["fill"], 1)
                G.all_emptied(pe, len(G.groups) - 1)

            def s5(first, end):
                G = S5G
                if first == 0:
                    pe.wait_ge(root_done, 1)
                if first:
                    for j in range(2):
                        pe.wait_ge(used[j], first_pair["ffn1_out1" if first == 1 else "glu", 0])
                for q, (what, a, owner) in list(enumerate(G.groups))[first:end]:
                    if q == G.first("K"):
                        G.all_emptied(pe, q)
                        sums(s5_norm)
                        pe.wait_ge(root_done, s5_norm + 1)
                    if what == "h0":
                        pe.wait_ge(s5_state_in, 64)
                    G.reuse(pe, q)
                    bank = bank_of(q)
                    if what == "par":
                        pe.wait_ge(s5_small, 1)
                        ins = pe.transpose(bank[:, 0:96], prow[:], ident[0:96, 0:96])
                    elif what == "c":
                        pe.wait_ge(s5_bc, 16 * 8)
                        e, f = a
                        for b in range(4):
                            ins = pe.transpose(bank[:, b * P:(b + 1) * P], cRaw[:, e, 4 * f + b, :], ident[:])
                    elif what == "F":
                        pe.wait_ge(s5_tables_f, 1)
                        for u in range(4):
                            j, e = 2 * a + u // 2, u % 2
                            ins = pe.transpose(bank[:, u * P:(u + 1) * P],
                                               sF[:, e, j].rearrange("p d c -> p (d c)"), ident[:])
                    elif what == "K":
                        if a == 0:
                            pe.wait_ge(s5_tables_made, 1)
                            pe.wait_ge(s5_g0, 1)
                        for u in range(4):
                            j = 4 * a + u
                            for e in range(2):
                                ins = pe.matmul(bank[0:2 * SC, u * P:(u + 1) * P],
                                                bZ[:, e, j, :, :].rearrange("p g c -> p (g c)"),
                                                sG[:, e, j, 0:CS, :], start=e == 0, stop=e == 1)
                    elif what == "h0":
                        for e in range(2):
                            for f in range(2):
                                ins = pe.transpose(bank[:, (2 * e + f) * P:(2 * e + f + 1) * P], hrow[:, e, f, :],
                                                   ident[:])
                    elif what == "X":
                        f, e = a
                        pe.wait_ge(s5_z, f + 1)
                        for u in range(4):
                            step_ = 4 * e + 3 - u
                            ins = pe.transpose(bank[0:UC, u * P:(u + 1) * P], sZ[:, f % 2, step_, :], ident[:])
                    elif what == "U":
                        if a % 8 == 0:
                            G.all_emptied(pe, q)
                        for u in range(4):
                            g = (4 * a + u) % 32
                            ins = pe.transpose(bank[:, u * UC:(u + 1) * UC],
                                               sX[:, g, :, :].rearrange("n s c -> n (s c)"),
                                               ident[0:UC, 0:UC])
                    elif what == "FU":
                        if a % 8 == 0:
                            G.all_emptied(pe, q)
                        pe.wait_ge(s5_tabf_in[a % 2], 16 * (a // 2 + 1))
                        for u in range(4):
                            j, e = 2 * a + u // 2, u % 2
                            for g in range(2):
                                c = (u // 2) * 256 + e * P + 64 * g
                                ins = pe.matmul(bank[64 * g:64 * g + 64, u * UC:(u + 1) * UC],
                                                sTabF[:, a % 2, c:c + 64], sU[:, 2 * j + g, :], start=True, stop=True)
                    elif what == "hfin":
                        pe.wait_ge(s5_scanned, 2)
                        ins = pe.transpose(bank[0:64, 0:P], hfin[:].rearrange("p e j -> p (e j)"), ident[:])
                    elif what == "hs1":
                        for e in range(2):
                            for f in range(2):
                                ins = pe.transpose(bank[:, (2 * e + f) * P:(2 * e + f + 1) * P],
                                                   hs1[:, e, 4 * f:4 * f + 4, :].rearrange("p b j -> p (b j)"), ident[:])
                    elif what == "Y":
                        pe.wait_ge(s5_scanned, 1 + a // 8)
                        pe.wait_ge(s5_tab_in[a % 2], 16 * 3 * (a // 2 + 1))
                        for v in range(2):
                            j = 2 * a + v
                            for g in range(2):
                                dst = bank[0:YC, (2 * v + g) * P:(2 * v + g + 1) * P]
                                pe.matmul(dst, sU[:, 2 * j + g, 0:YC], sTab[:, a % 2, v, g * P:(g + 1) * P],
                                          start=True, stop=False)
                                for e in range(2):
                                    c = 256 * g + e * P
                                    ins = pe.matmul(dst, sFH[:, j, e, 0:YC], sTabG[:, a % 2, v, c:c + P],
                                                    start=False, stop=e == 1)
                    elif what == "y":
                        f, e = a
                        if f % 4 == 0 and e == 0:
                            G.all_emptied(pe, q)
                        for u in range(4):
                            ins = pe.transpose(bank[:, u * YC:(u + 1) * YC],
                                               sY[:, 4 * e + u, (f % 4) * P:(f % 4 + 1) * P], ident[0:YC, 0:YC])
                    ins.then_inc(s5_fill, 1)
                if first:
                    G.all_emptied(pe, end)

            def hgrn():
                G = HG
                for j in range(2):
                    pe.wait_ge(used[j], first_pair["hg_out", 1])
                pe.wait_ge(gated, 2 * HH)
                for q, (what, a, owner) in enumerate(G.groups):
                    G.reuse(pe, q)
                    bank = bank_of(q)
                    if what == "A":
                        h, u = a
                        e = h % 2
                        if u < len(LEVELS):
                            pe.wait_ge(hg["scaled_pool"], (2 + len(LEVELS)) * h + 1 + u)
                            k_, q_ = lvl[e][u], lvl[e][u]
                        else:
                            pe.wait_ge(hg["scaled_dve"], h + 1)
                            k_, q_ = dgK[e], dgQ[e]
                        for t in range(4):
                            c = slice(t * P, (t + 1) * P)
                            ins = pe.matmul(bank[:, c], k_[:, c], q_[:, c], start=True, stop=True)
                    elif what == "O":
                        h, e = a, a % 2
                        pe.wait_ge(hg["void_dve"], G.before(G.at("A", (h, len(LEVELS))) + 1, "dve"))
                        pe.wait_ge(hg["void_act"], G.before(G.at("V", h) + 1, "act"))
                        pe.wait_ge(hg["state"], h + 1)
                        pe.wait_ge(hg["scaled_pool"], (2 + len(LEVELS)) * (h + 1))
                        for t in range(4):
                            pe.matmul(bank[:, t * P:(t + 1) * P], vTok[:, t, :], attn[e][:, t, :],
                                      start=True, stop=False,
                                      skip_group_check=True)
                            for n in range(2 * t, 2 * t + 2):
                                if n:
                                    c = slice(n * HC, (n + 1) * HC)
                                    ins = pe.matmul(bank[:, c], hS[:, n - 1, :], inQ[e][:, c], start=False, stop=True,
                                                    skip_group_check=True)
                    elif what == "V" or what == "K":
                        h, e = a, a % 2
                        if what == "K":
                            pe.wait_ge(hg["scaled_pool"], (2 + len(LEVELS)) * h + 1 + len(LEVELS))
                        for t in range(4):
                            c = slice(t * P, (t + 1) * P)
                            ins = pe.transpose(bank[:, c], hgV[:, h, c] if what == "V" else outK[e][:, c], ident[:])
                    elif what == "D":
                        h, odd = a
                        pe.wait_ge(hg["void_act"], G.before(G.at("K", h) + 1, "act"))
                        rows = slice(HC * odd, HC * (odd + 1))
                        for t in range(4):
                            ins = pe.matmul(bank[:, t * P:(t + 1) * P], kTok[rows, t, :], vTok[rows, t, :],
                                            start=True, stop=True)
                    elif what == "B":
                        b, f = a
                        for u in range(4):
                            h = 4 * f + u
                            ins = pe.matmul(bank[:, u * P:(u + 1) * P],
                                            hgV[:, h, SEQ + b:SEQ + b + 1].to_broadcast([P, P]), ident[:],
                                            start=True, stop=True)
                    elif what == "S":
                        for b in range(NS):
                            pe.wait_ge(hg["s_state"], 2 * (b + 1))
                            for h in range(HH):
                                ins = pe.matmul(bank[:, h * NS + b:h * NS + b + 1], sS[:, b, h, :],
                                                hgQ[:, h, SEQ + b:SEQ + b + 1], start=True, stop=True)
                    elif what == "N":
                        if a == 0:
                            G.reuse(pe, q + 1)
                        for h in range(HH) if a == 0 else range(HH - 1, HH):
                            if a == 0:
                                pe.wait_ge(hg["squares"], h + 1)
                            for e in range(2):
                                if (a == 1) != (h == HH - 1 and e == 1):
                                    continue
                                ins_ = pe.matmul(bank_of(q + e - a)[0:HH, 0:HT], one[:, HH - h:2 * HH - h],
                                                 (t1, t2)[h % 2][:, e * HT:(e + 1) * HT], start=h == 0, stop=h == HH - 1)
                                if e == 1 and h < HH - 1:
                                    ins_.then_inc(hg["squares_read"], 1)
                                else:
                                    ins = ins_
                    else:
                        h, e = a
                        pe.wait_ge(hg["inverse"], 1)
                        ins = pe.matmul(bank[:, 0:HT], ident[0:HH, h:h + 1].to_broadcast([HH, P]),
                                        t3[0:HH, e * HT:(e + 1) * HT], start=True, stop=True)
                    ins.then_inc(hg["fill"], 1)
                G.all_emptied(pe, len(G.groups))

            def transposes_kv(layer, which):
                src = kT[layer] if which == 0 else vT
                n = next(n for n, s_ in enumerate(ST) if s_[:2] == ("v" if which else "k", layer))
                for j in range(2):
                    pe.wait_ge(used[j], first_pair[ST[n][0], layer] + ST[n][2])
                for t in range(2):
                    for half in range(2):
                        q = 8 * layer + 4 * which + 2 * t + half
                        wait(pe, kv_evac, q - 1)
                        if q == 0:
                            pe.wait_ge(mem_root, 1)
                        for u in range(4):
                            ins = pe.transpose(mis[:, 2 + q % 2, u * P:(u + 1) * P],
                                               src[:, 4 * half + u, t * P:(t + 1) * P], ident[:])
                        ins.then_inc(kv_tr, 1)

            def stream(n):
                name, layer, pairs, kt = ST[n]
                r = norm_of.get((name, layer))
                mem = name in ("k", "v")
                hidden = from_hidden(name)
                x_hi, x_lo = (m_hi, m_lo) if mem else (h_hi, h_lo) if hidden else (a_hi, a_lo)
                if hidden:
                    x_done, x0 = h_lo_done, hidden_before(n)
                elif mem:
                    x_done, x0 = m_lo_done, KD * layer
                else:
                    r_in = next(norm_of[k_] for k_ in reversed([s_[:2] for s_ in ST[:n + 1]]) if k_ in norm_of)
                    x_done, x0 = a_lo_done, KD * split_norms.index(r_in)

                def body(p, i, first, last):
                    for j in range(2):
                        pe.wait_ge(lo_ready, 2 * p + j + 1)
                        wait(pe, used[j], p)
                        for k in range(kt):
                            if first and j == 0:
                                pe.wait_ge(x_done, x0 + k + 1)
                            for u, (w, x) in enumerate(((w_hi, x_hi), (w_hi, x_lo), (w_lo, x_hi))):
                                start, stop = k == 0 and u == 0, k == kt - 1 and u == 2
                                if mem:
                                    ins = pe.matmul(lslot(j, NM), w[:, j, k, :], x[:, k, :], start=start, stop=stop)
                                    continue
                                for half in range(2):
                                    ins = pe.matmul(lin[:, j, half, 0:HT], w[:, j, k, :],
                                                    x[:, k, half * HT:(half + 1) * HT], start=start, stop=stop)
                        ins.then_inc(chunk_done, 1)
                        if first and j == 0 and r is not None:
                            sums(r)
                        if first and j == 0 and n == 0:
                            memory_sums()
                over_pairs(pe, n, body)
                if mem:
                    transposes_kv(layer, 0 if name == "k" else 1)

            for n in range(len(ST)):
                if ST[n][:2] == ("ffn1_out0", 0) and s5_norm is not None:
                    s5(0, 1)
                if ST[n][:2] == ("ffn1_out1", 0) and s5_norm is not None:
                    s5(1, S5_EARLY)
                if ST[n][0] == "glu":
                    s5(S5_EARLY, len(S5G.groups))
                if ST[n][0] == "hg_out":
                    hgrn()
                if ST[n][0] == "xo":
                    attend(ST[n][1])
                stream(n)
            sums(NORMS - 1)
            for q in range(10):
                t, half = q // 2, q % 2
                wait(pe, y_evac, q - 1)
                cols = P if t < 4 else NS
                for u in range(4):
                    pe.wait_ge(y_normed, 4 * half + u + 1)
                    ins = pe.transpose(mis[0:cols, 2 + q % 2, u * P:(u + 1) * P],
                                       yT[:, 4 * half + u, t * P:t * P + cols], ident[:])
                ins.then_inc(y_tr, 1)


_INS = ["x_prompt", "x_sample", "mem_prompt", "state_s5_re", "state_s5_im", "state_hgrn", "cache_mem_k", "cache_mem_v",
        "ffn1_norm", "ffn1_w_in", "ffn1_w_out", "mix_norm", "xattn_norm", "mem_norm", "xattn_w_q", "xattn_w_kv",
        "xattn_w_o", "ffn2_norm", "ffn2_w_in", "ffn2_w_out", "s5_a_re", "s5_a_im", "s5_log_dt", "s5_b_re", "s5_b_im",
        "s5_c_re", "s5_c_im", "s5_d", "s5_w_glu", "hg_w_in", "hg_lb_logits", "hg_norm", "hg_w_out", "final_norm"]
_OUTS = [("y_prompt", (1, SEQ, D)), ("y_sample", (NS, 1, D)), ("s5_re_p", (1, 1, SG, SP_)), ("s5_im_p", (1, 1, SG, SP_)),
         ("s5_re_s", (1, NS, SG, SP_)), ("s5_im_s", (1, NS, SG, SP_)), ("hg_p", (1, 1, HH, P, P)),
         ("hg_s", (1, NS, HH, P, P)), ("mem_k", (DEPTH, 1, NM, MH, D // MH)), ("mem_v", (DEPTH, 1, NM, MH, D // MH))]


def kernel(**inputs):
    import numpy as _np
    import concourse.bacc as _bacc
    from concourse import mybir as _mybir
    from concourse.bass_utils import run_bass_kernel_spmd as _run

    nc = _bacc.Bacc("TRN2", target_bir_lowering=False, num_devices=1)
    arrays, ins, outs = {}, {}, {}
    for name in _INS:
        a = _np.ascontiguousarray(inputs[name])
        arrays[f"in_{name}_dram"] = a
        ins[name] = nc.dram_tensor(f"in_{name}_dram", a.shape, _mybir.dt.from_np(a.dtype), kind="ExternalInput").ap()
    for name, shape in _OUTS:
        outs[name] = nc.dram_tensor(f"out_{name}_dram", shape, F32, kind="ExternalOutput").ap()
    trunk_kernel(nc, ins, outs)
    r = _run(nc, [arrays], core_ids=[0])
    return tuple(r.results[0][f"out_{name}_dram"] for name, _ in _OUTS)
```
